# Optimizing a Trainium2 kernel written in Bass

```python
import math
import jax
import jax.numpy as jnp
from jax import lax
import numpy as np

D_MODEL = 1024
BATCH = 1
SEQ = 2048
DEPTH = 1

ATTN_HEADS = 8
HEAD_DIM = 64
D_ATTN = ATTN_HEADS * HEAD_DIM
RNN_BLOCKS = 8
D_RNN = 512
RNN_BLOCK_W = D_RNN // RNN_BLOCKS
D_MIX = D_ATTN + D_RNN
D_IN = 3 * D_ATTN + 2 * D_RNN
DILATED_BRANCHES = ((128, 1), (512, 4), (2048, 16))
Q_BLOCK = 128
REL_BUCKETS = 32
REL_MAX_DIST = 2048
CONV_WIDTH = 4
RG_C = 8.0
N_GROUPS = 4
EXPERTS_PER_GROUP = 8
N_EXPERTS = N_GROUPS * EXPERTS_PER_GROUP
TOP_K = 2
D_EXPERT = 512
MOE_BLOCK = 128
EPS = 1e-6
NEG_INF = -1e30

kernel_name = 'hymba_dilated_rglru_hmoe'

def rms_norm(x, gain):
    xf = x.astype(jnp.float32)
    y = xf * lax.rsqrt(jnp.mean(xf * xf, axis=-1, keepdims=True) + EPS)
    return (y * gain.astype(jnp.float32)).astype(x.dtype)

def t5_bucket(dist):
    exact = REL_BUCKETS // 2
    d = jnp.maximum(dist, 1).astype(jnp.float32)
    log_b = exact + (jnp.log(d / exact) / math.log(REL_MAX_DIST / exact) * (REL_BUCKETS - exact)).astype(jnp.int32)
    return jnp.where(dist < exact, dist, jnp.minimum(log_b, REL_BUCKETS - 1))

def dilated_branch(q, k, v, rel_table, window, dil):
    b, s, h, e = q.shape
    span = dil * Q_BLOCK
    s_pad = -(-s // span) * span
    n_blk = s_pad // span
    sub_len = s_pad // dil
    pad = ((0, 0), (0, s_pad - s), (0, 0), (0, 0))
    qb = jnp.pad(q, pad).reshape(b, n_blk, Q_BLOCK, dil, h, e)

    def key_windows(t):
        t = jnp.pad(t, pad).reshape(b, sub_len, dil, h, e)
        t = jnp.pad(t, ((0, 0), (Q_BLOCK, 0), (0, 0), (0, 0), (0, 0)))
        t = t.reshape(b, n_blk + 1, Q_BLOCK, dil, h, e)
        return jnp.concatenate([t[:, :-1], t[:, 1:]], axis=2)

    kw = key_windows(k)
    vw = key_windows(v)
    j_idx = jnp.arange(2 * Q_BLOCK)
    steps = jnp.arange(Q_BLOCK)[:, None] + Q_BLOCK - j_idx[None, :]
    band = (steps >= 0) & (steps <= window // dil)
    first = (jnp.arange(n_blk)[:, None, None] == 0) & (j_idx[None, None, :] < Q_BLOCK)
    valid = band[None] & ~first
    bias = rel_table[t5_bucket(jnp.maximum(steps, 0) * dil)]
    bias = jnp.transpose(bias, (2, 0, 1)).astype(jnp.float32)
    logits = jnp.einsum('bnirhe,bnjrhe->bnrhij', qb, kw).astype(jnp.float32) + bias
    logits = jnp.where(valid[None, :, None, None], logits, NEG_INF)
    m = jnp.max(logits, axis=-1, keepdims=True)
    p = jnp.exp(logits - m)
    denom = jnp.sum(p, axis=-1, keepdims=True)
    o = jnp.einsum('bnrhij,bnjrhe->bnirhe', (p / denom).astype(v.dtype), vw)
    lse = (m + jnp.log(denom))[..., 0]
    o = o.reshape(b, s_pad, h, e)[:, :s]
    lse = jnp.transpose(lse, (0, 1, 4, 2, 3)).reshape(b, s_pad, h)[:, :s]
    return o, lse

def dilated_attention(q, k, v, rel_table):
    outs = []
    lses = []
    for window, dil in DILATED_BRANCHES:
        o, lse = dilated_branch(q, k, v, rel_table, window, dil)
        outs.append(o)
        lses.append(lse)
    w = jax.nn.softmax(jnp.stack(lses, axis=-1), axis=-1)
    o = sum(outs[i].astype(jnp.float32) * w[..., i, None] for i in range(len(outs)))
    return o.astype(q.dtype)

def lru_combine(left, right):
    a_l, b_l = left
    a_r, b_r = right
    return a_l * a_r, a_r * b_l + b_r

def rglru_branch(xr, gr, conv_w, conv_b, w_a, b_a, w_x, b_x, lam):
    b, s, c = xr.shape
    u = lax.conv_general_dilated(xr, conv_w[:, None, :], window_strides=(1,),
                                 padding=((CONV_WIDTH - 1, 0),),
                                 dimension_numbers=('NWC', 'WIO', 'NWC'),
                                 feature_group_count=c) + conv_b
    ub = u.reshape(b, s, RNN_BLOCKS, RNN_BLOCK_W)
    r = jax.nn.sigmoid(jnp.einsum('bsgi,gij->bsgj', ub, w_a) + b_a).reshape(b, s, c)
    i = jax.nn.sigmoid(jnp.einsum('bsgi,gij->bsgj', ub, w_x) + b_x).reshape(b, s, c)
    log_a = -RG_C * r.astype(jnp.float32) * jax.nn.softplus(-lam.astype(jnp.float32))
    a = jnp.exp(log_a)
    drive = jnp.sqrt(-jnp.expm1(2.0 * log_a)) * (i * u).astype(jnp.float32)
    _, hseq = lax.associative_scan(lru_combine, (a, drive), axis=1)
    return hseq.astype(xr.dtype) * jax.nn.gelu(gr)

def expert_mlp(xb, wg, wu, wd):
    return (jax.nn.silu(xb @ wg) * (xb @ wu)) @ wd

def hier_moe(h, wr_g, br_g, wr_e, br_e, w_gate, w_up, w_down):
    b, s, d = h.shape
    m = b * s
    hf = h.reshape(m, d)
    g_logits = (hf @ wr_g + br_g).astype(jnp.float32)
    _, g_sel = lax.top_k(g_logits, 1)
    g_w = jnp.take_along_axis(jax.nn.softmax(g_logits, axis=-1), g_sel, axis=-1)
    e_logits = (hf @ wr_e + br_e).astype(jnp.float32).reshape(m, N_GROUPS, EXPERTS_PER_GROUP)
    e_logits = jnp.take_along_axis(e_logits, g_sel[:, :, None], axis=1)[:, 0]
    e_top, e_idx = lax.top_k(e_logits, TOP_K)
    gate = (g_w * jax.nn.softmax(e_top, axis=-1)).reshape(-1)
    expert = (g_sel * EXPERTS_PER_GROUP + e_idx).reshape(-1)
    token = jnp.repeat(jnp.arange(m), TOP_K)
    n_assign = m * TOP_K
    order = jnp.argsort(expert)
    e_sorted = expert[order]
    tok_sorted = token[order]
    counts = jnp.zeros((N_EXPERTS,), jnp.int32).at[expert].add(1)
    padded = (counts + MOE_BLOCK - 1) // MOE_BLOCK * MOE_BLOCK
    starts = jnp.cumsum(counts) - counts
    p_ends = jnp.cumsum(padded)
    p_starts = p_ends - padded
    dest = p_starts[e_sorted] + jnp.arange(n_assign) - starts[e_sorted]
    n_rows = n_assign + N_EXPERTS * MOE_BLOCK
    n_blocks = n_rows // MOE_BLOCK
    rows = jnp.zeros((n_rows, d), h.dtype).at[dest].set(hf[tok_sorted])
    block_expert = jnp.minimum(
        jnp.searchsorted(p_ends, jnp.arange(n_blocks) * MOE_BLOCK, side='right'), N_EXPERTS - 1)

    def run_block(args):
        xb, e = args
        return expert_mlp(xb, w_gate[e], w_up[e], w_down[e])

    out_rows = lax.map(run_block, (rows.reshape(n_blocks, MOE_BLOCK, d), block_expert)).reshape(n_rows, d)
    contrib = (out_rows[dest].astype(jnp.float32) * gate[order][:, None]).astype(h.dtype)
    return jnp.zeros((m, d), h.dtype).at[tok_sorted].add(contrib).reshape(b, s, d)

def setup_inputs(seed: int = 0) -> dict:
    key = jax.random.key(seed)
    ks = jax.random.split(key, 24)
    f32 = jnp.float32

    def nrm(k, shape, scale):
        return jax.random.normal(k, shape, f32) * scale

    def gain(k, shape):
        return 1.0 + 0.01 * jax.random.normal(k, shape, f32)

    a0 = jax.random.uniform(ks[12], (DEPTH, D_RNN), f32, minval=0.9, maxval=0.999)
    return {
        'x': nrm(ks[0], (BATCH, SEQ, D_MODEL), 1.0),
        'rel_bias_table': nrm(ks[1], (REL_BUCKETS, ATTN_HEADS), 0.2),
        'norm_mix': gain(ks[2], (DEPTH, D_MODEL)),
        'w_in': nrm(ks[3], (DEPTH, D_MODEL, D_IN), D_MODEL ** -0.5),
        'q_norm': gain(ks[4], (DEPTH, HEAD_DIM)),
        'k_norm': gain(ks[5], (DEPTH, HEAD_DIM)),
        'conv_w': nrm(ks[6], (DEPTH, CONV_WIDTH, D_RNN), CONV_WIDTH ** -0.5),
        'conv_b': nrm(ks[7], (DEPTH, D_RNN), 0.01),
        'rg_w_a': nrm(ks[8], (DEPTH, RNN_BLOCKS, RNN_BLOCK_W, RNN_BLOCK_W), RNN_BLOCK_W ** -0.5),
        'rg_b_a': nrm(ks[9], (DEPTH, RNN_BLOCKS, RNN_BLOCK_W), 0.01),
        'rg_w_x': nrm(ks[10], (DEPTH, RNN_BLOCKS, RNN_BLOCK_W, RNN_BLOCK_W), RNN_BLOCK_W ** -0.5),
        'rg_b_x': nrm(ks[11], (DEPTH, RNN_BLOCKS, RNN_BLOCK_W), 0.01),
        'rg_lambda': jnp.log(a0) - jnp.log1p(-a0),
        'norm_attn_out': gain(ks[13], (DEPTH, D_ATTN)),
        'norm_rnn_out': gain(ks[14], (DEPTH, D_RNN)),
        'w_out': nrm(ks[15], (DEPTH, D_MIX, D_MODEL), D_MIX ** -0.5),
        'norm_ffn': gain(ks[16], (DEPTH, D_MODEL)),
        'router_group_w': nrm(ks[17], (DEPTH, D_MODEL, N_GROUPS), D_MODEL ** -0.5),
        'router_group_b': nrm(ks[18], (DEPTH, N_GROUPS), 0.01),
        'router_expert_w': nrm(ks[19], (DEPTH, D_MODEL, N_EXPERTS), D_MODEL ** -0.5),
        'router_expert_b': nrm(ks[20], (DEPTH, N_EXPERTS), 0.01),
        'expert_w_gate': nrm(ks[21], (DEPTH, N_EXPERTS, D_MODEL, D_EXPERT), D_MODEL ** -0.5),
        'expert_w_up': nrm(ks[22], (DEPTH, N_EXPERTS, D_MODEL, D_EXPERT), D_MODEL ** -0.5),
        'expert_w_down': nrm(ks[23], (DEPTH, N_EXPERTS, D_EXPERT, D_MODEL), D_EXPERT ** -0.5),
    }

def reference(x, rel_bias_table, norm_mix, w_in, q_norm, k_norm, conv_w, conv_b,
              rg_w_a, rg_b_a, rg_w_x, rg_b_x, rg_lambda, norm_attn_out, norm_rnn_out,
              w_out, norm_ffn, router_group_w, router_group_b, router_expert_w,
              router_expert_b, expert_w_gate, expert_w_up, expert_w_down):
    b, s, _ = x.shape
    scale = HEAD_DIM ** -0.5
    splits = [D_ATTN, 2 * D_ATTN, 3 * D_ATTN, 3 * D_ATTN + D_RNN]
    for l in range(DEPTH):
        hn = rms_norm(x, norm_mix[l])
        z = hn @ w_in[l]
        q, k, v, xr, gr = jnp.split(z, splits, axis=-1)
        q = rms_norm(q.reshape(b, s, ATTN_HEADS, HEAD_DIM), q_norm[l]) * scale
        k = rms_norm(k.reshape(b, s, ATTN_HEADS, HEAD_DIM), k_norm[l])
        v = v.reshape(b, s, ATTN_HEADS, HEAD_DIM)
        attn = dilated_attention(q, k, v, rel_bias_table).reshape(b, s, D_ATTN)
        rnn = rglru_branch(xr, gr, conv_w[l], conv_b[l], rg_w_a[l], rg_b_a[l],
                           rg_w_x[l], rg_b_x[l], rg_lambda[l])
        mix = jnp.concatenate([rms_norm(attn, norm_attn_out[l]), rms_norm(rnn, norm_rnn_out[l])], axis=-1)
        x = x + mix @ w_out[l]
        x = x + hier_moe(rms_norm(x, norm_ffn[l]), router_group_w[l], router_group_b[l],
                         router_expert_w[l], router_expert_b[l], expert_w_gate[l],
                         expert_w_up[l], expert_w_down[l])
    return x


_drawn_inputs = setup_inputs


def setup_inputs(seed=0):
    import zlib

    import numpy as np

    out = dict(_drawn_inputs(seed))
    spreads = {}
    factors = {'norm_mix': 2.753,
     'q_norm': 4.91,
     'k_norm': 4.29,
     'rg_b_a': 8.0,
     'rg_b_x': 8.0,
     'norm_attn_out': 5.015,
     'norm_rnn_out': 4.57,
     'norm_ffn': 4.222,
     'router_group_b': 4.864,
     'router_expert_b': 5.376}
    for name, (base, spread) in spreads.items():
        noise = np.random.default_rng([zlib.crc32(name.encode()), seed]).standard_normal(out[name].shape)
        drawn = base * np.exp(spread * noise) if base else spread * noise
        out[name] = jnp.asarray(drawn.astype(out[name].dtype))
    for name, factor in factors.items():
        out[name] = (out[name] * factor).astype(out[name].dtype)
    return out
```

```python
from contextlib import ExitStack

import numpy as np

import concourse.bass as bass
from concourse import mybir

F32 = mybir.dt.float32
F32R = mybir.dt.float32r
I32 = mybir.dt.int32
U32 = mybir.dt.uint32
ALU = mybir.AluOpType
ACT = mybir.ActivationFunctionType
X = mybir.AxisListType.X

P = 128
SEQ, DM = 2048, 1024
HEADS, HD = 8, 64
D_ATTN, D_RNN = 512, 512
RNN_W = 64
D_QKV = 3 * D_ATTN
D_IN = D_QKV + 2 * D_RNN
TILES = SEQ // P
KM = DM // P
BRANCHES = ((128, 1), (512, 4), (2048, 16))
QB = 128
BUCKETS, MAX_DIST = 32, 2048
CONV = 4
RG_C = 8.0
GROUPS, PER_GROUP = 4, 8
EXPERTS = GROUPS * PER_GROUP
TOP_K = 2
DE = 512
EPS = 1e-6
NEG = -1e30
BIG = 1e30

TW = 3 * QB - 1
OW = D_ATTN + 2 * HEADS
MAX_BLOCKS = SEQ * TOP_K // P + EXPERTS - 1
MIN_BLOCKS = SEQ * TOP_K // P


def bias_buckets():
    oh = np.zeros((BUCKETS + 1, len(BRANCHES), TW), np.float32)
    for b, (window, dil) in enumerate(BRANCHES):
        for c in range(TW):
            steps = QB - (c - (QB - 1))
            if steps < 0 or steps > window // dil:
                oh[BUCKETS, b, c] = 1.0
                continue
            dist = steps * dil
            exact = BUCKETS // 2
            if dist < exact:
                k = dist
            else:
                f = np.float32
                log = np.log(f(dist) / f(exact), dtype=np.float32) / f(np.log(MAX_DIST / exact))
                k = min(exact + int(log * f(BUCKETS - exact)), BUCKETS - 1)
            oh[k, b, c] = 1.0
    return oh.reshape(BUCKETS + 1, len(BRANCHES) * TW)


class Scope:

    def __init__(self, nc, name):
        self.nc, self.name, self.ctx, self.sems = nc, name, ExitStack(), []

    def __enter__(self):
        self.ctx.__enter__()
        return self

    def __exit__(self, *a):
        result = self.ctx.__exit__(*a)
        if self.sems:
            self.clear()
        return result

    def sb(self, name, shape, dt=F32):
        return self.ctx.enter_context(self.nc.sbuf_tensor(f"{self.name}_{name}", shape, dt))

    def ps(self, name, shape, dt=F32):
        return self.ctx.enter_context(self.nc.psum_tensor(f"{self.name}_{name}", shape, dt))

    def sem(self, name):
        sem = self.ctx.enter_context(self.nc.semaphore(f"{self.name}_{name}"))
        self.sems.append(sem.num)
        return sem

    def clear(self):
        runs = []
        for num in sorted(self.sems):
            if runs and num == runs[-1][1]:
                runs[-1][1] += 1
            else:
                runs.append([num, num + 1])
        with self.nc.Block() as block:
            @block.gpsimd
            def _(pool):
                for first, end in runs:
                    pool.sem_clear(range(first, end))

    def block(self):
        return self.ctx.enter_context(self.nc.Block())


def column(ap, n):
    return ap.rearrange("a (k p) -> p (a k)", p=P)



def wait(engine, sem, value):
    if not isinstance(value, int) or value > 0:
        engine.wait_ge(sem, value)


def project_and_recur(nc, x, norm_mix, w_in, conv_w, conv_b, rg_w_a, rg_b_a, rg_w_x, rg_b_x,
                      rg_lambda, qkv, rnn_t):
    CH = 512
    NCH = SEQ // CH
    TC = CH // P
    WC = 256
    NW = D_IN // WC
    NR = 2 * D_RNN // WC
    NX = D_RNN // WC
    NQK = 2 * D_ATTN // WC
    CT = D_RNN // P
    HW = WC // HD
    AHEAD = 3

    w_cols = [D_QKV + n * WC for n in range(NR)] + [n * WC for n in range(NW - NR)]

    with Scope(nc, "a") as s:
        ident = s.sb("ident", [P, P])
        gain_row = s.sb("gain_row", [P, DM])
        x_t = s.sb("x_t", [P, TC, DM])
        junk = s.sb("junk", [P, DM])
        ss = s.sb("ss", [P, TC])
        rstd = s.sb("rstd", [P, TC])
        half = s.sb("half", [P, TC * HW])
        eps_x = s.sb("eps_x", [P, 1])
        eps_z = s.sb("eps_z", [P, TC * HW])
        hn_hi = s.sb("hn_hi", [P, KM, CH], F32R)
        hn_lo = s.sb("hn_lo", [P, KM, CH], F32R)
        w_raw = s.sb("w_raw", [P, 2, KM, WC])
        w_hi = s.sb("w_hi", [P, 2, KM, WC], F32R)
        w_lo = s.sb("w_lo", [P, 2, KM, WC], F32R)
        z = s.sb("z", [P, 2, TC, WC])
        z_sq = s.sb("z_sq", [P, TC, WC])
        z_ss = s.sb("z_ss", [P, TC * HW])
        z_rs = s.sb("z_rs", [P, TC * HW])
        xr = s.sb("xr", [P, CT, CONV - 1 + CH])
        gate = s.sb("gate", [P, CT, CH])
        u = s.sb("u", [P, CT, CH])
        r = s.sb("r", [P, CT, CH])
        inp = s.sb("inp", [P, CT, CH])
        a = s.sb("a", [P, CT, CH])
        hs = s.sb("hs", [P, CT, CH])
        carry = s.sb("carry", [P, CT])
        cw = s.sb("cw", [P, CONV, CT])
        cb = s.sb("cb", [P, CT])
        gb = s.sb("gb", [P, 2, CT])
        lam = s.sb("lam", [P, CT])
        sp = s.sb("sp", [P, 6, CT])
        coef = s.sb("coef", [P, 2, CT])
        wg = s.sb("wg", [P, 2, CT, P])
        tr_ps = s.ps("tr_ps", [P, KM, P])
        mm_ps = s.ps("mm_ps", [P, 2, 2, 512])
        g_ps = s.ps("g_ps", [P, 2, 512])

        two = range(2)
        x_in = [s.sem(f"x_in{j}") for j in range(TC)]
        consts_in = s.sem("consts_in")
        wg_zeroed = s.sem("wg_zeroed")
        wg_in = s.sem("wg_in")
        ident_step = s.sem("ident_step")
        consts = s.sem("consts")
        ss_done = [s.sem(f"ss_done{j}") for j in range(TC)]
        eps_added = s.sem("eps_added")
        rstd_done = [s.sem(f"rstd_done{j}") for j in range(TC)]
        xn_done = [s.sem(f"xn_done{j}") for j in range(TC)]
        tr_done = [s.sem(f"tr_done{j}") for j in range(TC)]
        hi_done = s.sem("hi_done")
        lo_done = s.sem("lo_done")
        w_loaded = [s.sem(f"w_loaded{j}") for j in two]
        whi_done = s.sem("whi_done")
        wlo_done = [s.sem(f"wlo_done{j}") for j in two]
        mm_done = [s.sem(f"mm_done{j}") for j in two]
        ev_done = [s.sem(f"ev_done{j}") for j in two]
        sq_done = s.sem("sq_done")
        zss_done = s.sem("zss_done")
        zeps_done = s.sem("zeps_done")
        zrs_done = s.sem("zrs_done")
        zn_done = s.sem("zn_done")
        z_out = [s.sem(f"z_out{j}") for j in two]
        coef_step = s.sem("coef_step")
        exp_lam = s.sem("exp_lam")
        coef_done = s.sem("coef_done")
        halo_done = s.sem("halo_done")
        conv_step = s.sem("conv_step")
        gmm_done = [s.sem(f"gmm_done{j}") for j in two]
        gsig_done = [s.sem(f"gsig_done{j}") for j in two]
        a_done = s.sem("a_done")
        th_done = s.sem("th_done")
        iu_done = s.sem("iu_done")
        a2_done = s.sem("a2_done")
        d2_done = s.sem("d2_done")
        sqrt_done = s.sem("sqrt_done")
        drive_done = s.sem("drive_done")
        scan_done = s.sem("scan_done")
        carry_done = s.sem("carry_done")
        y_done = s.sem("y_done")
        y_out = s.sem("y_out")

        block = s.block()
        NCONV = CONV * CT

        def chunks(engine, body):
            with engine.Fori(0, NCH - 1) as c:
                body(c, False)
            body(NCH - 1, True)

        @block.sync
        def _(sync):
            x_v = x[0].rearrange("(c t p) d -> c t p d", t=TC, p=P)
            qkv_v = qkv.rearrange("(c t p) n -> c p t n", t=TC, p=P)
            rnn_v = rnn_t.rearrange("(k p) (c n) -> c p k n", p=P, n=CH)

            def one(ap):
                return ap.rearrange("a p d -> (a p) d") if len(ap.shape) == 3 else \
                    ap.rearrange("a p t n -> (a p) t n")

            def load_x(c, t):
                wait(sync, tr_done[t], c)
                sync.dma_start(x_t[:, t, :], one(x_v[bass.ds(c, 1), t, :, :])).then_inc(x_in[t], 16)

            def load_w(c, n):
                j, m = n % 2, (NW // 2) * c + n // 2
                wait(sync, wlo_done[j], m)
                col = w_cols[n % NW]
                sync.dma_start(w_raw[:, j, :, :],
                               w_in[0].rearrange("(k p) n -> p k n", p=P)[:, :, col:col + WC]
                               ).then_inc(w_loaded[j], 16)

            load_x(0, 0)
            load_x(0, 1)
            sync.dma_start(gain_row[:, :], norm_mix.to_broadcast([P, DM])).then_inc(consts_in, 16)
            load_w(0, 0)
            for t in range(2, TC):
                load_x(0, t)
            for n in range(1, AHEAD):
                load_w(0, n)

            def body(c, last):
                for n in range(NW):
                    if not (last and n + AHEAD >= NW):
                        load_w(c, n + AHEAD)
                    if not last and 4 <= n < 4 + TC:
                        load_x(c + 1, n - 4)
                    if n > NR:
                        store_z(c, n - NR - 1)
                store_z(c, NW - NR - 1)
                sync.wait_ge(y_done, c + 1)
                sync.dma_start(one(rnn_v[bass.ds(c, 1), :, :, :]), u[:, :, :]).then_inc(y_out, 16)

            def store_z(c, i):
                if i < NQK:
                    sync.wait_ge(zn_done, NQK * c + i + 1)
                else:
                    n = NR + i
                    sync.wait_ge(ev_done[n % 2], (NW // 2) * c + n // 2 + 1)
                sync.dma_start(one(qkv_v[bass.ds(c, 1), :, :, i * WC:(i + 1) * WC]),
                               z[:, i % 2, :, :]).then_inc(z_out[i % 2], 16)

            chunks(sync, body)
            for j in two:
                sync.wait_ge(z_out[j], 16 * NCH * (NW - NR) // 2)
            sync.wait_ge(y_out, 16 * NCH)

        @block.gpsimd
        def _(pool):
            pool.memset(wg[:, :, :, :], 0.0).then_inc(wg_zeroed, 1)
            pool.memset(half[:, :], -0.5).then_inc(ident_step, 1)
            pool.memset(ident[:, :], 0.0).then_inc(ident_step, 1)
            pool.memset(eps_x[:, :], DM * EPS).then_inc(ident_step, 1)
            pool.memset(eps_z[:, :], HD * EPS).then_inc(ident_step, 1)
            pool.wait_ge(ident_step, 4)
            pool.affine_select(out=ident[:, :], in_=ident[:, :], compare_op=ALU.not_equal, fill=1.0, base=0,
                               pattern=[[-1, P]], channel_multiplier=1).then_inc(consts, 1)
            with nc.allow_non_contiguous_dma(reason="vectors of 512 values, by channel"):
                for ap, src in ((cb, conv_b), (lam, rg_lambda)):
                    pool.dma_start(ap[:, :], column(src, CT)).then_inc(wg_in, 16)
                for m, src in enumerate((rg_b_a, rg_b_x)):
                    pool.dma_start(gb[:, m, :], column(src.rearrange("a g w -> a (g w)"), CT)).then_inc(wg_in, 16)
                for k in range(CONV):
                    pool.dma_start(cw[:, k, :], column(conv_w[0, k:k + 1, :], CT)).then_inc(wg_in, 16)
            pool.wait_ge(wg_zeroed, 1)
            for m, w in enumerate((rg_w_a, rg_w_x)):
                for g in range(2):
                    q = slice(g * RNN_W, (g + 1) * RNN_W)
                    pool.dma_start(wg[q, m, :, q],
                                   w[0].rearrange("(k g) i j -> g i k j", g=2)[g]).then_inc(wg_in, 16)

            def rstd_of(c, t):
                j = t
                pool.wait_ge(ss_done[j], c + 1)
                pool.tensor_tensor(rstd[:, j:j + 1], ss[:, j:j + 1], eps_x[:, 0:1], ALU.add
                                   ).then_inc(eps_added, 1)
                pool.wait_ge(eps_added, TC * c + t + 1)
                pool.tensor_tensor(rstd[:, j:j + 1], rstd[:, j:j + 1], half[:, 0:1], ALU.pow
                                   ).then_inc(rstd_done[j], 1)

            for t in range(TC):
                rstd_of(0, t)

            def body(c, last):
                for n in range(NR, NW):
                    i = n - NR
                    if i == 2:
                        for j in two:
                            pool.wait_ge(gsig_done[j], CT * c + CT)
                        pool.tensor_tensor(inp[:, :, :], inp[:, :, :], u[:, :, :], ALU.mult).then_inc(iu_done, 1)
                        pool.wait_ge(a_done, CT * c + CT)
                        pool.tensor_tensor(hs[:, :, :], a[:, :, :], a[:, :, :], ALU.mult).then_inc(a2_done, 1)
                    if i == 4:
                        pool.wait_ge(sqrt_done, c + 1)
                        pool.wait_ge(iu_done, c + 1)
                        pool.tensor_tensor(inp[:, :, :], inp[:, :, :], r[:, :, :], ALU.mult).then_inc(drive_done, 1)
                    if i < NQK:
                        pool.wait_ge(ev_done[n % 2], (NW // 2) * c + n // 2 + 1)
                        pool.wait_ge(zss_done, NQK * c + i)
                        pool.tensor_tensor(z_sq[:, :, :], z[:, i % 2, :, :], z[:, i % 2, :, :], ALU.mult
                                           ).then_inc(sq_done, 1)
                        pool.wait_ge(zss_done, NQK * c + i + 1)
                        pool.wait_ge(zn_done, NQK * c + i)
                        pool.tensor_tensor(z_rs[:, :], z_ss[:, :], eps_z[:, :], ALU.add).then_inc(zeps_done, 1)
                        pool.wait_ge(zeps_done, NQK * c + i + 1)
                        pool.tensor_tensor(z_rs[:, :], z_rs[:, :], half[:, :], ALU.pow).then_inc(zrs_done, 1)
                    if not last and i < TC:
                        rstd_of(c + 1, i)
                pool.wait_ge(scan_done, CT * c + CT)
                pool.tensor_tensor(u[:, :, :], hs[:, :, :], gate[:, :, :], ALU.mult).then_inc(y_done, 1)

            chunks(pool, body)

        @block.scalar
        def _(act):
            def square(c, t):
                act.wait_ge(x_in[t], 16 * (c + 1))
                wait(act, ss_done[(t - 1) % TC], c + 1 if t else c)
                act.activation(junk[:, :], x_t[:, t, :], ACT.Square, accum_out=ss[:, t:t + 1]
                               ).then_inc(ss_done[t], 1)

            def hn_split(c, t):
                act.wait_ge(tr_done[t], c + 1)
                act.activation(hn_hi[:, :, t * P:(t + 1) * P], tr_ps[:, :, :], ACT.Copy).then_inc(hi_done, 1)

            def w_split(c, n):
                j, m = n % 2, (NW // 2) * c + n // 2
                act.wait_ge(w_loaded[j], 16 * (m + 1))
                wait(act, mm_done[j], m)
                act.activation(w_hi[:, j, :, :], w_raw[:, j, :, :], ACT.Copy).then_inc(whi_done, 1)

            for t in range(TC):
                square(0, t)
                if t >= 1:
                    hn_split(0, t - 1)
            w_split(0, 0)
            hn_split(0, TC - 1)
            w_split(0, 1)
            act.wait_ge(coef_step, 2)
            act.activation(sp[:, 1, :], sp[:, 0, :], ACT.Exp, scale=-1.0).then_inc(exp_lam, 1)
            act.wait_ge(wg_in, 16 * 12)

            def body(c, last):
                for n in range(NW):
                    if n == 5:
                        for k in range(2 * CT):
                            m, ct, j = k // CT, k % CT, k % 2
                            act.wait_ge(gmm_done[j], CT * c + k // 2 + 1)
                            if k == 0:
                                act.wait_ge(drive_done, c)
                            if k == CT:
                                act.wait_ge(scan_done, CT * c)
                            act.activation((r, inp)[m][:, ct, :], g_ps[:, j, :], ACT.Sigmoid,
                                           bias=gb[:, m, ct:ct + 1]).then_inc(gsig_done[j], 1)
                    if n == 6:
                        act.wait_ge(gsig_done[0], CT * c + CT // 2)
                        act.wait_ge(gsig_done[1], CT * c + CT // 2)
                        for ct in range(CT):
                            act.activation(a[:, ct, :], r[:, ct, :], ACT.Exp, scale=coef[:, 0, ct:ct + 1]
                                           ).then_inc(a_done, 1)
                        for ct in range(CT):
                            act.wait_ge(a_done, CT * c + ct + 1)
                            act.activation(r[:, ct, :], r[:, ct, :], ACT.Tanh, scale=coef[:, 1, ct:ct + 1]
                                           ).then_inc(th_done, 1)
                    if n == 7:
                        act.wait_ge(d2_done, c + 1)
                        act.activation(r[:, :, :], r[:, :, :], ACT.Sqrt).then_inc(sqrt_done, 1)
                    j, m = n % 2, (NW // 2) * c + n // 2
                    if not last and 5 <= n < 5 + TC:
                        square(c + 1, n - 5)
                    if n == NW - 1 and not last:
                        for t in range(TC - 1):
                            hn_split(c + 1, t)
                    act.wait_ge(mm_done[j], m + 1)
                    if n < NX:
                        act.wait_ge(halo_done, c)
                        act.activation(xr[:, 2 * n:2 * n + 2, CONV - 1:], mm_ps[:, j, :, :], ACT.Copy
                                       ).then_inc(ev_done[j], 1)
                    elif n < NR:
                        act.wait_ge(y_done, c)
                        k = 2 * (n - NX)
                        act.activation(gate[:, k:k + 2, :], mm_ps[:, j, :, :], ACT.Gelu_apprx_tanh
                                       ).then_inc(ev_done[j], 1)
                    else:
                        i = n - NR
                        wait(act, z_out[i % 2], 16 * ((NW - NR) // 2 * c + i // 2))
                        act.activation(z[:, i % 2, :, :], mm_ps[:, j, :, :].rearrange("p b (t n) -> p (b t) n", n=WC),
                                       ACT.Copy).then_inc(ev_done[j], 1)
                    if not (last and n + 2 >= NW):
                        w_split(c, n + 2)
                if not last:
                    hn_split(c + 1, TC - 1)

            chunks(act, body)

        @block.vector
        def _(dve):
            def normalise(c, t):
                j = t
                dve.wait_ge(rstd_done[j], c + 1)
                dve.scalar_tensor_tensor(out=x_t[:, j, :], in0=x_t[:, j, :], scalar=rstd[:, j:j + 1],
                                         in1=gain_row[:, :], op0=ALU.mult, op1=ALU.mult
                                         ).then_inc(xn_done[j], 1)

            def hn_split(c, t):
                dve.wait_ge(hi_done, TC * c + t + 1)
                dve.tensor_tensor(hn_lo[:, :, t * P:(t + 1) * P], tr_ps[:, :, :],
                                  hn_hi[:, :, t * P:(t + 1) * P].bitcast(F32), ALU.subtract).then_inc(lo_done, 1)

            def w_split(c, n):
                j = n % 2
                dve.wait_ge(whi_done, NW * c + n + 1)
                dve.tensor_tensor(w_lo[:, j, :, :], w_raw[:, j, :, :], w_hi[:, j, :, :].bitcast(F32),
                                  ALU.subtract).then_inc(wlo_done[j], 1)

            dve.memset(carry[:, :], 0.0).then_inc(coef_done, 1)
            dve.memset(xr[:, :, 0:CONV - 1], 0.0).then_inc(coef_done, 1)
            dve.wait_ge(consts_in, 16)
            dve.tensor_scalar(gain_row[:, :], gain_row[:, :], DM ** 0.5, None, ALU.mult).then_inc(coef_done, 1)
            dve.wait_ge(coef_done, 3)
            for t in range(TC):
                normalise(0, t)
                if t >= 1:
                    hn_split(0, t - 1)
            w_split(0, 0)
            hn_split(0, TC - 1)
            w_split(0, 1)

            steps = [0]

            def link(ins):
                steps[0] += 1
                ins.then_inc(coef_step, 1)
                dve.wait_ge(coef_step, steps[0])

            absl, e, sv, s2, t_, neg = (sp[:, k, :] for k in range(6))
            dve.wait_ge(wg_in, 16 * 12)
            link(dve.tensor_scalar(neg, lam[:, :], -1.0, None, ALU.mult))
            link(dve.tensor_tensor(absl, lam[:, :], neg, ALU.max))
            dve.wait_ge(exp_lam, 1)
            link(dve.tensor_scalar(s2, e, 2.0, None, ALU.add))
            link(dve.reciprocal(t_, s2))
            link(dve.tensor_tensor(sv, e, t_, ALU.mult))
            link(dve.tensor_tensor(s2, sv, sv, ALU.mult))
            link(dve.tensor_scalar(t_, s2, 1.0 / 17, None, ALU.mult))
            for k in range(15, 1, -2):
                link(dve.scalar_tensor_tensor(out=t_, in0=t_, scalar=1.0 / k, in1=s2, op0=ALU.add, op1=ALU.mult))
            link(dve.scalar_tensor_tensor(out=t_, in0=t_, scalar=1.0, in1=sv, op0=ALU.add, op1=ALU.mult))
            link(dve.tensor_scalar(neg, neg, 0.0, None, ALU.max))
            link(dve.scalar_tensor_tensor(out=t_, in0=t_, scalar=2.0, in1=neg, op0=ALU.mult, op1=ALU.add))
            dve.tensor_scalar(coef[:, 0, :], t_, -RG_C, None, ALU.mult).then_inc(coef_done, 1)
            dve.tensor_scalar(coef[:, 1, :], t_, RG_C, None, ALU.mult).then_inc(coef_done, 1)

            def body(c, last):
                for n in range(NW):
                    if n == 7:
                        dve.wait_ge(a2_done, c + 1)
                        dve.wait_ge(th_done, CT * c + CT)
                        dve.scalar_tensor_tensor(out=r[:, :, :].rearrange("p k n -> p (k n)"),
                                                 in0=hs[:, :, :].rearrange("p k n -> p (k n)"), scalar=1.0,
                                                 in1=r[:, :, :].rearrange("p k n -> p (k n)"), op0=ALU.add,
                                                 op1=ALU.mult).then_inc(d2_done, 1)
                    if n == 9:
                        dve.wait_ge(drive_done, c + 1)
                        dve.wait_ge(carry_done, c)
                        for ct in range(CT):
                            dve.tensor_tensor_scan(hs[:, ct, :], a[:, ct, :], inp[:, ct, :],
                                                   carry[:, ct:ct + 1], ALU.mult, ALU.add).then_inc(scan_done, 1)
                        dve.wait_ge(scan_done, CT * c + CT)
                        dve.tensor_copy(carry[:, :], hs[:, :, CH - 1]).then_inc(carry_done, 1)
                    if n == NW - 1 and not last:
                        for t in range(TC - 1):
                            hn_split(c + 1, t)
                    if not last and 5 <= n < 5 + TC:
                        normalise(c + 1, n - 5)
                    if not (last and n + 2 >= NW):
                        w_split(c, n + 2)
                    if n == NX:
                        for j in two:
                            dve.wait_ge(ev_done[j], (NW // 2) * c + 1)
                        wait(dve, y_out, 16 * c)
                        for k in range(CONV):
                            for ct in range(CT):
                                tap, src = cw[:, k, ct:ct + 1], xr[:, ct, k:k + CH]
                                if k == 0:
                                    ins = dve.tensor_scalar(u[:, ct, :], src, tap, cb[:, ct:ct + 1],
                                                            ALU.mult, ALU.add)
                                else:
                                    dve.wait_ge(conv_step, NCONV * c + CT * (k - 1) + ct + 1)
                                    ins = dve.scalar_tensor_tensor(out=u[:, ct, :], in0=src, scalar=tap,
                                                                   in1=u[:, ct, :], op0=ALU.mult, op1=ALU.add)
                                ins.then_inc(conv_step, 1)
                        dve.wait_ge(conv_step, NCONV * c + NCONV)
                        dve.tensor_copy(xr[:, :, 0:CONV - 1], xr[:, :, CH:CH + CONV - 1]).then_inc(halo_done, 1)
                    i = n - NR
                    if 0 <= i < NQK:
                        dve.wait_ge(sq_done, NQK * c + i + 1)
                        dve.tensor_reduce(z_ss[:, :], z_sq[:, :, :].rearrange("p t (h d) -> p (t h) d", d=HD), X,
                                          ALU.add).then_inc(zss_done, 1)
                        dve.wait_ge(zrs_done, NQK * c + i + 1)
                        zv = z[:, i % 2, :, :].rearrange("p t (h d) -> p (t h) d", d=HD)
                        dve.tensor_tensor(zv, zv, z_rs[:, :].unsqueeze(2).to_broadcast([P, TC * HW, HD]),
                                          ALU.mult).then_inc(zn_done, 1)
                if not last:
                    hn_split(c + 1, TC - 1)

            chunks(dve, body)

        @block.tensor
        def _(pe):
            def transposes(c, t):
                pe.wait_ge(xn_done[t], c + 1)
                wait(pe, lo_done, TC * c + t)
                for k in range(KM):
                    ins = pe.transpose(tr_ps[:, k, :], x_t[:, t, k * P:(k + 1) * P], ident[:, :])
                ins.then_inc(tr_done[t], 1)

            def products(out, pairs):
                n = len(pairs)
                for k, (s_hi, s_lo, m_hi, m_lo) in enumerate(pairs):
                    pe.matmul(out, s_lo, m_hi, start=(k == 0), stop=False)
                    pe.matmul(out, s_hi, m_lo, start=False, stop=False)
                    ins = pe.matmul(out, s_hi, m_hi, start=False, stop=(k == n - 1))
                return ins

            pe.wait_ge(consts, 1)
            for t in range(TC):
                transposes(0, t)

            def body(c, last):
                wait_lo = TC * c + TC
                pe.wait_ge(lo_done, wait_lo)
                for n in range(NW):
                    j, m = n % 2, (NW // 2) * c + n // 2
                    pe.wait_ge(wlo_done[j], m + 1)
                    wait(pe, ev_done[j], m)
                    if n < NR:
                        for b in two:
                            cols = slice(b * P, (b + 1) * P)
                            ins = products(mm_ps[:, j, b, :],
                                           [(w_hi[:, j, k, cols], w_lo[:, j, k, cols], hn_hi[:, k, :], hn_lo[:, k, :])
                                            for k in range(KM)])
                        ins.then_inc(mm_done[j], 1)
                        continue
                    for t in range(TC):
                        cols = slice(t * P, (t + 1) * P)
                        ins = products(mm_ps[:, j, t // 2, (t % 2) * WC:(t % 2 + 1) * WC],
                                       [(hn_hi[:, k, cols], hn_lo[:, k, cols], w_hi[:, j, k, :], w_lo[:, j, k, :])
                                        for k in range(KM)])
                        if t == TC - 1:
                            ins.then_inc(mm_done[j], 1)
                        if n == 5:
                            if t == 0:
                                pe.wait_ge(conv_step, NCONV * c + NCONV)
                                pe.wait_ge(wg_in, 16 * 12)
                            for g in two:
                                k = 2 * t + g
                                pe.wait_ge(gsig_done[g], CT * c + k // 2)
                                pe.matmul(g_ps[:, g, :], wg[:, k // CT, k % CT, :], u[:, k % CT, :],
                                          start=True, stop=True).then_inc(gmm_done[g], 1)
                        if n == NW - 1 and not last:
                            transposes(c + 1, t)

            chunks(pe, body)



def attend(nc, rel_table, one_hot, q_norm, k_norm, qkv, toeplitz, attn_o):
    NB = len(BRANCHES)
    TT = 4
    NG = TILES // TT
    HU = HEADS // 2
    UG = 2 * TT
    TRL, PVL = 2, 3

    with Scope(nc, "b") as s:
        ident = s.sb("ident", [P, P])
        exchange = s.sb("exchange", [P, P])
        rel = s.sb("rel", [BUCKETS + 1, HEADS])
        oh = s.sb("oh", [BUCKETS + 1, NB * TW])
        trow = s.sb("trow", [HEADS, NB * TW])
        bias = s.sb("bias", [P, NB, HEADS, 2 * QB])
        gk = s.sb("gk", [P, 1])
        gq = s.sb("gq", [P, 1])
        gqk = s.sb("gqk", [P, 1])
        qk_in = s.sb("qk_in", [P, TT, 2 * D_ATTN])
        v_in = s.sb("v_in", [P, TT, D_ATTN])
        q_t = s.sb("q_t", [P, 2, 4, P])
        k_t = s.sb("k_t", [P, TT, 4, P])
        sc = s.sb("sc", [P, 2, HU, 2 * QB])
        p = s.sb("p", [P, 4, HU, 2 * QB])
        pt = s.sb("pt", [P, 2, HU, 2, QB])
        ow = s.sb("ow", [P, TT, OW])
        gate = s.sb("gate", [P, 2])
        t_ps = s.ps("t_ps", [P, 4, P])
        s_ps = s.ps("s_ps", [P, 2, 2, 2, 2 * QB])
        pt_ps = s.ps("pt_ps", [P, 2, 2, 2, QB])
        o_ps = s.ps("o_ps", [P, HEADS, HD])

        ident_step = s.sem("ident_step")
        consts = s.sem("consts")
        setup_in = s.sem("setup_in")
        trow_mm = s.sem("trow_mm")
        trow_ev = s.sem("trow_ev")
        trow_out = s.sem("trow_out")
        bias_in = [s.sem(f"bias_in{b}") for b in range(NB)]
        exchanged = s.sem("exchanged")
        flip_mm = s.sem("flip_mm")
        flip_ev = s.sem("flip_ev")
        gqk_done = s.sem("gqk_done")
        qk_loaded = [s.sem(f"qk_loaded{j}") for j in range(TT)]
        v_loaded = [s.sem(f"v_loaded{j}") for j in range(TT)]
        qT = s.sem("qT")
        qT_ev = s.sem("qT_ev")
        kT = s.sem("kT")
        kT_ev = s.sem("kT_ev")
        qk_done = s.sem("qk_done")
        gated = s.sem("gated")
        sc_done = s.sem("sc_done")
        p_done = s.sem("p_done")
        pt_done = [s.sem(f"pt_done{j}") for j in range(2)]
        pt_ev = [s.sem(f"pt_ev{j}") for j in range(2)]
        pv_done = s.sem("pv_done")
        o_ev = s.sem("o_ev")
        stored = [s.sem(f"stored{j}") for j in range(TT)]

        block = s.block()

        def groups(engine, body):
            body(0, 0, 0, True)
            with engine.Fori(1, NG) as G:
                body(0, G, G, False)
            with engine.Fori(NG, 2 * NG) as G:
                body(1, G, G - NG, False)
            body(2, 2 * NG, 0, True)
            with engine.Fori(2 * NG + 1, 3 * NG) as G:
                body(2, G, G - 2 * NG, False)

        def halves(b, peeled, j):
            if j < 0:
                return (1,) if b == 2 and not peeled else (0, 1)
            return (1,) if b == 2 or (b == 1 and j == 0) or (b == 0 and peeled and j == 0) else (0, 1)

        def tile_rows(t, b, i, j):
            v = t.rearrange("(n q d) c -> n d q c", d=BRANCHES[b][1], q=QB)
            if b == 0:
                v = v[bass.ds(TT * i + j, 1), 0, :, :]
            elif b == 1:
                v = v[j, bass.ds(i, 1), :, :]
            else:
                v = v[0, bass.ds(TT * i + j, 1), :, :]
            return v.rearrange("a q c -> (a q) c")

        @block.sync
        def _(sync):
            sync.dma_start(rel[0:BUCKETS, :], rel_table).then_inc(setup_in, 16)
            sync.dma_start(oh[:, :], one_hot).then_inc(setup_in, 16)
            with nc.allow_non_contiguous_dma(reason="64 gains, one to a partition"):
                for h in range(2):
                    dims = slice(h * HD, (h + 1) * HD)
                    sync.dma_start(gq[dims, :], q_norm.rearrange("a d -> d a")).then_inc(setup_in, 16)
                    sync.dma_start(gk[dims, :], k_norm.rearrange("a d -> d a")).then_inc(setup_in, 16)

            def body(b, G, i, peeled):
                for j in range(TT):
                    wait(sync, kT, TT * (G - 1) + j + 1)
                    sync.dma_start(qk_in[:, j, :], tile_rows(qkv, b, i, j)[:, 0:2 * D_ATTN]
                                   ).then_inc(qk_loaded[j], 16)
                    wait(sync, pv_done, UG * (G - 1) + 2 * (j + 1) + 2)
                    sync.dma_start(v_in[:, j, :], tile_rows(qkv, b, i, j)[:, 2 * D_ATTN:]
                                   ).then_inc(v_loaded[j], 16)

            groups(sync, body)

        @block.gpsimd
        def _(pool):
            pool.memset(ident[:, :], 0.0).then_inc(ident_step, 1)
            pool.wait_ge(ident_step, 1)
            pool.affine_select(out=exchange[:, :], in_=ident[:, :], compare_op=ALU.not_equal, fill=1.0,
                               base=1 - P, pattern=[[1, P]], channel_multiplier=1).then_inc(exchanged, 1)
            pool.wait_ge(exchanged, 1)
            pool.affine_select(out=ident[:, :], in_=ident[:, :], compare_op=ALU.not_equal, fill=1.0, base=0,
                               pattern=[[-1, P]], channel_multiplier=1).then_inc(consts, 1)
            pool.wait_ge(trow_ev, NB)
            pool.dma_start(toeplitz, trow[:, :]).then_inc(trow_out, 16)
            pool.wait_ge(trow_out, 16)
            for b in range(NB):
                src = bass.AP(toeplitz.tensor, b * TW, [[1, P], [NB * TW, HEADS], [1, 2 * QB]])
                pool.dma_start(bias[:, b, :, :], src).then_inc(bias_in[b], 16)

            def body(b, G, i, peeled):
                for j in range(TT):
                    pool.wait_ge(o_ev, TT * G + j + 1)
                    pool.dma_start(tile_rows(attn_o[b * SEQ:(b + 1) * SEQ, :], b, i, j), ow[:, j, :]
                                   ).then_inc(stored[j], 16)

            groups(pool, body)
            for j in range(TT):
                pool.wait_ge(stored[j], 16 * NB * NG)

        @block.scalar
        def _(act):
            act.wait_ge(gqk_done, 1)

            def pt_copy(V, k, w):
                act.wait_ge(pt_done[0], V + 1)
                wait(act, pv_done, V - 1)
                act.activation(pt[:, k % 2, 0:2, w[0]:2, :], pt_ps[:, 0, :, w[0]:2, :], ACT.Copy
                               ).then_inc(pt_ev[0], 1)

            def body(b, G, i, peeled):
                for k in range(UG):
                    U, j, hq = UG * G + k, k // 2, k % 2
                    T = TT * G + j
                    if hq == 0:
                        act.wait_ge(qT, T + 1)
                        wait(act, qk_done, 2 * (T - 1))
                        act.activation(q_t[:, j % 2, :, :], t_ps[:, :, :], ACT.Copy, scale=gqk[:, 0:1]
                                       ).then_inc(qT_ev, 1)
                    if not (isinstance(G, int) and G == 0 and k < TRL):
                        pt_copy(U - TRL, k, halves(b, peeled, (k - TRL) // 2))
                    if hq == 0:
                        act.wait_ge(kT, T + 1)
                        act.activation(k_t[:, j, :, :], t_ps[:, :, :], ACT.Copy).then_inc(kT_ev, 1)
                    w = halves(b, peeled, j)[0] * QB
                    for x in range(HU):
                        h = HU * hq + x
                        act.wait_ge(sc_done, HU * U + x + 1)
                        if x == 0:
                            for q in range(2):
                                wait(act, pt_done[q], U - 3)
                        act.activation(p[:, k % 4, x, w:], sc[:, k % 2, x, w:], ACT.Exp, scale=-1.0,
                                       bias=ow[:, j, D_ATTN + h:D_ATTN + h + 1],
                                       accum_out=ow[:, j, D_ATTN + HEADS + h:D_ATTN + HEADS + h + 1]
                                       ).then_inc(p_done, 1)

            groups(act, body)
            for k in range(TRL):
                pt_copy(UG * 3 * NG + k - TRL, k, (1,))

        @block.vector
        def _(dve):
            dve.memset(rel[BUCKETS:BUCKETS + 1, :], NEG).then_inc(consts, 1)
            dve.wait_ge(setup_in, 16 * 6)
            dve.tensor_tensor(gqk[:, :], gq[:, :], gk[:, :], ALU.mult).then_inc(gated, 1)
            dve.wait_ge(gated, 1)
            dve.tensor_scalar(gqk[:, :], gqk[:, :], HD * HD ** -0.5, None, ALU.mult).then_inc(gqk_done, 1)
            for b in range(NB):
                dve.wait_ge(trow_mm, b + 1)
                dve.tensor_copy(trow[:, b * TW:(b + 1) * TW], s_ps[0:HEADS, 0, b % 2, :, :]
                                .rearrange("p a n -> p (a n)")[:, 0:TW]).then_inc(trow_ev, 1)
            for n in range(NB * HEADS):
                dve.wait_ge(flip_mm, n + 1)
                dve.tensor_copy(bias[:, n // HEADS, n % HEADS, :], s_ps[:, n % 2, 0, 0, :]).then_inc(flip_ev, 1)
            dve.wait_ge(flip_ev, NB * HEADS)

            def pt_copy(V, k, w):
                dve.wait_ge(pt_done[1], V + 1)
                wait(dve, pv_done, V - 1)
                dve.tensor_copy(pt[:, k % 2, 2:4, w[0]:2, :], pt_ps[:, 1, :, w[0]:2, :]).then_inc(pt_ev[1], 1)

            def o_copy(V, j):
                dve.wait_ge(pv_done, V + 1)
                dve.tensor_copy(ow[:, j % TT, 0:D_ATTN], o_ps[:, :, :].rearrange("p h d -> p (h d)")
                                ).then_inc(o_ev, 1)

            def body(b, G, i, peeled):
                for k in range(UG):
                    U, j, hq = UG * G + k, k // 2, k % 2
                    if not (isinstance(G, int) and G == 0 and k < TRL):
                        pt_copy(U - TRL, k, halves(b, peeled, (k - TRL) // 2))
                    if hq == 0 and not (isinstance(G, int) and G == 0 and k < PVL):
                        o_copy(U - PVL, (k - PVL) // 2)
                    w = halves(b, peeled, j)[0] * QB
                    for x in range(HU):
                        h, pp, o = HU * hq + x, x // 2, x % 2
                        if x == 0:
                            dve.wait_ge(qk_done, U + 1)
                            wait(dve, p_done, HU * (U - 1))
                            if hq == 0:
                                wait(dve, stored[j], 16 * G)
                            dve.wait_ge(gated, U + 1)
                            dve.tensor_copy(gate[:, 0:1], gqk[:, :]).then_inc(gated, 1)
                        dve.tensor_tensor_reduce(
                            sc[:, k % 2, x, w:], s_ps[:, k % 2, o, pp, w:], bias[:, b, h, w:], -1.0, BIG,
                            ALU.add, ALU.min, ow[:, j, D_ATTN + h:D_ATTN + h + 1]).then_inc(sc_done, 1)

            groups(dve, body)
            last = UG * 3 * NG
            pt_copy(last - 2, 0, (1,))
            o_copy(last - 3, TT - 2)
            pt_copy(last - 1, 1, (1,))
            o_copy(last - 1, TT - 1)

        @block.tensor
        def _(pe):
            pe.wait_ge(consts, 2)
            pe.wait_ge(setup_in, 16 * 6)
            for b in range(NB):
                if b == 2:
                    pe.wait_ge(trow_ev, 1)
                pe.matmul(s_ps[0:HEADS, 0, b % 2, :, :].rearrange("p a n -> p (a n)")[:, 0:TW], rel[:, :],
                          oh[:, b * TW:(b + 1) * TW], start=True, stop=True).then_inc(trow_mm, 1)
            pe.wait_ge(trow_ev, NB)
            for n in range(NB * HEADS):
                if n % HEADS == 0:
                    pe.wait_ge(bias_in[n // HEADS], 16)
                wait(pe, flip_ev, n - 1)
                pe.matmul(s_ps[:, n % 2, 0, 0, :], exchange[:, :], bias[:, n // HEADS, n % HEADS, :],
                          start=True, stop=True).then_inc(flip_mm, 1)
            pe.wait_ge(flip_ev, NB * HEADS)

            def transposes(T, j, of, c0, done):
                for k in range(4):
                    ins = pe.transpose(t_ps[:, k, :], qk_in[:, j, c0 + k * P:c0 + (k + 1) * P], ident[:, :])
                ins.then_inc(done, 1)

            def p_transposes(V, k, w):
                for pp in range(2):
                    pe.wait_ge(p_done, HU * V + 2 * pp + 2)
                    wait(pe, pt_ev[pp], V)
                    for o in range(2):
                        for n in w:
                            ins = pe.transpose(pt_ps[:, pp, o, n, :], p[:, (k - TRL) % 4, 2 * pp + o, n * QB:(n + 1) * QB],
                                               ident[:, :])
                    ins.then_inc(pt_done[pp], 1)

            def pv(V, G, k, w):
                j, hq = k // 2, k % 2
                for pp in range(2):
                    pe.wait_ge(pt_ev[pp], V + 1)
                if hq == 0:
                    pe.wait_ge(v_loaded[j], 16 * (G + 1))
                    wait(pe, o_ev, TT * G + j)
                for x in range(HU):
                    h = HU * hq + x
                    for n in w:
                        ins = pe.matmul(o_ps[:, h, :], pt[:, k % 2, x, n, :],
                                        v_in[:, (j - 1 + n) % TT, h * HD:(h + 1) * HD],
                                        start=(n == w[0]), stop=(n == 1))
                ins.then_inc(pv_done, 1)

            def body(b, G, i, peeled):
                for k in range(UG):
                    U, j, hq = UG * G + k, k // 2, k % 2
                    T, w = TT * G + j, halves(b, peeled, j)
                    start = isinstance(G, int) and G == 0
                    if hq == 0:
                        pe.wait_ge(qk_loaded[j], 16 * (G + 1))
                        wait(pe, kT_ev, T)
                        transposes(T, j, "q", 0, qT)
                    if not (start and k < TRL):
                        p_transposes(U - TRL, k, halves(b, peeled, (k - TRL) // 2))
                    if hq == 0:
                        pe.wait_ge(qT_ev, T + 1)
                        transposes(T, j, "k", D_ATTN, kT)
                    if not (start and k < PVL):
                        kk = (k - PVL) % UG
                        pv(U - PVL, G if k >= PVL else G - 1, kk, halves(b, peeled, (k - PVL) // 2))
                    if hq == 0:
                        pe.wait_ge(kT_ev, T + 1)
                    wait(pe, sc_done, HU * (U - 1))
                    for pp in range(2):
                        for n in w:
                            for o in range(2):
                                dims = slice(o * HD, (o + 1) * HD)
                                ins = pe.matmul(s_ps[:, k % 2, o, pp, n * QB:(n + 1) * QB],
                                                q_t[dims, j % 2, 2 * hq + pp, :],
                                                k_t[dims, (j - 1 + n) % TT, 2 * hq + pp, :], start=True, stop=True)
                    ins.then_inc(qk_done, 1)

            groups(pe, body)
            last = UG * 3 * NG
            p_transposes(last - 2, 0, (1,))
            pv(last - 3, 3 * NG - 1, UG - 3, (1,))
            p_transposes(last - 1, 1, (1,))
            pv(last - 2, 3 * NG - 1, UG - 2, (1,))
            pv(last - 1, 3 * NG - 1, UG - 1, (1,))



def mix(nc, x, attn_o, rnn_t, norm_attn, norm_rnn, w_out, norm_ffn, wr_g, br_g, wr_e, br_e,
                  x2_d, h_d, lg):
    NB = len(BRANCHES)
    CT = D_RNN // P
    NR = GROUPS + EXPERTS
    LAG = 2

    with Scope(nc, "c") as s:
        ident = s.sb("ident", [P, P])
        ones = s.sb("ones", [P, P])
        ob = s.sb("ob", [P, 2, NB, OW])
        x_t = s.sb("x_t", [P, 2, DM])
        rt = s.sb("rt", [P, 2, CT, P])
        rsq = s.sb("rsq", [P, CT, P])
        rg = s.sb("rg", [P, CT, P])
        wb = s.sb("wb", [P, NB, D_ATTN])
        at = s.sb("at", [P, D_ATTN])
        junk = s.sb("junk", [P, DM])
        sm = s.sb("sm", [P, 4, NB, HEADS])
        sh = s.sb("sh", [P, 3, HEADS])
        st = s.sb("st", [P, 6])
        half = s.sb("half", [P, 1])
        eps_a = s.sb("eps_a", [P, 1])
        eps_x = s.sb("eps_x", [P, 1])
        ga = s.sb("ga", [P, D_ATTN])
        gf = s.sb("gf", [P, DM])
        gr = s.sb("gr", [P, CT])
        a_hi = s.sb("a_hi", [P, 4, P], F32R)
        a_lo = s.sb("a_lo", [P, 4, P], F32R)
        r_hi = s.sb("r_hi", [P, CT, P], F32R)
        r_lo = s.sb("r_lo", [P, CT, P], F32R)
        w_raw = s.sb("w_raw", [P, 2, DM])
        w_hi = s.sb("w_hi", [P, KM, DM], F32R)
        w_lo = s.sb("w_lo", [P, KM, DM], F32R)
        h_t = s.sb("h_t", [P, 2, DM])
        ht = s.sb("ht", [P, KM, P])
        wr = s.sb("wr", [P, KM, NR])
        br = s.sb("br", [P, NR])
        a_ps = s.ps("a_ps", [P, 4, P])
        l_ps = s.ps("l_ps", [P, 512])
        y_ps = s.ps("y_ps", [P, 2, 2, 512])
        h_ps = s.ps("h_ps", [P, KM, P])

        two = range(2)
        gate_in = s.sem("gate_in")
        small_in = s.sem("small_in")
        pool_step = s.sem("pool_step")
        consts = s.sem("consts")
        wo_in = [s.sem(f"wo_in{j}") for j in two]
        wo_hi = s.sem("wo_hi")
        wo_lo = [s.sem(f"wo_lo{j}") for j in two]
        ob_in = [s.sem(f"ob_in{j}") for j in two]
        x_in = [s.sem(f"x_in{j}") for j in two]
        rt_in = [s.sem(f"rt_in{j}") for j in two]
        gains_done = s.sem("gains_done")
        jm_done = s.sem("jm_done")
        dm_done = s.sem("dm_done")
        em_done = s.sem("em_done")
        merge_step = s.sem("merge_step")
        wb_done = s.sem("wb_done")
        add1_done = s.sem("add1_done")
        at_done = s.sem("at_done")
        ssa_done = s.sem("ssa_done")
        ra_step = s.sem("ra_step")
        ra_done = s.sem("ra_done")
        an_done = s.sem("an_done")
        aT_done = s.sem("aT_done")
        ahi_done = s.sem("ahi_done")
        alo_done = s.sem("alo_done")
        rsq_done = s.sem("rsq_done")
        ssr_mm = s.sem("ssr_mm")
        ssr_ev = s.sem("ssr_ev")
        rr_done = s.sem("rr_done")
        rg_done = s.sem("rg_done")
        rhi_done = s.sem("rhi_done")
        rlo_done = s.sem("rlo_done")
        y_done = s.sem("y_done")
        x1_done = s.sem("x1_done")
        x2_done = s.sem("x2_done")
        ssx_done = s.sem("ssx_done")
        rx_step = s.sem("rx_step")
        rx_done = s.sem("rx_done")
        hn_done = s.sem("hn_done")
        x2_out = [s.sem(f"x2_out{j}") for j in two]
        h_out = [s.sem(f"h_out{j}") for j in two]
        hT_done = s.sem("hT_done")
        hT_ev = s.sem("hT_ev")
        lg_mm = s.sem("lg_mm")
        lg_ev = s.sem("lg_ev")

        block = s.block()

        def rows(ap, t):
            return ap.rearrange("(t p) c -> t p c", p=P)[bass.ds(t, 1), :, :].rearrange("a p c -> (a p) c")

        def tiles(engine, body):
            for t in range(2):
                body(t, t)
            with engine.Fori(1, TILES // 2) as i:
                for j in two:
                    body(2 * i + j, j)

        @block.sync
        def _(sync):
            wo_v = w_out[0].rearrange("(k p) n -> p k n", p=P)

            def load(m, j):
                t = 2 * m + j
                wait(sync, x2_done, 2 * m + j - 1)
                sync.dma_start(ob[:, j, :, :],
                               attn_o.rearrange("(b t p) c -> t p b c", b=NB, p=P)[bass.ds(t, 1), :, :, :]
                               .rearrange("a p b c -> (a p) b c")).then_inc(ob_in[j], 16)
                sync.dma_start(rt[:, j, :, :],
                               rnn_t.rearrange("(k p) (t n) -> t p k n", p=P, n=P)[bass.ds(t, 1), :, :, :]
                               .rearrange("a p k n -> (a p) k n")).then_inc(rt_in[j], 16)
                wait(sync, x2_out[j], 16 * m)
                sync.dma_start(x_t[:, j, :], rows(x[0], t)).then_inc(x_in[j], 16)

            def store(m, j):
                sync.wait_ge(x2_done, 2 * m + j + 1)
                sync.dma_start(rows(x2_d, 2 * m + j), x_t[:, j, :]).then_inc(x2_out[j], 16)
                sync.wait_ge(hn_done, 2 * m + j + 1)
                sync.dma_start(rows(h_d, 2 * m + j), h_t[:, j, :]).then_inc(h_out[j], 16)

            load(0, 0)
            sync.dma_start(ga[:, :], norm_attn.to_broadcast([P, D_ATTN])).then_inc(small_in, 16)
            sync.dma_start(gf[:, :], norm_ffn.to_broadcast([P, DM])).then_inc(small_in, 16)
            sync.dma_start(br[:, 0:GROUPS], br_g.to_broadcast([P, GROUPS])).then_inc(small_in, 16)
            sync.dma_start(br[:, GROUPS:], br_e.to_broadcast([P, EXPERTS])).then_inc(small_in, 16)
            sync.dma_start(wr[:, :, 0:GROUPS], wr_g[0].rearrange("(k p) n -> p k n", p=P)).then_inc(small_in, 16)
            sync.dma_start(wr[:, :, GROUPS:], wr_e[0].rearrange("(k p) n -> p k n", p=P)).then_inc(small_in, 16)
            with nc.allow_non_contiguous_dma(reason="512 gains, by channel"):
                sync.dma_start(gr[:, :], column(norm_rnn, CT)).then_inc(small_in, 16)
            for k in range(KM):
                wait(sync, wo_lo[k % 2], k // 2)
                sync.dma_start(w_raw[:, k % 2, :], wo_v[:, k, :]).then_inc(wo_in[k % 2], 16)
            load(0, 1)
            with sync.Fori(1, TILES // 2) as m:
                for j in two:
                    store(m - 1, j)
                    load(m, j)
            for j in two:
                store(TILES // 2 - 1, j)
            for j in two:
                sync.wait_ge(x2_out[j], 16 * TILES // 2)
                sync.wait_ge(h_out[j], 16 * TILES // 2)

        @block.gpsimd
        def _(pool):
            pool.memset(half[:, :], -0.5).then_inc(pool_step, 1)
            pool.memset(eps_a[:, :], D_ATTN * EPS).then_inc(pool_step, 1)
            pool.memset(eps_x[:, :], DM * EPS).then_inc(pool_step, 1)
            pool.memset(ident[:, :], 0.0).then_inc(pool_step, 1)
            pool.memset(ones[:, :], 1.0).then_inc(pool_step, 1)
            pool.wait_ge(pool_step, 5)
            pool.affine_select(out=ident[:, :], in_=ident[:, :], compare_op=ALU.not_equal, fill=1.0, base=0,
                               pattern=[[-1, P]], channel_multiplier=1).then_inc(consts, 1)

            def body(t, j):
                m1 = t + 1
                pool.wait_ge(rt_in[j], 16 * (t // 2 + 1) if isinstance(t, int) else 8 * (t - j) + 16)
                wait(pool, ssr_mm, t)
                pool.tensor_tensor(rsq[:, :, :], rt[:, j, :, :], rt[:, j, :, :], ALU.mult).then_inc(rsq_done, 1)
                pool.wait_ge(wb_done, m1)
                wait(pool, at_done, t)
                pool.tensor_tensor(at[:, :], wb[:, 0, :], wb[:, 1, :], ALU.add).then_inc(add1_done, 1)
                for done, ss, step, eps, out, rdone in (
                        (ssr_ev, 1, None, None, 4, rr_done), (ssa_done, 0, ra_step, eps_a, 3, ra_done),
                        (ssx_done, 2, rx_step, eps_x, 5, rx_done)):
                    pool.wait_ge(done, m1)
                    src = st[:, ss:ss + 1]
                    if step is not None:
                        pool.tensor_tensor(st[:, out:out + 1], src, eps[:, :], ALU.add).then_inc(step, 1)
                        pool.wait_ge(step, m1)
                        src = st[:, out:out + 1]
                    pool.tensor_tensor(st[:, out:out + 1], src, half[:, :], ALU.pow).then_inc(rdone, 1)

            tiles(pool, body)

        @block.scalar
        def _(act):
            for k in range(KM):
                act.wait_ge(wo_in[k % 2], 16 * (k // 2 + 1))
                act.activation(w_hi[:, k, :], w_raw[:, k % 2, :], ACT.Copy).then_inc(wo_hi, 1)

            def lagged(t):
                act.wait_ge(hT_done, t + 1)
                wait(act, lg_mm, t)
                act.activation(ht[:, :, :], h_ps[:, :, :], ACT.Copy).then_inc(hT_ev, 1)

            def body(t, j):
                act.wait_ge(dm_done, t + 1)
                act.activation(sm[:, 1, :, :], sm[:, 0, :, :], ACT.Exp).then_inc(em_done, 1)
                act.wait_ge(rg_done, t + 1)
                wait(act, y_done, t)
                act.activation(r_hi[:, :, :], rg[:, :, :], ACT.Copy).then_inc(rhi_done, 1)
                act.wait_ge(at_done, t + 1)
                wait(act, ssx_done, t)
                act.activation(junk[:, 0:D_ATTN], at[:, :], ACT.Square, accum_out=st[:, 0:1]).then_inc(ssa_done, 1)
                act.wait_ge(aT_done, t + 1)
                act.activation(a_hi[:, :, :], a_ps[:, :, :], ACT.Copy).then_inc(ahi_done, 1)
                if not (isinstance(t, int) and t < LAG):
                    lagged(t - LAG)
                act.wait_ge(x2_done, t + 1)
                act.wait_ge(ssa_done, t + 1)
                act.activation(junk[:, :], x_t[:, j, :], ACT.Square, accum_out=st[:, 2:3]).then_inc(ssx_done, 1)

            tiles(act, body)
            for t in range(TILES - LAG, TILES):
                lagged(t)

        @block.vector
        def _(dve):
            dve.wait_ge(small_in, 16 * 7)
            dve.tensor_scalar(ga[:, :], ga[:, :], D_ATTN ** 0.5, None, ALU.mult).then_inc(gains_done, 1)
            dve.tensor_scalar(gr[:, :], gr[:, :], D_RNN ** 0.5, None, ALU.mult).then_inc(gains_done, 1)
            dve.tensor_scalar(gf[:, :], gf[:, :], DM ** 0.5, None, ALU.mult).then_inc(gains_done, 1)
            dve.wait_ge(gains_done, 3)
            for k in range(KM):
                dve.wait_ge(wo_hi, k + 1)
                dve.tensor_tensor(w_lo[:, k, :], w_raw[:, k % 2, :], w_hi[:, k, :].bitcast(F32), ALU.subtract
                                  ).then_inc(wo_lo[k % 2], 1)

            def lagged(t):
                dve.wait_ge(lg_mm, t + 1)
                dve.tensor_tensor(lg[:, bass.ds(t, 1), :].rearrange("p a n -> p (a n)"), l_ps[:, 64:64 + NR],
                                  br[:, :], ALU.add).then_inc(lg_ev, 1)

            MS = 4

            def body(t, j):
                n_in = 16 * (t // 2 + 1) if isinstance(t, int) else 8 * (t - j) + 16
                neg_m = ob[:, j, :, D_ATTN:D_ATTN + HEADS]
                den = ob[:, j, :, D_ATTN + HEADS:]
                dve.wait_ge(ob_in[j], n_in)
                dve.tensor_reduce(sh[:, 0, :], neg_m.rearrange("p b h -> p h b"), X, ALU.min).then_inc(jm_done, 1)
                dve.wait_ge(jm_done, t + 1)
                dve.tensor_tensor(sm[:, 0, :, :], sh[:, 0, :].unsqueeze(1).to_broadcast([P, NB, HEADS]), neg_m,
                                  ALU.subtract).then_inc(dm_done, 1)
                dve.wait_ge(rt_in[j], n_in)
                wait(dve, rlo_done, t)
                dve.tensor_tensor(rg[:, :, :], rt[:, j, :, :], gr[:, :].unsqueeze(2).to_broadcast([P, CT, P]),
                                  ALU.mult).then_inc(rg_done, 1)
                dve.wait_ge(em_done, t + 1)
                dve.tensor_tensor(sm[:, 2, :, :], sm[:, 1, :, :], den, ALU.mult).then_inc(merge_step, 1)
                dve.wait_ge(merge_step, MS * t + 1)
                dve.tensor_reduce(sh[:, 1, :], sm[:, 2, :, :].rearrange("p b h -> p h b"), X, ALU.add
                                  ).then_inc(merge_step, 1)
                dve.wait_ge(merge_step, MS * t + 2)
                dve.reciprocal(sh[:, 2, :], sh[:, 1, :]).then_inc(merge_step, 1)
                dve.wait_ge(merge_step, MS * t + 3)
                dve.tensor_tensor(sm[:, 3, :, :], sm[:, 1, :, :],
                                  sh[:, 2, :].unsqueeze(1).to_broadcast([P, NB, HEADS]), ALU.mult
                                  ).then_inc(merge_step, 1)
                dve.wait_ge(merge_step, MS * t + 4)
                dve.tensor_tensor(wb[:, :, :].rearrange("p b (h d) -> p b h d", d=HD),
                                  ob[:, j, :, 0:D_ATTN].rearrange("p b (h d) -> p b h d", d=HD),
                                  sm[:, 3, :, :].unsqueeze(3).to_broadcast([P, NB, HEADS, HD]), ALU.mult
                                  ).then_inc(wb_done, 1)
                dve.wait_ge(rhi_done, t + 1)
                dve.tensor_tensor(r_lo[:, :, :], rg[:, :, :], r_hi[:, :, :].bitcast(F32), ALU.subtract
                                  ).then_inc(rlo_done, 1)
                dve.wait_ge(ssr_mm, t + 1)
                dve.wait_ge(add1_done, t + 1)
                wait(dve, rr_done, t)
                dve.tensor_scalar(st[:, 1:2], l_ps[:, 0:1], D_RNN * EPS, None, ALU.add).then_inc(ssr_ev, 1)
                dve.tensor_tensor(at[:, :], at[:, :], wb[:, 2, :], ALU.add).then_inc(at_done, 1)
                dve.wait_ge(ra_done, t + 1)
                dve.scalar_tensor_tensor(out=at[:, :], in0=at[:, :], scalar=st[:, 3:4], in1=ga[:, :],
                                         op0=ALU.mult, op1=ALU.mult).then_inc(an_done, 1)
                dve.wait_ge(ahi_done, t + 1)
                dve.tensor_tensor(a_lo[:, :, :], a_ps[:, :, :], a_hi[:, :, :].bitcast(F32), ALU.subtract
                                  ).then_inc(alo_done, 1)
                if not (isinstance(t, int) and t < LAG):
                    lagged(t - LAG)
                dve.wait_ge(y_done, t + 1)
                dve.wait_ge(rr_done, t + 1)
                dve.wait_ge(x_in[j], n_in)
                xv = x_t[:, j, :]
                dve.scalar_tensor_tensor(out=xv, in0=y_ps[:, 1, :, :].rearrange("p a n -> p (a n)"),
                                         scalar=st[:, 4:5], in1=xv, op0=ALU.mult, op1=ALU.add
                                         ).then_inc(x1_done, 1)
                dve.wait_ge(x1_done, t + 1)
                dve.tensor_tensor(xv, y_ps[:, 0, :, :].rearrange("p a n -> p (a n)"), xv, ALU.add
                                  ).then_inc(x2_done, 1)
                dve.wait_ge(rx_done, t + 1)
                wait(dve, h_out[j], 16 * (t // 2) if isinstance(t, int) else 8 * (t - j))
                wait(dve, hT_done, t - 1)
                dve.scalar_tensor_tensor(out=h_t[:, j, :], in0=xv, scalar=st[:, 5:6], in1=gf[:, :],
                                         op0=ALU.mult, op1=ALU.mult).then_inc(hn_done, 1)

            tiles(dve, body)
            for t in range(TILES - LAG, TILES):
                lagged(t)

        @block.tensor
        def _(pe):
            pe.wait_ge(consts, 1)

            def lagged(t, j):
                pe.wait_ge(hn_done, t + 1)
                wait(pe, hT_ev, t)
                for k in range(KM):
                    ins = pe.transpose(h_ps[:, k, :], h_t[:, j, k * P:(k + 1) * P], ident[:, :])
                ins.then_inc(hT_done, 1)

            def router(t):
                pe.wait_ge(hT_ev, t + 1)
                wait(pe, lg_ev, t)
                for k in range(KM):
                    ins = pe.matmul(l_ps[:, 64:64 + NR], ht[:, k, :], wr[:, k, :], start=(k == 0), stop=(k == KM - 1))
                ins.then_inc(lg_mm, 1)

            def body(t, j):
                pe.wait_ge(rsq_done, t + 1)
                if not (isinstance(t, int) and t < LAG + 1):
                    wait(pe, lg_ev, t - LAG)
                for k in range(CT):
                    ins = pe.matmul(l_ps[:, 0:1], rsq[:, k, :], ones[:, 0:1], start=(k == 0), stop=(k == CT - 1))
                ins.then_inc(ssr_mm, 1)
                pe.wait_ge(an_done, t + 1)
                for k in range(4):
                    ins = pe.transpose(a_ps[:, k, :], at[:, k * P:(k + 1) * P], ident[:, :])
                ins.then_inc(aT_done, 1)
                if not (isinstance(t, int) and t < LAG):
                    lagged(t - LAG, j)
                if isinstance(t, int) and t == 0:
                    for q in two:
                        pe.wait_ge(wo_lo[q], KM // 2)
                pe.wait_ge(rlo_done, t + 1)
                wait(pe, x2_done, t)
                for part, s_hi, s_lo in ((1, r_hi, r_lo), (0, a_hi, a_lo)):
                    if part == 0:
                        pe.wait_ge(alo_done, t + 1)
                    for n in two:
                        cols = slice(n * 512, (n + 1) * 512)
                        for k in range(4):
                            kk = 4 * part + k
                            out = y_ps[:, part, n, :]
                            pe.matmul(out, s_lo[:, k, :], w_hi[:, kk, cols], start=(k == 0), stop=False)
                            pe.matmul(out, s_hi[:, k, :], w_lo[:, kk, cols], start=False, stop=False)
                            ins = pe.matmul(out, s_hi[:, k, :], w_hi[:, kk, cols], start=False, stop=(k == 3))
                ins.then_inc(y_done, 1)
                if not (isinstance(t, int) and t < LAG):
                    pe.wait_ge(ssr_ev, t + 1)
                    router(t - LAG)

            tiles(pe, body)
            for t in range(TILES - LAG, TILES):
                lagged(t, t % 2)
                router(t)


B_EXP, B_FIRST, B_NEW, B_ORD, B_COUNT = (i * (MAX_BLOCKS + 1) for i in range(5))


def route(nc, lg, slots_d, gates, slots, table):
    NB = MAX_BLOCKS + 1
    T, E, G, EG = TILES, EXPERTS, GROUPS, PER_GROUP

    with Scope(nc, "d") as s:
        ones = s.sb("ones", [P, P])
        upper = s.sb("upper", [P, P])
        iota = s.sb("iota", [P, E])
        iota_b = s.sb("iota_b", [P, NB])
        start = s.sb("start", [P, 2, E])
        tok = s.sb("tok", [P, T], I32)
        gd = s.sb("gd", [P, T, G])
        geq = s.sb("geq", [P, T, G])
        goh = s.sb("goh", [P, T, G])
        eg = s.sb("eg", [P, T, G])
        el = s.sb("el", [P, T, G, EG])
        e8 = s.sb("e8", [P, 2, T, EG])
        eq = s.sb("eq", [P, T, EG])
        o = s.sb("o", [P, 2, T, EG])
        v = s.sb("v", [P, 12, T])
        oh = s.sb("oh", [P, 2, T, E])
        both = s.sb("both", [P, T, E])
        sums = s.sb("sums", [P, T + 1, E])
        rank = s.sb("rank", [P, T, E])
        place = s.sb("place", [P, T, E])
        prod = s.sb("prod", [P, T, E])
        more = s.sb("more", [P, E, T])
        nb = s.sb("nb", [P, E])
        pend = s.sb("pend", [P, E])
        pos = s.sb("pos", [P, 2, T])
        zeros = s.sb("zeros", [P, 1], I32)
        le = s.sb("le", [P, 3, NB, E])
        bv = s.sb("bv", [P, 8, NB])
        bt = s.sb("bt", [P, 4 * NB + 1])
        r_ps = s.ps("r_ps", [P, T, E])
        c_ps = s.ps("c_ps", [P, T, E])

        const_step = s.sem("const_step")
        consts = s.sem("consts")
        step = s.sem("step")
        gd_done = s.sem("gd_done")
        eg_done = s.sem("eg_done")
        d_done = s.sem("d_done")
        ex_done = s.sem("ex_done")
        both_done = s.sem("both_done")
        rank_mm = s.sem("rank_mm")
        slots_done = s.sem("slots_done")
        scattered = s.sem("scattered")
        tail_out = s.sem("tail_out")

        block = s.block()

        @block.gpsimd
        def _(pool):
            pool.memset(ones[:, :], 1.0).then_inc(const_step, 1)
            pool.wait_ge(const_step, 1)
            pool.affine_select(out=upper[:, :], in_=ones[:, :], compare_op=ALU.is_gt, fill=0.0, base=0,
                               pattern=[[1, P]], channel_multiplier=-1).then_inc(consts, 1)
            pool.iota(iota[:, :], [[1, E]], base=0, channel_multiplier=0,
                      allow_small_or_imprecise_dtypes=True).then_inc(consts, 1)
            pool.iota(iota_b[:, :], [[1, NB]], base=0, channel_multiplier=0,
                      allow_small_or_imprecise_dtypes=True).then_inc(consts, 1)
            pool.memset(zeros[:, :], 0).then_inc(consts, 1)
            pool.iota(tok[:, :], [[P, T]], base=0, channel_multiplier=1).then_inc(consts, 1)
            pool.wait_ge(consts, 5)
            pool.dma_start(slots_d[TOP_K * SEQ:, :], zeros[:, :]).then_inc(tail_out, 16)
            pool.wait_ge(slots_done, 1)
            for k in range(TOP_K):
                for t in range(T):
                    pool.indirect_dma_start(slots_d[0:TOP_K * SEQ, :],
                                            bass.IndirectOffsetOnAxis(slots[:, k, t:t + 1], 0),
                                            tok[:, t:t + 1], None).then_inc(scattered, 16)
            pool.wait_ge(scattered, 16 * TOP_K * T)
            pool.wait_ge(tail_out, 16)

        @block.scalar
        def _(act):
            act.wait_ge(gd_done, 1)
            act.activation(eg[:, :, :], gd[:, :, :], ACT.Exp).then_inc(eg_done, 1)
            act.wait_ge(d_done, 1)
            act.activation(v[:, 7, :], v[:, 6, :], ACT.Exp).then_inc(ex_done, 1)

        @block.tensor
        def _(pe):
            pe.wait_ge(consts, 5)
            pe.wait_ge(both_done, 1)
            flat = both[:, :, :].rearrange("p t e -> p (t e)")
            pe.matmul(r_ps[:, :, :].rearrange("p t e -> p (t e)"), upper[:, :], flat, start=True, stop=True)
            pe.matmul(c_ps[:, :, :].rearrange("p t e -> p (t e)"), ones[:, :], flat, start=True, stop=True
                      ).then_inc(rank_mm, 1)

        @block.vector
        def _(dve):
            n = [0]

            def done():
                n[0] += 1
                return n[0]

            def op(out, a, b, alu):
                dve.tensor_tensor(out, a, b, alu).then_inc(step, 1)
                dve.wait_ge(step, done())

            def reduce(out, a, alu):
                dve.tensor_reduce(out, a, X, alu).then_inc(step, 1)
                dve.wait_ge(step, done())

            def scaled(out, a, c, b, o0, o1):
                dve.scalar_tensor_tensor(out=out, in0=a, scalar=c, in1=b, op0=o0, op1=o1).then_inc(step, 1)
                dve.wait_ge(step, done())

            def over_t(ap, m):
                return ap.unsqueeze(2).to_broadcast([P, T, m])

            def over_e(ap, m):
                return ap.unsqueeze(1).to_broadcast([P, T, m])

            dve.wait_ge(consts, 5)
            gl = lg[:, :, 0:G]
            reduce(v[:, 0, :], gl, ALU.max)
            op(gd[:, :, :], gl, over_t(v[:, 0, :], G), ALU.subtract)
            op(geq[:, :, :], gl, over_t(v[:, 0, :], G), ALU.is_equal)
            scaled(geq[:, :, :], geq[:, :, :], -100.0, over_e(iota[:, 0:G], G), ALU.mult, ALU.add)
            reduce(v[:, 1, :], geq[:, :, :], ALU.min)
            dve.tensor_tensor(goh[:, :, :], geq[:, :, :], over_t(v[:, 1, :], G), ALU.is_equal).then_inc(gd_done, 1)
            dve.wait_ge(gd_done, 1)
            op(el[:, :, :, :], lg[:, :, G:].rearrange("p t (g e) -> p t g e", e=EG),
               goh[:, :, :].unsqueeze(3).to_broadcast([P, T, G, EG]), ALU.mult)
            reduce(e8[:, 0, :, :], el[:, :, :, :].rearrange("p t g e -> p t e g"), ALU.add)
            dve.wait_ge(eg_done, 1)
            reduce(v[:, 2, :], eg[:, :, :], ALU.add)
            for k in range(TOP_K):
                reduce(v[:, 3 + k, :], e8[:, k, :, :], ALU.max)
                op(eq[:, :, :], e8[:, k, :, :], over_t(v[:, 3 + k, :], EG), ALU.is_equal)
                scaled(eq[:, :, :], eq[:, :, :], -100.0, over_e(iota[:, 0:EG], EG), ALU.mult, ALU.add)
                reduce(v[:, 5, :], eq[:, :, :], ALU.min)
                op(o[:, k, :, :], eq[:, :, :], over_t(v[:, 5, :], EG), ALU.is_equal)
                if k == 0:
                    scaled(e8[:, 1, :, :], o[:, 0, :, :], -BIG, e8[:, 0, :, :], ALU.mult, ALU.add)
            dve.tensor_tensor(v[:, 6, :], v[:, 4, :], v[:, 3, :], ALU.subtract).then_inc(d_done, 1)
            for k in range(TOP_K):
                op(oh[:, k, :, :].rearrange("p t (g e) -> p t g e", e=EG),
                   goh[:, :, :].unsqueeze(3).to_broadcast([P, T, G, EG]),
                   o[:, k, :, :].unsqueeze(2).to_broadcast([P, T, G, EG]), ALU.mult)
            dve.tensor_tensor(both[:, :, :], oh[:, 0, :, :], oh[:, 1, :, :], ALU.add).then_inc(both_done, 1)
            dve.wait_ge(ex_done, 1)
            scaled(v[:, 8, :], v[:, 7, :], 1.0, v[:, 2, :], ALU.add, ALU.mult)
            dve.reciprocal(v[:, 9, :], v[:, 8, :]).then_inc(step, 1)
            dve.wait_ge(step, done())
            dve.tensor_copy(gates[:, 0, :], v[:, 9, :]).then_inc(step, 1)
            done()
            op(gates[:, 1, :], v[:, 9, :], v[:, 7, :], ALU.mult)
            dve.wait_ge(rank_mm, 1)
            dve.memset(sums[:, 0, :], 0.0).then_inc(step, 1)
            dve.wait_ge(step, done())
            for t in range(T):
                op(sums[:, t + 1, :], sums[:, t, :], c_ps[:, t, :], ALU.add)
            op(rank[:, :, :], r_ps[:, :, :], sums[:, 0:T, :], ALU.add)
            dve.tensor_tensor_scan(start[:, 0, :], ones[:, 0:E], sums[:, T, :], 0.0, ALU.mult, ALU.add
                                   ).then_inc(step, 1)
            dve.wait_ge(step, done())
            op(start[:, 1, :], start[:, 0, :], sums[:, T, :], ALU.subtract)
            op(place[:, :, :], rank[:, :, :], over_e(start[:, 1, :], E), ALU.add)
            for k in range(TOP_K):
                op(prod[:, :, :], oh[:, k, :, :], place[:, :, :], ALU.mult)
                reduce(pos[:, k, :], prod[:, :, :], ALU.add)
            dve.tensor_copy(slots[:, :, :], pos[:, :, :]).then_inc(slots_done, 1)
            dve.tensor_scalar(bv[:, 0, 0:T], iota_b[:, 0:T], float(P), None, ALU.mult).then_inc(step, 1)
            dve.wait_ge(step, done())
            op(more[:, :, :], sums[:, T, :].unsqueeze(2).to_broadcast([P, E, T]),
               bv[:, 0, 0:T].unsqueeze(1).to_broadcast([P, E, T]), ALU.is_gt)
            reduce(nb[:, :], more[:, :, :], ALU.add)
            dve.tensor_tensor_scan(pend[:, :], ones[:, 0:E], nb[:, :], 0.0, ALU.mult, ALU.add).then_inc(step, 1)
            dve.wait_ge(step, done())
            op(le[:, 0, :, :], pend[:, :].unsqueeze(1).to_broadcast([P, NB, E]),
               iota_b[:, :].unsqueeze(2).to_broadcast([P, NB, E]), ALU.is_le)
            op(le[:, 1, :, :], le[:, 0, :, :], nb[:, :].unsqueeze(1).to_broadcast([P, NB, E]), ALU.mult)
            op(le[:, 2, :, :], le[:, 0, :, :], sums[:, T, :].unsqueeze(1).to_broadcast([P, NB, E]), ALU.mult)
            reduce(bv[:, 1, :], le[:, 0, :, :], ALU.add)
            reduce(bv[:, 2, :], le[:, 1, :, :], ALU.add)
            reduce(bv[:, 7, :], le[:, 2, :, :], ALU.add)
            dve.tensor_scalar(bt[:, B_EXP:B_EXP + NB], bv[:, 1, :], float(E - 1), None, ALU.min).then_inc(step, 1)
            dve.wait_ge(step, done())
            op(bv[:, 3, :], iota_b[:, :], bv[:, 2, :], ALU.subtract)
            scaled(bv[:, 5, :], bv[:, 3, :], float(P), bv[:, 7, :], ALU.mult, ALU.add)
            dve.tensor_scalar(bt[:, B_FIRST:B_FIRST + NB], bv[:, 5, :], float(TOP_K * SEQ), None, ALU.min
                              ).then_inc(step, 1)
            dve.tensor_scalar(bv[:, 6, :], bv[:, 1, :], float(E), None, ALU.is_lt).then_inc(step, 1)
            done()
            dve.wait_ge(step, done())
            scaled(bt[:, B_NEW:B_NEW + NB], bv[:, 3, :], 0.0, bv[:, 6, :], ALU.is_equal, ALU.mult)
            dve.tensor_tensor_scan(bt[:, B_ORD:B_ORD + NB], ones[:, 0:NB], bt[:, B_NEW:B_NEW + NB], -1.0,
                                   ALU.mult, ALU.add).then_inc(step, 1)
            dve.tensor_scalar(bt[:, B_COUNT:], pend[:, E - 1:], float(MIN_BLOCKS), None, ALU.subtract
                              ).then_inc(step, 1)
            done()
            dve.wait_ge(step, done())
            dve.tensor_copy(table[:, :], bt[:, :]).then_inc(step, 1)
            dve.wait_ge(step, done())


def experts(nc, table, slots_d, h_d, w_gate, w_up, w_down, y_d):
    KD = DE // P
    PC = 2

    with Scope(nc, "e") as s:
        ident = s.sb("ident", [P, P])
        idx = s.sb("idx", [P, 1], I32)
        gate_copy = s.sb("gate_copy", [P, 1])
        xr = s.sb("xr", [P, DM])
        x_hi = s.sb("x_hi", [P, KM, P], F32R)
        x_lo = s.sb("x_lo", [P, KM, P], F32R)
        g_raw = s.sb("g_raw", [P, KM, DE])
        u_raw = s.sb("u_raw", [P, KM, DE])
        d_raw = s.sb("d_raw", [P, KD, DM])
        g_hi = s.sb("g_hi", [P, KM, DE], F32R)
        g_lo = s.sb("g_lo", [P, KM, DE], F32R)
        u_hi = s.sb("u_hi", [P, KM, DE], F32R)
        u_lo = s.sb("u_lo", [P, KM, DE], F32R)
        d_hi = s.sb("d_hi", [P, KD, DM], F32R)
        d_lo = s.sb("d_lo", [P, KD, DM], F32R)
        sg = s.sb("sg", [P, DE])
        hm = s.sb("hm", [P, DE])
        m_hi = s.sb("m_hi", [P, KD, P], F32R)
        m_lo = s.sb("m_lo", [P, KD, P], F32R)
        yo = s.sb("yo", [P, DM])
        x_ps = s.ps("x_ps", [P, KM, P])
        g_ps = s.ps("g_ps", [P, DE])
        u_ps = s.ps("u_ps", [P, DE])
        m_ps = s.ps("m_ps", [P, KD, P])
        y_ps = s.ps("y_ps", [P, 2, 512])

        ident_step = s.sem("ident_step")
        consts = s.sem("consts")
        idx_in = s.sem("idx_in")
        gated = s.sem("gated")
        x_in = s.sem("x_in")
        xT_done = s.sem("xT_done")
        xhi_done = s.sem("xhi_done")
        xlo_done = s.sem("xlo_done")
        g_in = s.sem("g_in")
        u_in = s.sem("u_in")
        d_in = s.sem("d_in")
        ghi_done = s.sem("ghi_done")
        uhi_done = s.sem("uhi_done")
        dhi_done = s.sem("dhi_done")
        glo_done = s.sem("glo_done")
        ulo_done = s.sem("ulo_done")
        dlo_done = s.sem("dlo_done")
        g_done = s.sem("g_done")
        u_done = s.sem("u_done")
        d_done = s.sem("d_done")
        silu_done = s.sem("silu_done")
        hm_done = s.sem("hm_done")
        mT_done = s.sem("mT_done")
        mhi_done = s.sem("mhi_done")
        mlo_done = s.sem("mlo_done")
        yev_done = [s.sem(f"yev_done{j}") for j in range(2)]
        y_out = s.sem("y_out")

        block = s.block()

        def read(engine, at, b, lo, hi):
            if isinstance(b, int):
                ap = table[0:1, at + b:at + b + 1]
            else:
                ap = table[0:1, bass.ds(at + b, 1)]
            return engine.value_load(ap, min_val=lo, max_val=hi)

        def begun(engine, b):
            return read(engine, B_ORD, b, 0, EXPERTS - 1) + 1

        def count(engine):
            return read(engine, B_COUNT, 0, 0, MAX_BLOCKS - MIN_BLOCKS) + MIN_BLOCKS

        def of(ap, e):
            return ap[0][bass.ds(e, 1), :, :].rearrange("a (k p) n -> (a p) k n", p=P)

        @block.sync
        def _(sync):
            def load(b, new):
                e = read(sync, B_EXP, b, 0, EXPERTS - 1)
                o = None if not new else begun(sync, b)
                for raw, src, loaded, split in ((g_raw, w_gate, g_in, glo_done), (u_raw, w_up, u_in, ulo_done),
                                                (d_raw, w_down, d_in, dlo_done)):
                    if new:
                        sync.wait_ge(split, PC * (o - 1))
                    sync.dma_start(raw[:, :, :], of(src, e)).then_inc(loaded, 16)

            load(0, False)
            nb = count(sync)
            with sync.Fori(1, MAX_BLOCKS) as b:
                with sync.If(b < nb):
                    with sync.If(read(sync, B_NEW, b, 0, 1) > 0):
                        load(b, True)

        @block.gpsimd
        def _(pool):
            pool.memset(ident[:, :], 0.0).then_inc(ident_step, 1)
            pool.wait_ge(ident_step, 1)
            pool.affine_select(out=ident[:, :], in_=ident[:, :], compare_op=ALU.not_equal, fill=1.0, base=0,
                               pattern=[[-1, P]], channel_multiplier=1).then_inc(consts, 1)
            pool.wait_ge(consts, 1)

            def gather(b):
                first = read(pool, B_FIRST, b, 0, TOP_K * SEQ)
                wait(pool, x_in, 16 * b)
                pool.dma_start(idx[:, :], slots_d[bass.ds(first, P), :]).then_inc(idx_in, 16)
                pool.wait_ge(idx_in, 16 * (b + 1))
                wait(pool, xT_done, b)
                wait(pool, gated, b)
                pool.tensor_tensor(gate_copy[:, :], ident[:, 0:1], ident[:, 0:1], ALU.mult).then_inc(gated, 1)
                pool.indirect_dma_start(xr[:, :], None, h_d, bass.IndirectOffsetOnAxis(idx[:, 0:1], 0)
                                        ).then_inc(x_in, 16)

            def store(b):
                for j in range(2):
                    pool.wait_ge(yev_done[j], b + 1)
                first = read(pool, B_FIRST, b, 0, TOP_K * SEQ)
                pool.dma_start(y_d[bass.ds(first, P), :], yo[:, :]).then_inc(y_out, 16)

            nb = count(pool)
            gather(0)
            gather(1)
            with pool.Fori(1, MAX_BLOCKS) as b:
                with pool.If(b < nb):
                    gather(b + 1)
                    store(b - 1)
            store(nb - 1)
            pool.wait_ge(x_in, 16 * (nb + 1))
            pool.wait_ge(y_out, 16 * nb)

        @block.scalar
        def _(act):
            def split(b, o, raw, hi, loaded, used, done):
                act.wait_ge(loaded, 16 * o)
                wait(act, used, b)
                n = raw.shape[1] // PC
                for i in range(PC):
                    act.activation(hi[:, i * n:(i + 1) * n, :], raw[:, i * n:(i + 1) * n, :], ACT.Copy
                                   ).then_inc(done, 1)

            def x_high(b):
                act.wait_ge(xT_done, b + 1)
                wait(act, u_done, b)
                act.activation(x_hi[:, :, :], x_ps[:, :, :], ACT.Copy).then_inc(xhi_done, 1)

            def silu(b):
                act.wait_ge(g_done, b + 1)
                wait(act, hm_done, b)
                act.activation(sg[:, :], g_ps[:, :], ACT.Silu).then_inc(silu_done, 1)

            def m_high(b):
                act.wait_ge(mT_done, b + 1)
                wait(act, d_done, b)
                act.activation(m_hi[:, :, :], m_ps[:, :, :], ACT.Copy).then_inc(mhi_done, 1)

            def y_half(b):
                act.wait_ge(d_done, b + 1)
                wait(act, y_out, 16 * b)
                act.activation(yo[:, 0:512], y_ps[:, 0, :], ACT.Copy).then_inc(yev_done[0], 1)

            g = (g_raw, g_hi, g_in, g_done, ghi_done)
            u = (u_raw, u_hi, u_in, u_done, uhi_done)
            d = (d_raw, d_hi, d_in, d_done, dhi_done)
            nb = count(act)
            x_high(0)
            split(0, 1, *g)
            split(0, 1, *u)
            split(0, 1, *d)
            silu(0)

            def new(b, *what):
                with act.If(read(act, B_NEW, b, 0, 1) > 0):
                    split(b, begun(act, b), *what)

            new(1, *g)
            x_high(1)
            new(1, *u)

            def body(b):
                silu(b)
                m_high(b - 1)
                new(b + 1, *g)
                x_high(b + 1)
                new(b + 1, *u)

            body(1)
            with act.Fori(2, MAX_BLOCKS) as b:
                with act.If(b < nb):
                    y_half(b - 2)
                    new(b - 1, *d)
                    body(b)
            y_half(nb - 2)
            new(nb - 1, *d)
            m_high(nb - 1)
            y_half(nb - 1)

        @block.vector
        def _(dve):
            def split(b, o, raw, hi, lo, hi_done, done):
                n = raw.shape[1] // PC
                for i in range(PC):
                    dve.wait_ge(hi_done, PC * (o - 1) + i + 1)
                    c = slice(i * n, (i + 1) * n)
                    dve.tensor_tensor(lo[:, c, :], raw[:, c, :], hi[:, c, :].bitcast(F32), ALU.subtract
                                      ).then_inc(done, 1)

            def x_low(b):
                dve.wait_ge(xhi_done, b + 1)
                dve.tensor_tensor(x_lo[:, :, :], x_ps[:, :, :], x_hi[:, :, :].bitcast(F32), ALU.subtract
                                  ).then_inc(xlo_done, 1)

            def middle(b):
                dve.wait_ge(silu_done, b + 1)
                dve.wait_ge(u_done, b + 1)
                wait(dve, mT_done, b)
                dve.tensor_tensor(hm[:, :], sg[:, :], u_ps[:, :], ALU.mult).then_inc(hm_done, 1)

            def m_low(b):
                dve.wait_ge(mhi_done, b + 1)
                dve.tensor_tensor(m_lo[:, :, :], m_ps[:, :, :], m_hi[:, :, :].bitcast(F32), ALU.subtract
                                  ).then_inc(mlo_done, 1)

            def y_half(b):
                dve.wait_ge(d_done, b + 1)
                wait(dve, y_out, 16 * b)
                dve.tensor_copy(yo[:, 512:], y_ps[:, 1, :]).then_inc(yev_done[1], 1)

            def new(b, *what):
                with dve.If(read(dve, B_NEW, b, 0, 1) > 0):
                    split(b, begun(dve, b), *what)

            g = (g_raw, g_hi, g_lo, ghi_done, glo_done)
            u = (u_raw, u_hi, u_lo, uhi_done, ulo_done)
            d = (d_raw, d_hi, d_lo, dhi_done, dlo_done)
            nb = count(dve)
            x_low(0)
            split(0, 1, *g)
            split(0, 1, *u)
            split(0, 1, *d)
            middle(0)
            new(1, *g)
            x_low(1)
            new(1, *u)

            def body(b):
                m_low(b - 1)
                new(b + 1, *g)
                middle(b)
                x_low(b + 1)
                new(b + 1, *u)

            body(1)
            with dve.Fori(2, MAX_BLOCKS) as b:
                with dve.If(b < nb):
                    y_half(b - 2)
                    new(b - 1, *d)
                    body(b)
            y_half(nb - 2)
            new(nb - 1, *d)
            m_low(nb - 1)
            y_half(nb - 1)

        @block.tensor
        def _(pe):
            def x_transposes(b):
                pe.wait_ge(x_in, 16 * (b + 1))
                wait(pe, xlo_done, b)
                for k in range(KM):
                    ins = pe.transpose(x_ps[:, k, :], xr[:, k * P:(k + 1) * P], ident[:, :])
                ins.then_inc(xT_done, 1)

            def product(out, s_hi, s_lo, w_hi, w_lo, n):
                for k in range(n):
                    pe.matmul(out, s_lo[:, k, :], w_hi(k), start=(k == 0), stop=False)
                    pe.matmul(out, s_hi[:, k, :], w_lo(k), start=False, stop=False)
                    ins = pe.matmul(out, s_hi[:, k, :], w_hi(k), start=False, stop=(k == n - 1))
                return ins

            def gate(b, o):
                pe.wait_ge(glo_done, PC * o)
                pe.wait_ge(xlo_done, b + 1)
                wait(pe, silu_done, b)
                product(g_ps[:, :], x_hi, x_lo, lambda k: g_hi[:, k, :], lambda k: g_lo[:, k, :], KM
                        ).then_inc(g_done, 1)

            def up(b, o):
                pe.wait_ge(ulo_done, PC * o)
                wait(pe, hm_done, b)
                product(u_ps[:, :], x_hi, x_lo, lambda k: u_hi[:, k, :], lambda k: u_lo[:, k, :], KM
                        ).then_inc(u_done, 1)

            def m_transposes(b):
                pe.wait_ge(hm_done, b + 1)
                wait(pe, mlo_done, b)
                for k in range(KD):
                    ins = pe.transpose(m_ps[:, k, :], hm[:, k * P:(k + 1) * P], ident[:, :])
                ins.then_inc(mT_done, 1)

            def down(b, o):
                pe.wait_ge(dlo_done, PC * o)
                pe.wait_ge(mlo_done, b + 1)
                for j in range(2):
                    wait(pe, yev_done[j], b)
                    c = slice(j * 512, (j + 1) * 512)
                    ins = product(y_ps[:, j, :], m_hi, m_lo, lambda k: d_hi[:, k, c], lambda k: d_lo[:, k, c], KD)
                ins.then_inc(d_done, 1)

            pe.wait_ge(consts, 1)
            nb = count(pe)
            x_transposes(0)
            gate(0, 1)
            up(0, 1)
            x_transposes(1)
            with pe.Fori(1, MAX_BLOCKS) as b:
                with pe.If(b < nb):
                    o = begun(pe, b)
                    gate(b, o)
                    m_transposes(b - 1)
                    up(b, o)
                    x_transposes(b + 1)
                    down(b - 1, begun(pe, b - 1))
            m_transposes(nb - 1)
            down(nb - 1, begun(pe, nb - 1))


def combine(nc, x2_d, y_d, gates, slots, out):
    NS = 4

    with Scope(nc, "f") as s:
        x2 = s.sb("x2", [P, NS, DM])
        y = s.sb("y", [P, NS, TOP_K, DM])
        x_in = [s.sem(f"x_in{j}") for j in range(NS)]
        y_in = [[s.sem(f"y_in{j}_{k}") for k in range(TOP_K)] for j in range(NS)]
        first = s.sem("first")
        added = s.sem("added")
        stored = [s.sem(f"stored{j}") for j in range(NS)]
        block = s.block()

        def rows(ap, t):
            return ap.rearrange("(t p) c -> t p c", p=P)[bass.ds(t, 1), :, :].rearrange("a p c -> (a p) c")

        @block.sync
        def _(sync):
            for j in range(NS):
                sync.dma_start(x2[:, j, :], rows(x2_d, j)).then_inc(x_in[j], 16)

            def store(i, j):
                sync.wait_ge(added, NS * i + j + 1)
                sync.dma_start(rows(out[0], NS * i + j), x2[:, j, :]).then_inc(stored[j], 16)

            with sync.Fori(1, TILES // NS) as i:
                for j in range(NS):
                    store(i - 1, j)
                for j in range(NS):
                    sync.wait_ge(stored[j], 16 * i)
                    sync.dma_start(x2[:, j, :], rows(x2_d, NS * i + j)).then_inc(x_in[j], 16)
            for j in range(NS):
                store(TILES // NS - 1, j)
            for j in range(NS):
                sync.wait_ge(stored[j], 16 * TILES // NS)

        @block.gpsimd
        def _(pool):
            for t in range(TILES):
                j = t % NS
                wait(pool, added, t - NS + 1)
                for k in range(TOP_K):
                    pool.indirect_dma_start(y[:, j, k, :], None, y_d[0:TOP_K * SEQ, :],
                                            bass.IndirectOffsetOnAxis(slots[:, k, t:t + 1], 0)
                                            ).then_inc(y_in[j][k], 16)

        @block.vector
        def _(dve):
            with dve.Fori(0, TILES // NS) as i:
                for j in range(NS):
                    t = NS * i + j
                    xv = x2[:, j, :]
                    dve.wait_ge(x_in[j], 16 * (i + 1))
                    dve.wait_ge(y_in[j][0], 16 * (i + 1))
                    dve.scalar_tensor_tensor(out=xv, in0=y[:, j, 0, :],
                                             scalar=gates[:, 0, bass.ds(t, 1)], in1=xv,
                                             op0=ALU.mult, op1=ALU.add).then_inc(first, 1)
                    dve.wait_ge(first, t + 1)
                    dve.wait_ge(y_in[j][1], 16 * (i + 1))
                    dve.scalar_tensor_tensor(out=xv, in0=y[:, j, 1, :],
                                             scalar=gates[:, 1, bass.ds(t, 1)], in1=xv,
                                             op0=ALU.mult, op1=ALU.add).then_inc(added, 1)


def build(nc, x, rel_bias_table, norm_mix, w_in, q_norm, k_norm, conv_w, conv_b, rg_w_a, rg_b_a, rg_w_x,
          rg_b_x, rg_lambda, norm_attn_out, norm_rnn_out, w_out, norm_ffn, router_group_w, router_group_b,
          router_expert_w, router_expert_b, expert_w_gate, expert_w_up, expert_w_down, one_hot, out):
    def scratch(name, shape, dt=F32):
        return nc.dram_tensor(name, shape, dt, kind="Internal").ap()

    qkv = scratch("qkv", [SEQ, D_QKV])
    rnn_t = scratch("rnn_t", [D_RNN, SEQ])
    toeplitz = scratch("toeplitz", [HEADS, len(BRANCHES) * TW])
    attn_o = scratch("attn_o", [len(BRANCHES) * SEQ, OW])
    x2_d = scratch("x2_d", [SEQ, DM])
    h_d = scratch("h_d", [SEQ, DM])
    slots_d = scratch("slots_d", [TOP_K * SEQ + P, 1], I32)
    y_d = scratch("y_d", [TOP_K * SEQ + P, DM])

    project_and_recur(nc, x, norm_mix, w_in, conv_w, conv_b, rg_w_a, rg_b_a, rg_w_x, rg_b_x, rg_lambda,
                      qkv, rnn_t)
    attend(nc, rel_bias_table, one_hot, q_norm, k_norm, qkv, toeplitz, attn_o)
    with Scope(nc, "routing") as s:
        lg = s.sb("lg", [P, TILES, GROUPS + EXPERTS])
        gates = s.sb("gates", [P, TOP_K, TILES])
        slots = s.sb("slots", [P, TOP_K, TILES], I32)
        table = s.sb("table", [P, 4 * (MAX_BLOCKS + 1) + 1], I32)
        mix(nc, x, attn_o, rnn_t, norm_attn_out, norm_rnn_out, w_out, norm_ffn, router_group_w,
            router_group_b, router_expert_w, router_expert_b, x2_d, h_d, lg)
        route(nc, lg, slots_d, gates, slots, table)
        experts(nc, table, slots_d, h_d, expert_w_gate, expert_w_up, expert_w_down, y_d)
        combine(nc, x2_d, y_d, gates, slots, out)


def kernel(x, rel_bias_table, norm_mix, w_in, q_norm, k_norm, conv_w, conv_b, rg_w_a, rg_b_a, rg_w_x,
           rg_b_x, rg_lambda, norm_attn_out, norm_rnn_out, w_out, norm_ffn, router_group_w, router_group_b,
           router_expert_w, router_expert_b, expert_w_gate, expert_w_up, expert_w_down):
    import concourse.bacc as bacc
    from concourse import bass_utils

    arrays = {"x": x, "rel_bias_table": rel_bias_table, "norm_mix": norm_mix, "w_in": w_in,
              "q_norm": q_norm, "k_norm": k_norm, "conv_w": conv_w, "conv_b": conv_b, "rg_w_a": rg_w_a,
              "rg_b_a": rg_b_a, "rg_w_x": rg_w_x, "rg_b_x": rg_b_x, "rg_lambda": rg_lambda,
              "norm_attn_out": norm_attn_out, "norm_rnn_out": norm_rnn_out, "w_out": w_out,
              "norm_ffn": norm_ffn, "router_group_w": router_group_w, "router_group_b": router_group_b,
              "router_expert_w": router_expert_w, "router_expert_b": router_expert_b,
              "expert_w_gate": expert_w_gate, "expert_w_up": expert_w_up,
              "expert_w_down": expert_w_down, "one_hot": bias_buckets()}
    arrays = {n: np.ascontiguousarray(a) for n, a in arrays.items()}
    nc = bacc.Bacc("TRN2", target_bir_lowering=False, num_devices=1)
    ins = [nc.dram_tensor(n, a.shape, mybir.dt.from_np(a.dtype), kind="ExternalInput").ap()
           for n, a in arrays.items()]
    out = nc.dram_tensor("out", x.shape, F32, kind="ExternalOutput").ap()
    build(nc, *ins, out)
    nc.finalize()
    res = bass_utils.run_bass_kernel_spmd(nc, [arrays], core_ids=[0])
    return np.asarray(res.results[0]["out"])
```

```python
from contextlib import ExitStack

import numpy as np

import concourse.bass as bass
from concourse import mybir

F32 = mybir.dt.float32
F32R = mybir.dt.float32r
I32 = mybir.dt.int32
ALU = mybir.AluOpType
ACT = mybir.ActivationFunctionType
X = mybir.AxisListType.X

P = 128
SEQ, DM = 2048, 1024
HEADS, HD = 8, 64
D_ATTN, D_RNN = 512, 512
RNN_W = 64
D_QKV = 3 * D_ATTN
D_IN = D_QKV + 2 * D_RNN
TILES = SEQ // P
KM = DM // P
BRANCHES = ((128, 1), (512, 4), (2048, 16))
QB = 128
BUCKETS, MAX_DIST = 32, 2048
CONV = 4
RG_C = 8.0
GROUPS, PER_GROUP = 4, 8
EXPERTS = GROUPS * PER_GROUP
TOP_K = 2
DE = 512
EPS = 1e-6
NEG = -1e30
BIG = 1e30

TW = 3 * QB - 1
OW = D_ATTN + 2 * HEADS
MAX_BLOCKS = SEQ * TOP_K // P + EXPERTS - 1
MIN_BLOCKS = SEQ * TOP_K // P


def bias_buckets():
    oh = np.zeros((BUCKETS + 1, len(BRANCHES), TW), np.float32)
    for b, (window, dil) in enumerate(BRANCHES):
        for c in range(TW):
            steps = QB - (c - (QB - 1))
            if steps < 0 or steps > window // dil:
                oh[BUCKETS, b, c] = 1.0
                continue
            dist = steps * dil
            exact = BUCKETS // 2
            if dist < exact:
                k = dist
            else:
                f = np.float32
                log = np.log(f(dist) / f(exact), dtype=np.float32) / f(np.log(MAX_DIST / exact))
                k = min(exact + int(log * f(BUCKETS - exact)), BUCKETS - 1)
            oh[k, b, c] = 1.0
    return oh.reshape(BUCKETS + 1, len(BRANCHES) * TW)


class Scope:

    def __init__(self, nc, name):
        self.nc, self.name, self.ctx, self.sems = nc, name, ExitStack(), []

    def __enter__(self):
        self.ctx.__enter__()
        return self

    def __exit__(self, *a):
        result = self.ctx.__exit__(*a)
        if self.sems:
            self.clear()
        return result

    def sb(self, name, shape, dt=F32):
        return self.ctx.enter_context(self.nc.sbuf_tensor(f"{self.name}_{name}", shape, dt))

    def ps(self, name, shape, dt=F32):
        return self.ctx.enter_context(self.nc.psum_tensor(f"{self.name}_{name}", shape, dt))

    def sem(self, name):
        sem = self.ctx.enter_context(self.nc.semaphore(f"{self.name}_{name}"))
        self.sems.append(sem.num)
        return sem

    def pool_sem(self, name):
        return self.nc.alloc_semaphore(f"{self.name}_{name}")

    def clear(self):
        runs = []
        for num in sorted(self.sems):
            if runs and num == runs[-1][1]:
                runs[-1][1] += 1
            else:
                runs.append([num, num + 1])
        with self.nc.Block() as block:
            @block.gpsimd
            def _(pool):
                for first, end in runs:
                    pool.sem_clear(range(first, end))

    def block(self):
        return self.ctx.enter_context(self.nc.Block())


def column(ap, n):
    return ap.rearrange("a (k p) -> p (a k)", p=P)


def wait(engine, sem, value):
    if not isinstance(value, int) or value > 0:
        engine.wait_ge(sem, value)


def project_and_recur(nc, x, norm_mix, w_in, conv_w, conv_b, rg_w_a, rg_b_a, rg_w_x, rg_b_x,
                      rg_lambda, rel_table, one_hot, qkv, rnn_t, toeplitz):
    CH = 512
    NCH = SEQ // CH
    TC = CH // P
    WC = 256
    NW = D_IN // WC
    NR = 2 * D_RNN // WC
    NX = D_RNN // WC
    NQK = 2 * D_ATTN // WC
    CT = D_RNN // P
    HW = WC // HD
    AHEAD = 3

    w_cols = [D_QKV + n * WC for n in range(NR)] + [n * WC for n in range(NW - NR)]

    with Scope(nc, "a") as s:
        ident = s.sb("ident", [P, P])
        gain_row = s.sb("gain_row", [P, DM])
        x_t = s.sb("x_t", [P, TC, DM])
        junk = s.sb("junk", [P, DM])
        ss = s.sb("ss", [P, TC])
        rstd = s.sb("rstd", [P, TC])
        half = s.sb("half", [P, TC * HW])
        eps_x = s.sb("eps_x", [P, 1])
        eps_z = s.sb("eps_z", [P, TC * HW])
        hn_hi = s.sb("hn_hi", [P, KM, CH], F32R)
        hn_lo = s.sb("hn_lo", [P, KM, CH], F32R)
        w_raw = s.sb("w_raw", [P, 2, KM, WC])
        w_hi = s.sb("w_hi", [P, 2, KM, WC], F32R)
        w_lo = s.sb("w_lo", [P, 2, KM, WC], F32R)
        z = s.sb("z", [P, 2, TC, WC])
        z_sq = s.sb("z_sq", [P, TC, WC])
        z_ss = s.sb("z_ss", [P, TC * HW])
        z_rs = s.sb("z_rs", [P, TC * HW])
        xr = s.sb("xr", [P, CT, CONV - 1 + CH])
        gate = s.sb("gate", [P, CT, CH])
        u = s.sb("u", [P, CT, CH])
        r = s.sb("r", [P, CT, CH])
        inp = s.sb("inp", [P, CT, CH])
        a = s.sb("a", [P, CT, CH])
        hs = s.sb("hs", [P, CT, CH])
        carry = s.sb("carry", [P, CT])
        cw = s.sb("cw", [P, CONV, CT])
        cb = s.sb("cb", [P, CT])
        gb = s.sb("gb", [P, 2, CT])
        lam = s.sb("lam", [P, CT])
        sp = s.sb("sp", [P, 6, CT])
        coef = s.sb("coef", [P, 2, CT])
        wg = s.sb("wg", [P, 2, CT, P])
        rel = s.sb("rel", [BUCKETS + 1, HEADS])
        oh = s.sb("oh", [BUCKETS + 1, len(BRANCHES) * TW])
        trow = s.sb("trow", [HEADS, len(BRANCHES) * TW])
        tr_ps = s.ps("tr_ps", [P, KM, P])
        mm_ps = s.ps("mm_ps", [P, 2, 2, 512])
        g_ps = s.ps("g_ps", [P, 2, 512])

        two = range(2)
        x_in = [s.sem(f"x_in{j}") for j in range(TC)]
        consts_in = s.sem("consts_in")
        wg_zeroed = s.sem("wg_zeroed")
        wg_in = s.pool_sem("wg_in")
        ident_step = s.sem("ident_step")
        consts = s.sem("consts")
        ss_done = [s.sem(f"ss_done{j}") for j in range(TC)]
        eps_added = s.sem("eps_added")
        rstd_done = [s.sem(f"rstd_done{j}") for j in range(TC)]
        xn_done = [s.sem(f"xn_done{j}") for j in range(TC)]
        tr_done = [s.sem(f"tr_done{j}") for j in range(TC)]
        hi_done = s.sem("hi_done")
        lo_done = s.sem("lo_done")
        w_loaded = [s.sem(f"w_loaded{j}") for j in two]
        whi_done = s.sem("whi_done")
        wlo_done = [s.sem(f"wlo_done{j}") for j in two]
        mm_done = [s.sem(f"mm_done{j}") for j in two]
        ev_done = [s.sem(f"ev_done{j}") for j in two]
        sq_done = s.sem("sq_done")
        zss_done = s.sem("zss_done")
        zeps_done = s.sem("zeps_done")
        zrs_done = s.sem("zrs_done")
        zn_done = s.sem("zn_done")
        z_out = [s.sem(f"z_out{j}") for j in two]
        coef_step = s.sem("coef_step")
        exp_lam = s.sem("exp_lam")
        coef_done = s.sem("coef_done")
        bias_table_in = s.sem("bias_table_in")
        mask_done = s.sem("mask_done")
        trow_mm = s.sem("trow_mm")
        trow_ev = s.sem("trow_ev")
        trow_out = s.sem("trow_out")
        halo_done = s.sem("halo_done")
        conv_step = s.sem("conv_step")
        gmm_done = [s.sem(f"gmm_done{j}") for j in two]
        gsig_done = [s.sem(f"gsig_done{j}") for j in two]
        a_done = s.sem("a_done")
        th_done = s.sem("th_done")
        iu_done = s.sem("iu_done")
        a2_done = s.sem("a2_done")
        d2_done = s.sem("d2_done")
        sqrt_done = s.sem("sqrt_done")
        drive_done = s.sem("drive_done")
        scan_done = s.sem("scan_done")
        carry_done = s.sem("carry_done")
        y_done = s.sem("y_done")
        y_out = s.sem("y_out")

        block = s.block()
        NCONV = CONV * CT

        def chunks(engine, body):
            body(0, False)
            with engine.Fori(1, NCH - 1) as c:
                body(c, False)
            body(NCH - 1, True)

        @block.sync
        def _(sync):
            x_v = x[0].rearrange("(c t p) d -> c t p d", t=TC, p=P)
            qkv_v = qkv.rearrange("(c t p) n -> c p t n", t=TC, p=P)
            rnn_v = rnn_t.rearrange("(k p) (c n) -> c p k n", p=P, n=CH)

            def one(ap):
                return ap.rearrange("a p d -> (a p) d") if len(ap.shape) == 3 else \
                    ap.rearrange("a p t n -> (a p) t n")

            def load_x(c, t):
                wait(sync, tr_done[t], c)
                sync.dma_start(x_t[:, t, :], one(x_v[bass.ds(c, 1), t, :, :])).then_inc(x_in[t], 16)

            def load_w(c, n):
                j, m = n % 2, (NW // 2) * c + n // 2
                wait(sync, wlo_done[j], m)
                col = w_cols[n % NW]
                sync.dma_start(w_raw[:, j, :, :],
                               w_in[0].rearrange("(k p) n -> p k n", p=P)[:, :, col:col + WC]
                               ).then_inc(w_loaded[j], 16)

            load_x(0, 0)
            load_x(0, 1)
            sync.dma_start(rel[0:BUCKETS, :], rel_table).then_inc(bias_table_in, 16)
            sync.dma_start(oh[:, :], one_hot).then_inc(bias_table_in, 16)
            sync.dma_start(gain_row[:, :], norm_mix.to_broadcast([P, DM])).then_inc(consts_in, 16)
            load_w(0, 0)
            for t in range(2, TC):
                load_x(0, t)
            for n in range(1, AHEAD):
                load_w(0, n)

            def body(c, last):
                for n in range(NW):
                    if not (last and n + AHEAD >= NW):
                        load_w(c, n + AHEAD)
                    if not last and n < TC:
                        load_x(c + 1, n)
                    if n > NR:
                        store_z(c, n - NR - 1)
                store_z(c, NW - NR - 1)
                sync.wait_ge(y_done, c + 1)
                sync.dma_start(one(rnn_v[bass.ds(c, 1), :, :, :]), u[:, :, :]).then_inc(y_out, 16)

            def store_z(c, i):
                if i < NQK:
                    sync.wait_ge(zn_done, NQK * c + i + 1)
                else:
                    n = NR + i
                    sync.wait_ge(ev_done[n % 2], (NW // 2) * c + n // 2 + 1)
                sync.dma_start(one(qkv_v[bass.ds(c, 1), :, :, i * WC:(i + 1) * WC]),
                               z[:, i % 2, :, :]).then_inc(z_out[i % 2], 16)

            sync.wait_ge(trow_ev, len(BRANCHES))
            sync.dma_start(toeplitz, trow[:, :]).then_inc(trow_out, 16)
            chunks(sync, body)
            sync.wait_ge(trow_out, 16)
            for j in two:
                sync.wait_ge(z_out[j], 16 * NCH * (NW - NR) // 2)
            sync.wait_ge(y_out, 16 * NCH)

        @block.gpsimd
        def _(pool):
            pool.memset(wg[:, :, :, :], 0.0).then_inc(wg_zeroed, 1)
            pool.memset(half[:, :], -0.5).then_inc(ident_step, 1)
            pool.memset(ident[:, :], 0.0).then_inc(ident_step, 1)
            pool.memset(eps_x[:, :], DM * EPS).then_inc(ident_step, 1)
            pool.memset(eps_z[:, :], HD * EPS).then_inc(ident_step, 1)
            pool.wait_ge(ident_step, 4)
            pool.affine_select(out=ident[:, :], in_=ident[:, :], compare_op=ALU.not_equal, fill=1.0, base=0,
                               pattern=[[-1, P]], channel_multiplier=1).then_inc(consts, 1)
            with nc.allow_non_contiguous_dma(reason="vectors of 512 values, by channel"):
                for ap, src in ((cb, conv_b), (lam, rg_lambda)):
                    pool.dma_start(ap[:, :], column(src, CT)).then_inc(wg_in, 16)
                for m, src in enumerate((rg_b_a, rg_b_x)):
                    pool.dma_start(gb[:, m, :], column(src.rearrange("a g w -> a (g w)"), CT)).then_inc(wg_in, 16)
                for k in range(CONV):
                    pool.dma_start(cw[:, k, :], column(conv_w[0, k:k + 1, :], CT)).then_inc(wg_in, 16)
            pool.wait_ge(wg_zeroed, 1)
            for m, w in enumerate((rg_w_a, rg_w_x)):
                for g in range(2):
                    q = slice(g * RNN_W, (g + 1) * RNN_W)
                    pool.dma_start(wg[q, m, :, q],
                                   w[0].rearrange("(k g) i j -> g i k j", g=2)[g]).then_inc(wg_in, 16)

            def rstd_of(c, t):
                j = t
                pool.wait_ge(ss_done[j], c + 1)
                pool.tensor_tensor(rstd[:, j:j + 1], ss[:, j:j + 1], eps_x[:, 0:1], ALU.add
                                   ).then_inc(eps_added, 1)
                pool.wait_ge(eps_added, TC * c + t + 1)
                pool.tensor_tensor(rstd[:, j:j + 1], rstd[:, j:j + 1], half[:, 0:1], ALU.pow
                                   ).then_inc(rstd_done[j], 1)

            for t in range(TC):
                rstd_of(0, t)

            def body(c, last):
                for n in range(NR, NW):
                    i = n - NR
                    if i == 4:
                        pool.wait_ge(sqrt_done, c + 1)
                        pool.wait_ge(iu_done, c + 1)
                        pool.tensor_tensor(inp[:, :, :], inp[:, :, :], r[:, :, :], ALU.mult).then_inc(drive_done, 1)
                    if i < NQK:
                        pool.wait_ge(ev_done[n % 2], (NW // 2) * c + n // 2 + 1)
                        wait(pool, zss_done, NQK * c + i)
                        pool.tensor_tensor(z_sq[:, :, :], z[:, i % 2, :, :], z[:, i % 2, :, :], ALU.mult
                                           ).then_inc(sq_done, 1)
                        pool.wait_ge(zss_done, NQK * c + i + 1)
                        wait(pool, zn_done, NQK * c + i)
                        pool.tensor_tensor(z_rs[:, :], z_ss[:, :], eps_z[:, :], ALU.add).then_inc(zeps_done, 1)
                        pool.wait_ge(zeps_done, NQK * c + i + 1)
                        pool.tensor_tensor(z_rs[:, :], z_rs[:, :], half[:, :], ALU.pow).then_inc(zrs_done, 1)
                    if i == 2:
                        for j in two:
                            pool.wait_ge(gsig_done[j], CT * c + CT)
                        pool.tensor_tensor(inp[:, :, :], inp[:, :, :], u[:, :, :], ALU.mult).then_inc(iu_done, 1)
                    if not last and i < TC:
                        rstd_of(c + 1, i)
                pool.wait_ge(scan_done, CT * c + CT)
                pool.tensor_tensor(u[:, :, :], hs[:, :, :], gate[:, :, :], ALU.mult).then_inc(y_done, 1)

            chunks(pool, body)

        @block.scalar
        def _(act):
            def square(c, t):
                act.wait_ge(x_in[t], 16 * (c + 1))
                wait(act, ss_done[(t - 1) % TC], c + 1 if t else c)
                act.activation(junk[:, :], x_t[:, t, :], ACT.Square, accum_out=ss[:, t:t + 1]
                               ).then_inc(ss_done[t], 1)

            def hn_split(c, t):
                act.wait_ge(tr_done[t], c + 1)
                act.activation(hn_hi[:, :, t * P:(t + 1) * P], tr_ps[:, :, :], ACT.Copy).then_inc(hi_done, 1)

            def w_split(c, n):
                j, m = n % 2, (NW // 2) * c + n // 2
                act.wait_ge(w_loaded[j], 16 * (m + 1))
                wait(act, mm_done[j], m)
                act.activation(w_hi[:, j, :, :], w_raw[:, j, :, :], ACT.Copy).then_inc(whi_done, 1)

            for t in range(TC):
                square(0, t)
                if t >= 1:
                    hn_split(0, t - 1)
            w_split(0, 0)
            hn_split(0, TC - 1)
            w_split(0, 1)
            act.wait_ge(coef_step, 2)
            act.activation(sp[:, 1, :], sp[:, 0, :], ACT.Exp, scale=-1.0).then_inc(exp_lam, 1)
            act.wait_ge(wg_in, 16 * 12)

            def body(c, last):
                for n in range(NW):
                    if n == 5:
                        for k in range(2 * CT):
                            m, ct, j = k // CT, k % CT, k % 2
                            act.wait_ge(gmm_done[j], CT * c + k // 2 + 1)
                            if k == 0:
                                wait(act, drive_done, c)
                            if k == CT:
                                wait(act, scan_done, CT * c)
                            act.activation((r, inp)[m][:, ct, :], g_ps[:, j, :], ACT.Sigmoid,
                                           bias=gb[:, m, ct:ct + 1]).then_inc(gsig_done[j], 1)
                    if n == 6:
                        act.wait_ge(gsig_done[0], CT * c + CT // 2)
                        act.wait_ge(gsig_done[1], CT * c + CT // 2)
                        for ct in range(CT):
                            act.activation(a[:, ct, :], r[:, ct, :], ACT.Exp, scale=coef[:, 0, ct:ct + 1]
                                           ).then_inc(a_done, 1)
                        for ct in range(CT):
                            act.wait_ge(a_done, CT * c + ct + 1)
                            act.activation(r[:, ct, :], r[:, ct, :], ACT.Tanh, scale=coef[:, 1, ct:ct + 1]
                                           ).then_inc(th_done, 1)
                        wait(act, y_done, c)
                        wait(act, carry_done, c)
                        act.activation(hs[:, :, :], a[:, :, :], ACT.Square).then_inc(a2_done, 1)
                    j, m = n % 2, (NW // 2) * c + n // 2
                    if not last and 1 <= n < 1 + TC:
                        square(c + 1, n - 1)
                    if n == NW - 1 and not last:
                        for t in range(TC - 1):
                            hn_split(c + 1, t)
                    act.wait_ge(mm_done[j], m + 1)
                    if n < NX:
                        wait(act, halo_done, c)
                        act.activation(xr[:, 2 * n:2 * n + 2, CONV - 1:], mm_ps[:, j, :, :], ACT.Copy
                                       ).then_inc(ev_done[j], 1)
                    elif n < NR:
                        wait(act, y_done, c)
                        k = 2 * (n - NX)
                        act.activation(gate[:, k:k + 2, :], mm_ps[:, j, :, :], ACT.Gelu_apprx_tanh
                                       ).then_inc(ev_done[j], 1)
                    else:
                        i = n - NR
                        wait(act, z_out[i % 2], 16 * ((NW - NR) // 2 * c + i // 2))
                        act.activation(z[:, i % 2, :, :], mm_ps[:, j, :, :].rearrange("p b (t n) -> p (b t) n", n=WC),
                                       ACT.Copy).then_inc(ev_done[j], 1)
                    if n + 2 < NW or (not last and n + 2 == NW):
                        w_split(c, n + 2)
                    if n == 8:
                        act.wait_ge(d2_done, c + 1)
                        act.activation(r[:, :, :], r[:, :, :], ACT.Sqrt).then_inc(sqrt_done, 1)
                if not last:
                    hn_split(c + 1, TC - 1)
                    w_split(c, NW + 1)

            chunks(act, body)

        @block.vector
        def _(dve):
            def normalise(c, t):
                j = t
                dve.wait_ge(rstd_done[j], c + 1)
                dve.scalar_tensor_tensor(out=x_t[:, j, :], in0=x_t[:, j, :], scalar=rstd[:, j:j + 1],
                                         in1=gain_row[:, :], op0=ALU.mult, op1=ALU.mult
                                         ).then_inc(xn_done[j], 1)

            def hn_split(c, t):
                dve.wait_ge(hi_done, TC * c + t + 1)
                dve.tensor_tensor(hn_lo[:, :, t * P:(t + 1) * P], tr_ps[:, :, :],
                                  hn_hi[:, :, t * P:(t + 1) * P].bitcast(F32), ALU.subtract).then_inc(lo_done, 1)

            def w_split(c, n):
                j = n % 2
                dve.wait_ge(whi_done, NW * c + n + 1)
                dve.tensor_tensor(w_lo[:, j, :, :], w_raw[:, j, :, :], w_hi[:, j, :, :].bitcast(F32),
                                  ALU.subtract).then_inc(wlo_done[j], 1)

            dve.memset(rel[BUCKETS:BUCKETS + 1, :], NEG).then_inc(mask_done, 1)
            dve.memset(carry[:, :], 0.0).then_inc(coef_done, 1)
            dve.memset(xr[:, :, 0:CONV - 1], 0.0).then_inc(coef_done, 1)
            dve.wait_ge(consts_in, 16)
            dve.tensor_scalar(gain_row[:, :], gain_row[:, :], DM ** 0.5, None, ALU.mult).then_inc(coef_done, 1)
            dve.wait_ge(coef_done, 3)
            for t in range(TC):
                normalise(0, t)
                if t >= 1:
                    hn_split(0, t - 1)
                if t < len(BRANCHES):
                    dve.wait_ge(trow_mm, t + 1)
                    dve.tensor_copy(trow[:, t * TW:(t + 1) * TW], g_ps[0:HEADS, t % 2, 0:TW]).then_inc(trow_ev, 1)
            w_split(0, 0)
            hn_split(0, TC - 1)
            w_split(0, 1)

            steps = [0]

            def link(ins):
                steps[0] += 1
                ins.then_inc(coef_step, 1)
                dve.wait_ge(coef_step, steps[0])

            absl, e, sv, s2, t_, neg = (sp[:, k, :] for k in range(6))
            dve.wait_ge(wg_in, 16 * 12)
            link(dve.tensor_scalar(neg, lam[:, :], -1.0, None, ALU.mult))
            link(dve.tensor_tensor(absl, lam[:, :], neg, ALU.max))
            dve.wait_ge(exp_lam, 1)
            link(dve.tensor_scalar(s2, e, 2.0, None, ALU.add))
            link(dve.reciprocal(t_, s2))
            link(dve.tensor_tensor(sv, e, t_, ALU.mult))
            link(dve.tensor_tensor(s2, sv, sv, ALU.mult))
            link(dve.tensor_scalar(t_, s2, 1.0 / 17, None, ALU.mult))
            for k in range(15, 1, -2):
                link(dve.scalar_tensor_tensor(out=t_, in0=t_, scalar=1.0 / k, in1=s2, op0=ALU.add, op1=ALU.mult))
            link(dve.scalar_tensor_tensor(out=t_, in0=t_, scalar=1.0, in1=sv, op0=ALU.add, op1=ALU.mult))
            link(dve.tensor_scalar(neg, neg, 0.0, None, ALU.max))
            link(dve.scalar_tensor_tensor(out=t_, in0=t_, scalar=2.0, in1=neg, op0=ALU.mult, op1=ALU.add))
            dve.tensor_scalar(coef[:, 0, :], t_, -RG_C, None, ALU.mult).then_inc(coef_done, 1)
            dve.tensor_scalar(coef[:, 1, :], t_, RG_C, None, ALU.mult).then_inc(coef_done, 1)

            def body(c, last):
                for n in range(NW):
                    if n == NW - 1 and not last:
                        for t in range(TC - 1):
                            hn_split(c + 1, t)
                    if not last and 5 <= n < 5 + TC:
                        normalise(c + 1, n - 5)
                    if n + 2 < NW or (not last and n + 2 == NW):
                        w_split(c, n + 2)
                    if n == NX:
                        for j in two:
                            dve.wait_ge(ev_done[j], (NW // 2) * c + 1)
                        wait(dve, y_out, 16 * c)
                        for k in range(CONV):
                            for ct in range(CT):
                                tap, src = cw[:, k, ct:ct + 1], xr[:, ct, k:k + CH]
                                if k == 0:
                                    ins = dve.tensor_scalar(u[:, ct, :], src, tap, cb[:, ct:ct + 1],
                                                            ALU.mult, ALU.add)
                                else:
                                    dve.wait_ge(conv_step, NCONV * c + CT * (k - 1) + ct + 1)
                                    ins = dve.scalar_tensor_tensor(out=u[:, ct, :], in0=src, scalar=tap,
                                                                   in1=u[:, ct, :], op0=ALU.mult, op1=ALU.add)
                                ins.then_inc(conv_step, 1)
                        dve.wait_ge(conv_step, NCONV * c + NCONV)
                        dve.tensor_copy(xr[:, :, 0:CONV - 1], xr[:, :, CH:CH + CONV - 1]).then_inc(halo_done, 1)
                    i = n - NR
                    if 0 <= i < NQK:
                        dve.wait_ge(sq_done, NQK * c + i + 1)
                        dve.tensor_reduce(z_ss[:, :], z_sq[:, :, :].rearrange("p t (h d) -> p (t h) d", d=HD), X,
                                          ALU.add).then_inc(zss_done, 1)
                        dve.wait_ge(zrs_done, NQK * c + i + 1)
                        zv = z[:, i % 2, :, :].rearrange("p t (h d) -> p (t h) d", d=HD)
                        dve.tensor_tensor(zv, zv, z_rs[:, :].unsqueeze(2).to_broadcast([P, TC * HW, HD]),
                                          ALU.mult).then_inc(zn_done, 1)
                    if n == 7:
                        dve.wait_ge(a2_done, c + 1)
                        dve.wait_ge(th_done, CT * c + CT)
                        dve.scalar_tensor_tensor(out=r[:, :, :].rearrange("p k n -> p (k n)"),
                                                 in0=hs[:, :, :].rearrange("p k n -> p (k n)"), scalar=1.0,
                                                 in1=r[:, :, :].rearrange("p k n -> p (k n)"), op0=ALU.add,
                                                 op1=ALU.mult).then_inc(d2_done, 1)
                if not last:
                    hn_split(c + 1, TC - 1)
                    w_split(c, NW + 1)
                dve.wait_ge(drive_done, c + 1)
                wait(dve, carry_done, c)
                for ct in range(CT):
                    dve.tensor_tensor_scan(hs[:, ct, :], a[:, ct, :], inp[:, ct, :],
                                           carry[:, ct:ct + 1], ALU.mult, ALU.add).then_inc(scan_done, 1)
                dve.wait_ge(scan_done, CT * c + CT)
                dve.tensor_copy(carry[:, :], hs[:, :, CH - 1]).then_inc(carry_done, 1)

            chunks(dve, body)

        @block.tensor
        def _(pe):
            def transposes(c, t):
                pe.wait_ge(xn_done[t], c + 1)
                wait(pe, lo_done, TC * c + t)
                for k in range(KM):
                    ins = pe.transpose(tr_ps[:, k, :], x_t[:, t, k * P:(k + 1) * P], ident[:, :])
                ins.then_inc(tr_done[t], 1)

            def products(out, pairs):
                n = len(pairs)
                for k, (s_hi, s_lo, m_hi, m_lo) in enumerate(pairs):
                    pe.matmul(out, s_lo, m_hi, start=(k == 0), stop=False)
                    pe.matmul(out, s_hi, m_lo, start=False, stop=False)
                    ins = pe.matmul(out, s_hi, m_hi, start=False, stop=(k == n - 1))
                return ins

            pe.wait_ge(consts, 1)
            pe.wait_ge(bias_table_in, 16 * 2)
            pe.wait_ge(mask_done, 1)
            for t in range(TC):
                if t < len(BRANCHES):
                    wait(pe, trow_ev, t - 1)
                    pe.matmul(g_ps[0:HEADS, t % 2, 0:TW], rel[:, :], oh[:, t * TW:(t + 1) * TW],
                              start=True, stop=True).then_inc(trow_mm, 1)
                transposes(0, t)
            pe.wait_ge(trow_ev, len(BRANCHES))

            def body(c, last):
                wait_lo = TC * c + TC
                pe.wait_ge(lo_done, wait_lo)
                for n in range(NW):
                    j, m = n % 2, (NW // 2) * c + n // 2
                    pe.wait_ge(wlo_done[j], m + 1)
                    wait(pe, ev_done[j], m)
                    if n < NR:
                        for b in two:
                            cols = slice(b * P, (b + 1) * P)
                            ins = products(mm_ps[:, j, b, :],
                                           [(w_hi[:, j, k, cols], w_lo[:, j, k, cols], hn_hi[:, k, :], hn_lo[:, k, :])
                                            for k in range(KM)])
                        ins.then_inc(mm_done[j], 1)
                        continue
                    for t in range(TC):
                        cols = slice(t * P, (t + 1) * P)
                        ins = products(mm_ps[:, j, t // 2, (t % 2) * WC:(t % 2 + 1) * WC],
                                       [(hn_hi[:, k, cols], hn_lo[:, k, cols], w_hi[:, j, k, :], w_lo[:, j, k, :])
                                        for k in range(KM)])
                        if t == TC - 1:
                            ins.then_inc(mm_done[j], 1)
                        if n == 5:
                            if t == 0:
                                pe.wait_ge(conv_step, NCONV * c + NCONV)
                                pe.wait_ge(wg_in, 16 * 12)
                            for g in two:
                                k = 2 * t + g
                                wait(pe, gsig_done[g], CT * c + k // 2)
                                pe.matmul(g_ps[:, g, :], wg[:, k // CT, k % CT, :], u[:, k % CT, :],
                                          start=True, stop=True).then_inc(gmm_done[g], 1)
                        if n == NW - 1 and not last:
                            transposes(c + 1, t)

            chunks(pe, body)


def attend(nc, toeplitz, q_norm, k_norm, qkv, attn_o, w_out, w_raw):
    NB = len(BRANCHES)
    TT = 4
    NG = TILES // TT
    HU = HEADS // 2
    UG = 2 * TT
    TRL, PVL = 2, 3

    with Scope(nc, "b") as s:
        ident = s.sb("ident", [P, P])
        exchange = s.sb("exchange", [P, P])
        bias = s.sb("bias", [P, NB, HEADS, 2 * QB])
        gk = s.sb("gk", [P, 1])
        gq = s.sb("gq", [P, 1])
        gqk = s.sb("gqk", [P, 1])
        qk_in = s.sb("qk_in", [P, TT, 2 * D_ATTN])
        v_in = s.sb("v_in", [P, TT, D_ATTN])
        q_t = s.sb("q_t", [P, 2, 4, P])
        k_t = s.sb("k_t", [P, TT, 4, P])
        sc = s.sb("sc", [P, 2, HU, 2 * QB])
        p = s.sb("p", [P, 4, HU, 2 * QB])
        pt = s.sb("pt", [P, 2, HU, 2, QB])
        ow = s.sb("ow", [P, TT, OW])
        gate = s.sb("gate", [P, 2])
        t_ps = s.ps("t_ps", [P, 4, P])
        s_ps = s.ps("s_ps", [P, 2, 2, 2, 2 * QB])
        pt_ps = s.ps("pt_ps", [P, 2, 2, 2, QB])
        o_ps = s.ps("o_ps", [P, HEADS, HD])

        ident_step = s.sem("ident_step")
        consts = s.sem("consts")
        setup_in = s.sem("setup_in")
        bias_in = [s.sem(f"bias_in{b}") for b in range(NB)]
        exchanged = s.sem("exchanged")
        flip_mm = s.sem("flip_mm")
        flip_ev = [s.sem(f"flip_ev{n}") for n in range(2)]
        gqk_done = s.sem("gqk_done")
        qk_loaded = [s.sem(f"qk_loaded{j}") for j in range(TT)]
        v_loaded = [s.sem(f"v_loaded{j}") for j in range(TT)]
        qT = s.sem("qT")
        qT_ev = s.sem("qT_ev")
        kT = s.sem("kT")
        kT_ev = s.sem("kT_ev")
        qk_done = s.sem("qk_done")
        gated = s.sem("gated")
        wo_in = s.sem("wo_in")
        sc_done = s.sem("sc_done")
        p_done = s.sem("p_done")
        pt_done = [s.sem(f"pt_done{j}") for j in range(2)]
        pt_ev = [s.sem(f"pt_ev{j}") for j in range(2)]
        pv_done = s.sem("pv_done")
        o_ev = s.sem("o_ev")
        stored = [s.pool_sem(f"stored{j}") for j in range(TT)]

        block = s.block()

        def groups(engine, body):
            body(0, 0, 0, True)
            with engine.Fori(1, NG) as G:
                body(0, G, G, False)
            with engine.Fori(NG, 2 * NG) as G:
                body(1, G, G - NG, False)
            body(2, 2 * NG, 0, True)
            with engine.Fori(2 * NG + 1, 3 * NG) as G:
                body(2, G, G - 2 * NG, False)

        def halves(b, peeled, j):
            if j < 0:
                return (1,) if b == 2 and not peeled else (0, 1)
            return (1,) if b == 2 or (b == 1 and j == 0) or (b == 0 and peeled and j == 0) else (0, 1)

        def following(engine, b, G, k, prepare):
            j = k // 2 + 1
            if j < TT:
                prepare(TT * G + j, j, G, k % 2)
            elif b == NB - 1 and not isinstance(G, int):
                with engine.If(G < NB * NG - 1):
                    prepare(TT * (G + 1), 0, G + 1, k % 2)
            else:
                prepare(TT * (G + 1), 0, G + 1, k % 2)

        def tile_rows(t, b, i, j):
            v = t.rearrange("(n q d) c -> n d q c", d=BRANCHES[b][1], q=QB)
            if b == 0:
                v = v[bass.ds(TT * i + j, 1), 0, :, :]
            elif b == 1:
                v = v[j, bass.ds(i, 1), :, :]
            else:
                v = v[0, bass.ds(TT * i + j, 1), :, :]
            return v.rearrange("a q c -> (a q) c")

        @block.sync
        def _(sync):
            def load_bias(b):
                src = bass.AP(toeplitz.tensor, b * TW, [[1, P], [NB * TW, HEADS], [1, 2 * QB]])
                sync.dma_start(bias[:, b, :, :], src).then_inc(bias_in[b], 16)

            load_bias(0)
            with nc.allow_non_contiguous_dma(reason="64 gains, one to a partition"):
                for h in range(2):
                    dims = slice(h * HD, (h + 1) * HD)
                    sync.dma_start(gq[dims, :], q_norm.rearrange("a d -> d a")).then_inc(setup_in, 16)
                    sync.dma_start(gk[dims, :], k_norm.rearrange("a d -> d a")).then_inc(setup_in, 16)
            sync.dma_start(qk_in[:, 0, :], tile_rows(qkv, 0, 0, 0)[:, 0:2 * D_ATTN]).then_inc(qk_loaded[0], 16)
            for b in range(1, NB):
                load_bias(b)

            def body(b, G, i, peeled):
                for j in range(TT):
                    wait(sync, kT, TT * (G - 1) + j + 1)
                    if not (isinstance(G, int) and G == 0 and j == 0):
                        sync.dma_start(qk_in[:, j, :], tile_rows(qkv, b, i, j)[:, 0:2 * D_ATTN]
                                       ).then_inc(qk_loaded[j], 16)
                    wait(sync, pv_done, UG * (G - 1) + 2 * (j + 1) + 2)
                    sync.dma_start(v_in[:, j, :], tile_rows(qkv, b, i, j)[:, 2 * D_ATTN:]
                                   ).then_inc(v_loaded[j], 16)
                if b < 2:
                    sync.dma_start(w_raw[:, bass.ds(G, 1), :].rearrange("p a n -> p (a n)"),
                                   w_out[0].rearrange("(k p) n -> k p n", p=P)[bass.ds(G, 1), :, :]
                                   .rearrange("a p n -> (a p) n")).then_inc(wo_in, 16)

            groups(sync, body)
            sync.wait_ge(wo_in, 16 * KM)

        @block.gpsimd
        def _(pool):
            pool.memset(ident[:, :], 0.0).then_inc(ident_step, 1)
            pool.wait_ge(ident_step, 1)
            pool.affine_select(out=exchange[:, :], in_=ident[:, :], compare_op=ALU.not_equal, fill=1.0,
                               base=1 - P, pattern=[[1, P]], channel_multiplier=1).then_inc(exchanged, 1)
            pool.wait_ge(exchanged, 1)
            pool.affine_select(out=ident[:, :], in_=ident[:, :], compare_op=ALU.not_equal, fill=1.0, base=0,
                               pattern=[[-1, P]], channel_multiplier=1).then_inc(consts, 1)

            def body(b, G, i, peeled):
                for j in range(TT):
                    pool.wait_ge(o_ev, TT * G + j + 1)
                    pool.dma_start(tile_rows(attn_o[b * SEQ:(b + 1) * SEQ, :], b, i, j), ow[:, j, :]
                                   ).then_inc(stored[j], 16)

            groups(pool, body)
            for j in range(TT):
                pool.wait_ge(stored[j], 16 * NB * NG)

        @block.scalar
        def _(act):
            act.wait_ge(gqk_done, 1)

            def next_evacuation(T, j, G, hq):
                if hq == 0:
                    act.wait_ge(qT, T + 1)
                    wait(act, qk_done, 2 * (T - 1))
                    act.activation(q_t[:, j % 2, :, :], t_ps[:, :, :], ACT.Copy, scale=gqk[:, 0:1]
                                   ).then_inc(qT_ev, 1)
                else:
                    act.wait_ge(kT, T + 1)
                    act.activation(k_t[:, j, :, :], t_ps[:, :, :], ACT.Copy).then_inc(kT_ev, 1)

            for hq in range(2):
                next_evacuation(0, 0, 0, hq)
            for n in range(1, NB * HEADS, 2):
                act.wait_ge(flip_mm, n + 1)
                act.activation(bias[:, n // HEADS, n % HEADS, :], s_ps[:, n // 2 % 2, 1, 0, :], ACT.Copy
                               ).then_inc(flip_ev[1], 1)

            def pt_copy(V, k, w):
                act.wait_ge(pt_done[0], V + 1)
                wait(act, pv_done, V - 1)
                act.activation(pt[:, k % 2, 0:2, w[0]:2, :], pt_ps[:, 0, :, w[0]:2, :], ACT.Copy
                               ).then_inc(pt_ev[0], 1)

            def body(b, G, i, peeled):
                for k in range(UG):
                    U, j, hq = UG * G + k, k // 2, k % 2
                    if not (isinstance(G, int) and G == 0 and k < TRL):
                        pt_copy(U - TRL, k, halves(b, peeled, (k - TRL) // 2))
                    following(act, b, G, k, next_evacuation)
                    w = halves(b, peeled, j)[0] * QB
                    for x in range(HU):
                        h = HU * hq + x
                        act.wait_ge(sc_done, HU * U + x + 1)
                        if x == 0:
                            for q in range(2):
                                wait(act, pt_done[q], U - 3)
                        act.activation(p[:, k % 4, x, w:], sc[:, k % 2, x, w:], ACT.Exp, scale=-1.0,
                                       bias=ow[:, j, D_ATTN + h:D_ATTN + h + 1],
                                       accum_out=ow[:, j, D_ATTN + HEADS + h:D_ATTN + HEADS + h + 1]
                                       ).then_inc(p_done, 1)

            groups(act, body)
            for k in range(TRL):
                pt_copy(UG * 3 * NG + k - TRL, k, (1,))

        @block.vector
        def _(dve):
            dve.wait_ge(setup_in, 16 * 4)
            dve.tensor_tensor(gqk[:, :], gq[:, :], gk[:, :], ALU.mult).then_inc(gated, 1)
            dve.wait_ge(gated, 1)
            dve.tensor_scalar(gqk[:, :], gqk[:, :], HD * HD ** -0.5, None, ALU.mult).then_inc(gqk_done, 1)
            for n in range(0, NB * HEADS, 2):
                dve.wait_ge(flip_mm, n + 1)
                dve.tensor_copy(bias[:, n // HEADS, n % HEADS, :], s_ps[:, n // 2 % 2, 0, 0, :]
                                ).then_inc(flip_ev[0], 1)
            for ev in flip_ev:
                dve.wait_ge(ev, NB * HEADS // 2)

            def pt_copy(V, k, w):
                dve.wait_ge(pt_done[1], V + 1)
                wait(dve, pv_done, V - 1)
                dve.tensor_copy(pt[:, k % 2, 2:4, w[0]:2, :], pt_ps[:, 1, :, w[0]:2, :]).then_inc(pt_ev[1], 1)

            def o_copy(V, j):
                dve.wait_ge(pv_done, V + 1)
                dve.tensor_copy(ow[:, j % TT, 0:D_ATTN], o_ps[:, :, :].rearrange("p h d -> p (h d)")
                                ).then_inc(o_ev, 1)

            def body(b, G, i, peeled):
                for k in range(UG):
                    U, j, hq = UG * G + k, k // 2, k % 2
                    if not (isinstance(G, int) and G == 0 and k < TRL):
                        pt_copy(U - TRL, k, halves(b, peeled, (k - TRL) // 2))
                    if hq == 0 and not (isinstance(G, int) and G == 0 and k < PVL):
                        o_copy(U - PVL, (k - PVL) // 2)
                    w = halves(b, peeled, j)[0] * QB
                    for x in range(HU):
                        h, pp, o = HU * hq + x, x // 2, x % 2
                        if x == 0:
                            dve.wait_ge(qk_done, U + 1)
                            wait(dve, p_done, HU * (U - 1))
                            if hq == 0:
                                wait(dve, stored[j], 16 * G)
                            dve.wait_ge(gated, U + 1)
                            dve.tensor_copy(gate[:, 0:1], gqk[:, :]).then_inc(gated, 1)
                        dve.tensor_tensor_reduce(
                            sc[:, k % 2, x, w:], s_ps[:, k % 2, o, pp, w:], bias[:, b, h, w:], -1.0, BIG,
                            ALU.add, ALU.min, ow[:, j, D_ATTN + h:D_ATTN + h + 1]).then_inc(sc_done, 1)

            groups(dve, body)
            last = UG * 3 * NG
            pt_copy(last - 2, 0, (1,))
            o_copy(last - 3, TT - 2)
            pt_copy(last - 1, 1, (1,))
            o_copy(last - 1, TT - 1)

        @block.tensor
        def _(pe):
            pe.wait_ge(consts, 1)

            def next_transposes(T, j, G, hq):
                c0, done = (0, qT) if hq == 0 else (D_ATTN, kT)
                if hq == 0:
                    pe.wait_ge(qk_loaded[j], 16 * (G + 1))
                    wait(pe, kT_ev, T)
                else:
                    pe.wait_ge(qT_ev, T + 1)
                for k in range(4):
                    ins = pe.transpose(t_ps[:, k, :], qk_in[:, j, c0 + k * P:c0 + (k + 1) * P], ident[:, :])
                ins.then_inc(done, 1)

            for hq in range(2):
                next_transposes(0, 0, 0, hq)
            for n in range(NB * HEADS):
                if n % HEADS == 0:
                    pe.wait_ge(bias_in[n // HEADS], 16)
                wait(pe, flip_ev[n % 2], n // 2 - 1)
                pe.matmul(s_ps[:, n // 2 % 2, n % 2, 0, :], exchange[:, :], bias[:, n // HEADS, n % HEADS, :],
                          start=True, stop=True).then_inc(flip_mm, 1)
            for ev in flip_ev:
                pe.wait_ge(ev, NB * HEADS // 2)

            def p_transposes(V, k, w):
                for pp in range(2):
                    pe.wait_ge(p_done, HU * V + 2 * pp + 2)
                    wait(pe, pt_ev[pp], V)
                    for o in range(2):
                        for n in w:
                            ins = pe.transpose(pt_ps[:, pp, o, n, :],
                                               p[:, (k - TRL) % 4, 2 * pp + o, n * QB:(n + 1) * QB],
                                               ident[:, :])
                    ins.then_inc(pt_done[pp], 1)

            def pv(V, G, k, w):
                j, hq = k // 2, k % 2
                for pp in range(2):
                    pe.wait_ge(pt_ev[pp], V + 1)
                if hq == 0:
                    pe.wait_ge(v_loaded[j], 16 * (G + 1))
                    wait(pe, o_ev, TT * G + j)
                for x in range(HU):
                    h = HU * hq + x
                    for n in w:
                        ins = pe.matmul(o_ps[:, h, :], pt[:, k % 2, x, n, :],
                                        v_in[:, (j - 1 + n) % TT, h * HD:(h + 1) * HD],
                                        start=(n == w[0]), stop=(n == 1))
                ins.then_inc(pv_done, 1)

            def body(b, G, i, peeled):
                for k in range(UG):
                    U, j, hq = UG * G + k, k // 2, k % 2
                    T, w = TT * G + j, halves(b, peeled, j)
                    start = isinstance(G, int) and G == 0
                    if not (start and k < TRL):
                        p_transposes(U - TRL, k, halves(b, peeled, (k - TRL) // 2))
                    following(pe, b, G, k, next_transposes)
                    if not (start and k < PVL):
                        kk = (k - PVL) % UG
                        pv(U - PVL, G if k >= PVL else G - 1, kk, halves(b, peeled, (k - PVL) // 2))
                    if hq == 0:
                        pe.wait_ge(qT_ev, T + 1)
                        pe.wait_ge(kT_ev, T + 1)
                    wait(pe, sc_done, HU * (U - 1))
                    for pp in range(2):
                        for n in w:
                            for o in range(2):
                                dims = slice(o * HD, (o + 1) * HD)
                                ins = pe.matmul(s_ps[:, k % 2, o, pp, n * QB:(n + 1) * QB],
                                                q_t[dims, j % 2, 2 * hq + pp, :],
                                                k_t[dims, (j - 1 + n) % TT, 2 * hq + pp, :], start=True, stop=True)
                    ins.then_inc(qk_done, 1)

            groups(pe, body)
            last = UG * 3 * NG
            p_transposes(last - 2, 0, (1,))
            pv(last - 3, 3 * NG - 1, UG - 3, (1,))
            p_transposes(last - 1, 1, (1,))
            pv(last - 2, 3 * NG - 1, UG - 2, (1,))
            pv(last - 1, 3 * NG - 1, UG - 1, (1,))


def mix(nc, x, attn_o, rnn_t, norm_attn, norm_rnn, w_raw, norm_ffn, wr_g, br_g, wr_e, br_e,
                  x2_d, h_d, lg):
    NB = len(BRANCHES)
    CT = D_RNN // P
    NR = GROUPS + EXPERTS

    with Scope(nc, "c") as s:
        ident = s.sb("ident", [P, P])
        ones = s.sb("ones", [P, P])
        ob = s.sb("ob", [P, 2, NB, OW])
        x_t = s.sb("x_t", [P, 2, DM])
        rt = s.sb("rt", [P, 2, CT, P])
        rsq = s.sb("rsq", [P, CT, P])
        rg = s.sb("rg", [P, CT, P])
        w_hi = s.sb("w_hi", [P, KM, DM], F32R)
        w_lo = s.sb("w_lo", [P, KM, DM], F32R)
        wb = s.sb("wb", [P, NB, D_ATTN])
        at = s.sb("at", [P, D_ATTN])
        junk = s.sb("junk", [P, DM])
        sm = s.sb("sm", [P, 4, NB, HEADS])
        sh = s.sb("sh", [P, 3, HEADS])
        st = s.sb("st", [P, 7])
        half = s.sb("half", [P, 1])
        eps_a = s.sb("eps_a", [P, 1])
        eps_x = s.sb("eps_x", [P, 1])
        ga = s.sb("ga", [P, D_ATTN])
        gf = s.sb("gf", [P, DM])
        gr = s.sb("gr", [P, CT])
        a_hi = s.sb("a_hi", [P, 2, 4, P], F32R)
        a_lo = s.sb("a_lo", [P, 2, 4, P], F32R)
        r_hi = s.sb("r_hi", [P, 2, CT, P], F32R)
        r_lo = s.sb("r_lo", [P, 2, CT, P], F32R)
        h_t = s.sb("h_t", [P, 2, DM])
        ht = s.sb("ht", [P, KM, P])
        wr = s.sb("wr", [P, KM, NR])
        br = s.sb("br", [P, NR])
        a_ps = s.ps("a_ps", [P, 4, P])
        l_ps = s.ps("l_ps", [P, 512])
        y_ps = s.ps("y_ps", [P, 2, 2, 512])
        h_ps = s.ps("h_ps", [P, KM, P])

        two = range(2)
        small_in = s.sem("small_in")
        router_in = s.sem("router_in")
        pool_step = s.sem("pool_step")
        consts = s.sem("consts")
        ob_in = [s.sem(f"ob_in{j}") for j in two]
        x_in = [s.sem(f"x_in{j}") for j in two]
        rt_in = [s.sem(f"rt_in{j}") for j in two]
        gains_done = s.sem("gains_done")
        jm_done = s.sem("jm_done")
        dm_done = s.sem("dm_done")
        wo_hi = s.sem("wo_hi")
        wo_lo = s.sem("wo_lo")
        em_done = s.sem("em_done")
        merge_step = s.sem("merge_step")
        wb_done = s.sem("wb_done")
        add1_done = s.sem("add1_done")
        at_done = s.sem("at_done")
        ssa_done = s.sem("ssa_done")
        ra_step = s.sem("ra_step")
        ra_done = s.sem("ra_done")
        an_done = s.sem("an_done")
        aT_done = s.sem("aT_done")
        ahi_done = s.sem("ahi_done")
        alo_done = s.sem("alo_done")
        rsq_done = s.sem("rsq_done")
        ssr_mm = s.sem("ssr_mm")
        ssr_ev = s.sem("ssr_ev")
        rr_done = s.sem("rr_done")
        rg_done = s.sem("rg_done")
        rhi_done = s.sem("rhi_done")
        rlo_done = s.sem("rlo_done")
        y_done = [s.sem(f"y_done{n}") for n in two]
        x1_done = [s.sem(f"x1_done{n}") for n in two]
        x2_done = [s.sem(f"x2_done{n}") for n in two]
        ssx_done = s.sem("ssx_done")
        rx_step = s.sem("rx_step")
        rx_done = s.sem("rx_done")
        hn_done = s.sem("hn_done")
        x2_out = [s.sem(f"x2_out{j}") for j in two]
        h_out = [s.sem(f"h_out{j}") for j in two]
        hT_done = s.sem("hT_done")
        hT_ev = s.sem("hT_ev")
        lg_mm = s.sem("lg_mm")
        lg_ev = s.sem("lg_ev")

        block = s.block()

        def rows(ap, t):
            return ap.rearrange("(t p) c -> t p c", p=P)[bass.ds(t, 1), :, :].rearrange("a p c -> (a p) c")

        def steps(engine, step):
            for t in range(-1, 4):
                step(t, t % 2, t // 2)
            with engine.Fori(2, TILES // 2 - 1) as m:
                for j in two:
                    step(2 * m + j, j, m)
            for t in range(TILES - 2, TILES + 3):
                step(t, t % 2, t // 2)

        def has(t, d):
            return not isinstance(t, int) or 0 <= t + d < TILES

        def ahead(j, m):
            return (1, m) if j == 0 else (0, m + 1)

        def behind(j, m):
            return (1, m - 1) if j == 0 else (0, m)

        @block.sync
        def _(sync):
            def load(m, j):
                t = 2 * m + j
                for used in (wb_done, rg_done, rsq_done):
                    wait(sync, used, t - 1)
                sync.dma_start(ob[:, j, :, :],
                               attn_o.rearrange("(b t p) c -> t p b c", b=NB, p=P)[bass.ds(t, 1), :, :, :]
                               .rearrange("a p b c -> (a p) b c")).then_inc(ob_in[j], 16)
                sync.dma_start(rt[:, j, :, :],
                               rnn_t.rearrange("(k p) (t n) -> t p k n", p=P, n=P)[bass.ds(t, 1), :, :, :]
                               .rearrange("a p k n -> (a p) k n")).then_inc(rt_in[j], 16)

            def load_x(m, j):
                wait(sync, x2_out[j], 16 * m)
                sync.dma_start(x_t[:, j, :], rows(x[0], 2 * m + j)).then_inc(x_in[j], 16)

            def store(m, j):
                for n in two:
                    sync.wait_ge(x2_done[n], 2 * m + j + 1)
                sync.dma_start(rows(x2_d, 2 * m + j), x_t[:, j, :]).then_inc(x2_out[j], 16)
                sync.wait_ge(hn_done, 2 * m + j + 1)
                sync.dma_start(rows(h_d, 2 * m + j), h_t[:, j, :]).then_inc(h_out[j], 16)

            load(0, 0)
            sync.dma_start(ga[:, :], norm_attn.to_broadcast([P, D_ATTN])).then_inc(small_in, 16)
            with nc.allow_non_contiguous_dma(reason="512 gains, by channel"):
                sync.dma_start(gr[:, :], column(norm_rnn, CT)).then_inc(small_in, 16)
            sync.dma_start(gf[:, :], norm_ffn.to_broadcast([P, DM])).then_inc(small_in, 16)
            load(0, 1)
            for j in two:
                load_x(0, j)
            sync.dma_start(br[:, 0:GROUPS], br_g.to_broadcast([P, GROUPS])).then_inc(router_in, 16)
            sync.dma_start(br[:, GROUPS:], br_e.to_broadcast([P, EXPERTS])).then_inc(router_in, 16)
            sync.dma_start(wr[:, :, 0:GROUPS], wr_g[0].rearrange("(k p) n -> p k n", p=P)).then_inc(router_in, 16)
            sync.dma_start(wr[:, :, GROUPS:], wr_e[0].rearrange("(k p) n -> p k n", p=P)).then_inc(router_in, 16)
            for j in two:
                load(1, j)
            with sync.Fori(1, TILES // 2 - 1) as m:
                for j in two:
                    load(m + 1, j)
                    store(m - 1, j)
                    load_x(m, j)
            for j in two:
                store(TILES // 2 - 2, j)
                load_x(TILES // 2 - 1, j)
            for j in two:
                store(TILES // 2 - 1, j)
            for j in two:
                sync.wait_ge(x2_out[j], 16 * TILES // 2)
                sync.wait_ge(h_out[j], 16 * TILES // 2)

        @block.gpsimd
        def _(pool):
            pool.memset(half[:, :], -0.5).then_inc(pool_step, 1)
            pool.memset(eps_a[:, :], D_ATTN * EPS).then_inc(pool_step, 1)
            pool.memset(eps_x[:, :], DM * EPS).then_inc(pool_step, 1)
            pool.memset(ident[:, :], 0.0).then_inc(pool_step, 1)
            pool.memset(ones[:, :], 1.0).then_inc(pool_step, 1)
            pool.wait_ge(pool_step, 5)
            pool.affine_select(out=ident[:, :], in_=ident[:, :], compare_op=ALU.not_equal, fill=1.0, base=0,
                               pattern=[[-1, P]], channel_multiplier=1).then_inc(consts, 1)

            def inverse_root(t, done, src, step, eps, out, rdone):
                pool.wait_ge(done, t + 1)
                if step is not None:
                    pool.tensor_tensor(st[:, out:out + 1], src, eps[:, :], ALU.add).then_inc(step, 1)
                    pool.wait_ge(step, t + 1)
                    src = st[:, out:out + 1]
                pool.tensor_tensor(st[:, out:out + 1], src, half[:, :], ALU.pow).then_inc(rdone, 1)

            def step(t, j, m):
                ja, ma = ahead(j, m)
                if has(t, 0):
                    inverse_root(t, ssr_ev, st[:, 1:2], None, None, (4, 6)[j], rr_done)
                if has(t, 1):
                    pool.wait_ge(rt_in[ja], 16 * (ma + 1))
                    wait(pool, ssr_mm, t + 1)
                    pool.tensor_tensor(rsq[:, :, :], rt[:, ja, :, :], rt[:, ja, :, :], ALU.mult
                                       ).then_inc(rsq_done, 1)
                    pool.wait_ge(wb_done, t + 2)
                    wait(pool, aT_done, t + 1)
                    pool.tensor_tensor(at[:, :], wb[:, 0, :], wb[:, 1, :], ALU.add).then_inc(add1_done, 1)
                    inverse_root(t + 1, ssa_done, st[:, 0:1], ra_step, eps_a, 3, ra_done)
                if has(t, -1):
                    inverse_root(t - 1, ssx_done, st[:, 2:3], rx_step, eps_x, 5, rx_done)

            steps(pool, step)

        @block.scalar
        def _(act):
            def step(t, j, m):
                ja, jb = ahead(j, m)[0], behind(j, m)[0]
                if has(t, 0):
                    act.wait_ge(aT_done, t + 1)
                    wait(act, y_done[1], t - 1)
                    act.activation(a_hi[:, j, :, :], a_ps[:, :, :], ACT.Copy).then_inc(ahi_done, 1)
                if has(t, -2):
                    act.wait_ge(hT_done, t - 1)
                    wait(act, lg_mm, t - 2)
                    act.activation(ht[:, :, :], h_ps[:, :, :], ACT.Copy).then_inc(hT_ev, 1)
                if has(t, 1):
                    act.wait_ge(dm_done, t + 2)
                    act.activation(sm[:, 1, :, :], sm[:, 0, :, :], ACT.Exp).then_inc(em_done, 1)
                    act.wait_ge(at_done, t + 2)
                    wait(act, ssx_done, t - 1)
                    act.activation(junk[:, 0:D_ATTN], at[:, :], ACT.Square, accum_out=st[:, 0:1]
                                   ).then_inc(ssa_done, 1)
                if has(t, -1):
                    for n in two:
                        act.wait_ge(x2_done[n], t)
                    act.wait_ge(ssa_done, t + 2 if has(t, 1) else TILES)
                    act.activation(junk[:, :], x_t[:, jb, :], ACT.Square, accum_out=st[:, 2:3]).then_inc(ssx_done, 1)
                if has(t, 1):
                    act.wait_ge(rg_done, t + 2)
                    wait(act, y_done[1], t)
                    act.activation(r_hi[:, ja, :, :], rg[:, :, :], ACT.Copy).then_inc(rhi_done, 1)
                if isinstance(t, int) and t == -1:
                    for k in range(KM):
                        act.activation(w_hi[:, k, :], w_raw[:, k, :], ACT.Copy).then_inc(wo_hi, 1)

            steps(act, step)

        @block.vector
        def _(dve):
            dve.wait_ge(small_in, 16 * 3)
            dve.tensor_scalar(ga[:, :], ga[:, :], D_ATTN ** 0.5, None, ALU.mult).then_inc(gains_done, 1)
            dve.tensor_scalar(gr[:, :], gr[:, :], D_RNN ** 0.5, None, ALU.mult).then_inc(gains_done, 1)
            dve.tensor_scalar(gf[:, :], gf[:, :], DM ** 0.5, None, ALU.mult).then_inc(gains_done, 1)
            dve.wait_ge(gains_done, 3)
            dve.wait_ge(router_in, 16 * 4)

            def residual(t, j, m, n):
                cols = slice(n * 512, (n + 1) * 512)
                xv = x_t[:, j, cols]
                dve.wait_ge(y_done[n], t + 1)
                if n == 0:
                    dve.wait_ge(rr_done, t + 1)
                    dve.wait_ge(x_in[j], 16 * (m + 1))
                dve.scalar_tensor_tensor(out=xv, in0=y_ps[:, 1, n, :], scalar=st[:, 4 + 2 * j:5 + 2 * j],
                                         in1=xv, op0=ALU.mult, op1=ALU.add).then_inc(x1_done[n], 1)
                dve.wait_ge(x1_done[n], t + 1)
                dve.tensor_tensor(xv, y_ps[:, 0, n, :], xv, ALU.add).then_inc(x2_done[n], 1)

            def merge(t, j, m):
                MS = 4
                neg_m = ob[:, j, :, D_ATTN:D_ATTN + HEADS]
                den = ob[:, j, :, D_ATTN + HEADS:]
                dve.wait_ge(ob_in[j], 16 * (m + 1))
                dve.tensor_reduce(sh[:, 0, :], neg_m.rearrange("p b h -> p h b"), X, ALU.min).then_inc(jm_done, 1)
                dve.wait_ge(jm_done, t + 1)
                dve.tensor_tensor(sm[:, 0, :, :], sh[:, 0, :].unsqueeze(1).to_broadcast([P, NB, HEADS]), neg_m,
                                  ALU.subtract).then_inc(dm_done, 1)
                dve.wait_ge(rt_in[j], 16 * (m + 1))
                wait(dve, rlo_done, t)
                dve.tensor_tensor(rg[:, :, :], rt[:, j, :, :], gr[:, :].unsqueeze(2).to_broadcast([P, CT, P]),
                                  ALU.mult).then_inc(rg_done, 1)
                dve.wait_ge(em_done, t + 1)
                dve.tensor_tensor(sm[:, 2, :, :], sm[:, 1, :, :], den, ALU.mult).then_inc(merge_step, 1)
                dve.wait_ge(merge_step, MS * t + 1)
                dve.tensor_reduce(sh[:, 1, :], sm[:, 2, :, :].rearrange("p b h -> p h b"), X, ALU.add
                                  ).then_inc(merge_step, 1)
                dve.wait_ge(merge_step, MS * t + 2)
                dve.reciprocal(sh[:, 2, :], sh[:, 1, :]).then_inc(merge_step, 1)
                dve.wait_ge(merge_step, MS * t + 3)
                dve.tensor_tensor(sm[:, 3, :, :], sm[:, 1, :, :],
                                  sh[:, 2, :].unsqueeze(1).to_broadcast([P, NB, HEADS]), ALU.mult
                                  ).then_inc(merge_step, 1)
                dve.wait_ge(merge_step, MS * t + 4)
                dve.tensor_tensor(wb[:, :, :].rearrange("p b (h d) -> p b h d", d=HD),
                                  ob[:, j, :, 0:D_ATTN].rearrange("p b (h d) -> p b h d", d=HD),
                                  sm[:, 3, :, :].unsqueeze(3).to_broadcast([P, NB, HEADS, HD]), ALU.mult
                                  ).then_inc(wb_done, 1)
                dve.wait_ge(add1_done, t + 1)
                dve.tensor_tensor(at[:, :], at[:, :], wb[:, 2, :], ALU.add).then_inc(at_done, 1)

            def step(t, j, m):
                (ja, ma), (jb, mb) = ahead(j, m), behind(j, m)
                if has(t, -3):
                    dve.wait_ge(lg_mm, t - 2)
                    dve.tensor_tensor(lg[:, bass.ds(t - 3, 1), :].rearrange("p a n -> p (a n)"),
                                      l_ps[:, 64:64 + NR], br[:, :], ALU.add).then_inc(lg_ev, 1)
                if has(t, -1):
                    residual(t - 1, jb, mb, 0)
                if has(t, 0):
                    dve.wait_ge(ssr_mm, t + 1)
                    wait(dve, rr_done, t)
                    dve.tensor_scalar(st[:, 1:2], l_ps[:, 0:1], D_RNN * EPS, None, ALU.add).then_inc(ssr_ev, 1)
                    dve.wait_ge(ahi_done, t + 1)
                    dve.tensor_tensor(a_lo[:, j, :, :], a_ps[:, :, :], a_hi[:, j, :, :].bitcast(F32), ALU.subtract
                                      ).then_inc(alo_done, 1)
                if has(t, 1):
                    merge(t + 1, ja, ma)
                    dve.wait_ge(ra_done, t + 2)
                    dve.scalar_tensor_tensor(out=at[:, :], in0=at[:, :], scalar=st[:, 3:4], in1=ga[:, :],
                                             op0=ALU.mult, op1=ALU.mult).then_inc(an_done, 1)
                if has(t, -1):
                    residual(t - 1, jb, mb, 1)
                if has(t, 1):
                    dve.wait_ge(rhi_done, t + 2)
                    dve.tensor_tensor(r_lo[:, ja, :, :], rg[:, :, :], r_hi[:, ja, :, :].bitcast(F32), ALU.subtract
                                      ).then_inc(rlo_done, 1)
                if has(t, -1):
                    dve.wait_ge(rx_done, t)
                    wait(dve, h_out[jb], 16 * mb)
                    wait(dve, hT_done, t - 2)
                    dve.scalar_tensor_tensor(out=h_t[:, jb, :], in0=x_t[:, jb, :], scalar=st[:, 5:6],
                                             in1=gf[:, :], op0=ALU.mult, op1=ALU.mult).then_inc(hn_done, 1)
                if isinstance(t, int) and t == -1:
                    for k in range(KM):
                        dve.wait_ge(wo_hi, k + 1)
                        dve.tensor_tensor(w_lo[:, k, :], w_raw[:, k, :], w_hi[:, k, :].bitcast(F32), ALU.subtract
                                          ).then_inc(wo_lo, 1)

            steps(dve, step)

        @block.tensor
        def _(pe):
            pe.wait_ge(consts, 1)

            def products(t, j, n):
                pe.wait_ge(rlo_done, t + 1)
                wait(pe, x2_done[n], t)
                cols = slice(n * 512, (n + 1) * 512)
                for part, s_hi, s_lo in ((1, r_hi, r_lo), (0, a_hi, a_lo)):
                    if part == 0:
                        pe.wait_ge(alo_done, t + 1)
                    out = y_ps[:, part, n, :]
                    for k in range(4):
                        kk = 4 * part + k
                        pe.matmul(out, s_lo[:, j, k, :], w_hi[:, kk, cols], start=(k == 0), stop=False)
                        pe.matmul(out, s_hi[:, j, k, :], w_lo[:, kk, cols], start=False, stop=False)
                        ins = pe.matmul(out, s_hi[:, j, k, :], w_hi[:, kk, cols], start=False, stop=(k == 3))
                ins.then_inc(y_done[n], 1)

            def step(t, j, m):
                jb = behind(j, m)[0]
                if isinstance(t, int) and t == 1:
                    pe.wait_ge(wo_lo, KM)
                if has(t, -1):
                    products(t - 1, jb, 0)
                if has(t, 0):
                    pe.wait_ge(an_done, t + 1)
                    wait(pe, alo_done, t)
                    for k in range(4):
                        ins = pe.transpose(a_ps[:, k, :], at[:, k * P:(k + 1) * P], ident[:, :])
                    ins.then_inc(aT_done, 1)
                    pe.wait_ge(rsq_done, t + 1)
                    wait(pe, lg_ev, t - 2)
                    for k in range(CT):
                        ins = pe.matmul(l_ps[:, 0:1], rsq[:, k, :], ones[:, 0:1], start=(k == 0), stop=(k == CT - 1))
                    ins.then_inc(ssr_mm, 1)
                if has(t, -2):
                    pe.wait_ge(hn_done, t - 1)
                    wait(pe, hT_ev, t - 2)
                    for k in range(KM):
                        ins = pe.transpose(h_ps[:, k, :], h_t[:, j, k * P:(k + 1) * P], ident[:, :])
                    ins.then_inc(hT_done, 1)
                if has(t, -1):
                    products(t - 1, jb, 1)
                if has(t, -2):
                    pe.wait_ge(hT_ev, t - 1)
                    pe.wait_ge(ssr_ev, t + 1 if has(t, 0) else TILES)
                    wait(pe, lg_ev, t - 2)
                    if isinstance(t, int) and t == 2:
                        pe.wait_ge(router_in, 16 * 4)
                    for k in range(KM):
                        ins = pe.matmul(l_ps[:, 64:64 + NR], ht[:, k, :], wr[:, k, :], start=(k == 0),
                                        stop=(k == KM - 1))
                    ins.then_inc(lg_mm, 1)

            steps(pe, step)


BLOCK_COLS = MAX_BLOCKS + 3
X2_SLOTS = 8
B_EXP, B_FIRST, B_NEW, B_ORD, B_COUNT = (i * BLOCK_COLS for i in range(5))


def table_entry(engine, table, at, b, lo, hi):
    if isinstance(b, int):
        ap = table[0:1, at + b:at + b + 1]
    else:
        ap = table[0:1, bass.ds(at + b, 1)]
    return engine.value_load(ap, min_val=lo, max_val=hi)


def of_expert(ap, e):
    return ap[0][bass.ds(e, 1), :, :].rearrange("a (k p) n -> (a p) k n", p=P)


def route(nc, lg, slots_d, gates, slots, table, raws):
    NB = BLOCK_COLS
    T, E, G, EG = TILES, EXPERTS, GROUPS, PER_GROUP

    with Scope(nc, "d") as s:
        ones = s.sb("ones", [P, P])
        upper = s.sb("upper", [P, P])
        iota = s.sb("iota", [P, E])
        iota_b = s.sb("iota_b", [P, NB])
        start = s.sb("start", [P, 2, E])
        tok = s.sb("tok", [P, T], I32)
        gd = s.sb("gd", [P, T, G])
        geq = s.sb("geq", [P, T, G])
        goh = s.sb("goh", [P, T, G])
        eg = s.sb("eg", [P, T, G])
        el = s.sb("el", [P, T, G, EG])
        e8 = s.sb("e8", [P, 2, T, EG])
        eq = s.sb("eq", [P, T, EG])
        o = s.sb("o", [P, 2, T, EG])
        v = s.sb("v", [P, 12, T])
        oh = s.sb("oh", [P, 2, T, E])
        both = s.sb("both", [P, T, E])
        sums = s.sb("sums", [P, T + 1, E])
        rank = s.sb("rank", [P, T, E])
        place = s.sb("place", [P, T, E])
        prod = s.sb("prod", [P, T, E])
        more = s.sb("more", [P, E, T])
        nb = s.sb("nb", [P, E])
        pend = s.sb("pend", [P, E])
        pos = s.sb("pos", [P, 2, T])
        zeros = s.sb("zeros", [P, 1], I32)
        le = s.sb("le", [P, 3, NB, E])
        bv = s.sb("bv", [P, 8, NB])
        bt = s.sb("bt", [P, 4 * NB + 1])
        r_ps = s.ps("r_ps", [P, T, E])
        c_ps = s.ps("c_ps", [P, T, E])

        const_step = s.sem("const_step")
        consts = s.sem("consts")
        step = s.sem("step")
        gd_done = s.sem("gd_done")
        eg_done = s.sem("eg_done")
        d_done = s.sem("d_done")
        ex_done = s.sem("ex_done")
        both_done = s.sem("both_done")
        rank_mm = s.sem("rank_mm")
        slots_done = s.sem("slots_done")
        scattered = s.pool_sem("scattered")
        tail_out = s.pool_sem("tail_out")
        table_done = s.sem("table_done")
        raw_in = s.sem("raw_in")

        block = s.block()

        @block.sync
        def _(sync):
            sync.wait_ge(table_done, 1)
            e = table_entry(sync, table, B_EXP, 0, 0, EXPERTS - 1)
            for raw, weight in raws:
                sync.dma_start(raw[:, :, :], of_expert(weight, e)).then_inc(raw_in, 16)
            sync.wait_ge(raw_in, 16 * len(raws))

        @block.gpsimd
        def _(pool):
            pool.memset(ones[:, :], 1.0).then_inc(const_step, 1)
            pool.wait_ge(const_step, 1)
            pool.affine_select(out=upper[:, :], in_=ones[:, :], compare_op=ALU.is_gt, fill=0.0, base=0,
                               pattern=[[1, P]], channel_multiplier=-1).then_inc(consts, 1)
            pool.iota(iota[:, :], [[1, E]], base=0, channel_multiplier=0,
                      allow_small_or_imprecise_dtypes=True).then_inc(consts, 1)
            pool.iota(iota_b[:, :], [[1, NB]], base=0, channel_multiplier=0,
                      allow_small_or_imprecise_dtypes=True).then_inc(consts, 1)
            pool.memset(zeros[:, :], 0).then_inc(consts, 1)
            pool.iota(tok[:, :], [[P, T]], base=0, channel_multiplier=1).then_inc(consts, 1)
            pool.wait_ge(consts, 5)
            pool.dma_start(slots_d[TOP_K * SEQ:, :], zeros[:, :]).then_inc(tail_out, 16)
            for k in range(TOP_K):
                pool.wait_ge(slots_done, k + 1)
                for t in range(T):
                    pool.indirect_dma_start(slots_d[0:TOP_K * SEQ, :],
                                            bass.IndirectOffsetOnAxis(slots[:, k, t:t + 1], 0),
                                            tok[:, t:t + 1], None).then_inc(scattered, 16)
            pool.wait_ge(scattered, 16 * TOP_K * T)
            pool.wait_ge(tail_out, 16)

        @block.scalar
        def _(act):
            act.wait_ge(gd_done, 1)
            act.activation(eg[:, :, :], gd[:, :, :], ACT.Exp).then_inc(eg_done, 1)
            act.wait_ge(d_done, 1)
            act.activation(v[:, 7, :], v[:, 6, :], ACT.Exp).then_inc(ex_done, 1)

        @block.tensor
        def _(pe):
            pe.wait_ge(consts, 5)
            pe.wait_ge(both_done, 1)
            flat = both[:, :, :].rearrange("p t e -> p (t e)")
            pe.matmul(r_ps[:, :, :].rearrange("p t e -> p (t e)"), upper[:, :], flat, start=True, stop=True)
            pe.matmul(c_ps[:, :, :].rearrange("p t e -> p (t e)"), ones[:, :], flat, start=True, stop=True
                      ).then_inc(rank_mm, 1)

        @block.vector
        def _(dve):
            n = [0]

            def done():
                n[0] += 1
                return n[0]

            def op(out, a, b, alu):
                dve.tensor_tensor(out, a, b, alu).then_inc(step, 1)
                dve.wait_ge(step, done())

            def reduce(out, a, alu):
                dve.tensor_reduce(out, a, X, alu).then_inc(step, 1)
                dve.wait_ge(step, done())

            def scaled(out, a, c, b, o0, o1):
                dve.scalar_tensor_tensor(out=out, in0=a, scalar=c, in1=b, op0=o0, op1=o1).then_inc(step, 1)
                dve.wait_ge(step, done())

            def over_t(ap, m):
                return ap.unsqueeze(2).to_broadcast([P, T, m])

            def over_e(ap, m):
                return ap.unsqueeze(1).to_broadcast([P, T, m])

            dve.wait_ge(consts, 5)
            gl = lg[:, :, 0:G]
            reduce(v[:, 0, :], gl, ALU.max)
            op(gd[:, :, :], gl, over_t(v[:, 0, :], G), ALU.subtract)
            op(geq[:, :, :], gl, over_t(v[:, 0, :], G), ALU.is_equal)
            scaled(geq[:, :, :], geq[:, :, :], -100.0, over_e(iota[:, 0:G], G), ALU.mult, ALU.add)
            reduce(v[:, 1, :], geq[:, :, :], ALU.min)
            dve.tensor_tensor(goh[:, :, :], geq[:, :, :], over_t(v[:, 1, :], G), ALU.is_equal).then_inc(gd_done, 1)
            dve.wait_ge(gd_done, 1)
            op(el[:, :, :, :], lg[:, :, G:].rearrange("p t (g e) -> p t g e", e=EG),
               goh[:, :, :].unsqueeze(3).to_broadcast([P, T, G, EG]), ALU.mult)
            reduce(e8[:, 0, :, :], el[:, :, :, :].rearrange("p t g e -> p t e g"), ALU.add)
            dve.wait_ge(eg_done, 1)
            reduce(v[:, 2, :], eg[:, :, :], ALU.add)
            for k in range(TOP_K):
                reduce(v[:, 3 + k, :], e8[:, k, :, :], ALU.max)
                op(eq[:, :, :], e8[:, k, :, :], over_t(v[:, 3 + k, :], EG), ALU.is_equal)
                scaled(eq[:, :, :], eq[:, :, :], -100.0, over_e(iota[:, 0:EG], EG), ALU.mult, ALU.add)
                reduce(v[:, 5, :], eq[:, :, :], ALU.min)
                op(o[:, k, :, :], eq[:, :, :], over_t(v[:, 5, :], EG), ALU.is_equal)
                if k == 0:
                    scaled(e8[:, 1, :, :], o[:, 0, :, :], -BIG, e8[:, 0, :, :], ALU.mult, ALU.add)
            dve.tensor_tensor(v[:, 6, :], v[:, 4, :], v[:, 3, :], ALU.subtract).then_inc(d_done, 1)
            for k in range(TOP_K):
                op(oh[:, k, :, :].rearrange("p t (g e) -> p t g e", e=EG),
                   goh[:, :, :].unsqueeze(3).to_broadcast([P, T, G, EG]),
                   o[:, k, :, :].unsqueeze(2).to_broadcast([P, T, G, EG]), ALU.mult)
            dve.tensor_tensor(both[:, :, :], oh[:, 0, :, :], oh[:, 1, :, :], ALU.add).then_inc(both_done, 1)
            dve.wait_ge(ex_done, 1)
            scaled(v[:, 8, :], v[:, 7, :], 1.0, v[:, 2, :], ALU.add, ALU.mult)
            dve.reciprocal(v[:, 9, :], v[:, 8, :]).then_inc(step, 1)
            dve.wait_ge(step, done())
            dve.tensor_copy(gates[:, 0, :], v[:, 9, :]).then_inc(step, 1)
            done()
            op(gates[:, 1, :], v[:, 9, :], v[:, 7, :], ALU.mult)
            dve.wait_ge(rank_mm, 1)
            dve.memset(sums[:, 0, :], 0.0).then_inc(step, 1)
            dve.wait_ge(step, done())
            for t in range(T):
                op(sums[:, t + 1, :], sums[:, t, :], c_ps[:, t, :], ALU.add)
            op(rank[:, :, :], r_ps[:, :, :], sums[:, 0:T, :], ALU.add)
            dve.tensor_tensor_scan(start[:, 0, :], ones[:, 0:E], sums[:, T, :], 0.0, ALU.mult, ALU.add
                                   ).then_inc(step, 1)
            dve.wait_ge(step, done())
            op(start[:, 1, :], start[:, 0, :], sums[:, T, :], ALU.subtract)
            op(place[:, :, :], rank[:, :, :], over_e(start[:, 1, :], E), ALU.add)
            for k in range(TOP_K):
                op(prod[:, :, :], oh[:, k, :, :], place[:, :, :], ALU.mult)
                reduce(pos[:, k, :], prod[:, :, :], ALU.add)
                dve.tensor_copy(slots[:, k, :], pos[:, k, :]).then_inc(slots_done, 1)
            dve.tensor_scalar(bv[:, 0, 0:T], iota_b[:, 0:T], float(P), None, ALU.mult).then_inc(step, 1)
            dve.wait_ge(step, done())
            op(more[:, :, :], sums[:, T, :].unsqueeze(2).to_broadcast([P, E, T]),
               bv[:, 0, 0:T].unsqueeze(1).to_broadcast([P, E, T]), ALU.is_gt)
            reduce(nb[:, :], more[:, :, :], ALU.add)
            dve.tensor_tensor_scan(pend[:, :], ones[:, 0:E], nb[:, :], 0.0, ALU.mult, ALU.add).then_inc(step, 1)
            dve.wait_ge(step, done())
            op(le[:, 0, :, :], pend[:, :].unsqueeze(1).to_broadcast([P, NB, E]),
               iota_b[:, :].unsqueeze(2).to_broadcast([P, NB, E]), ALU.is_le)
            op(le[:, 1, :, :], le[:, 0, :, :], nb[:, :].unsqueeze(1).to_broadcast([P, NB, E]), ALU.mult)
            op(le[:, 2, :, :], le[:, 0, :, :], sums[:, T, :].unsqueeze(1).to_broadcast([P, NB, E]), ALU.mult)
            reduce(bv[:, 1, :], le[:, 0, :, :], ALU.add)
            reduce(bv[:, 2, :], le[:, 1, :, :], ALU.add)
            reduce(bv[:, 7, :], le[:, 2, :, :], ALU.add)
            dve.tensor_scalar(bt[:, B_EXP:B_EXP + NB], bv[:, 1, :], float(E - 1), None, ALU.min).then_inc(step, 1)
            dve.wait_ge(step, done())
            op(bv[:, 3, :], iota_b[:, :], bv[:, 2, :], ALU.subtract)
            scaled(bv[:, 5, :], bv[:, 3, :], float(P), bv[:, 7, :], ALU.mult, ALU.add)
            dve.tensor_scalar(bt[:, B_FIRST:B_FIRST + NB], bv[:, 5, :], float(TOP_K * SEQ), None, ALU.min
                              ).then_inc(step, 1)
            dve.tensor_scalar(bv[:, 6, :], bv[:, 1, :], float(E), None, ALU.is_lt).then_inc(step, 1)
            done()
            dve.wait_ge(step, done())
            scaled(bt[:, B_NEW:B_NEW + NB], bv[:, 3, :], 0.0, bv[:, 6, :], ALU.is_equal, ALU.mult)
            dve.tensor_tensor_scan(bt[:, B_ORD:B_ORD + NB], ones[:, 0:NB], bt[:, B_NEW:B_NEW + NB], -1.0,
                                   ALU.mult, ALU.add).then_inc(step, 1)
            dve.tensor_scalar(bt[:, B_COUNT:], pend[:, E - 1:], float(MIN_BLOCKS), None, ALU.subtract
                              ).then_inc(step, 1)
            done()
            dve.wait_ge(step, done())
            dve.tensor_copy(table[:, :], bt[:, :]).then_inc(table_done, 1)


def experts(nc, table, slots_d, h_d, raws, y_d, x2_d, x2):
    KD = DE // P
    PC = 2
    (g_raw, w_gate), (u_raw, w_up), (d_raw, w_down) = raws

    with Scope(nc, "e") as s:
        ident = s.sb("ident", [P, P])
        idx = s.sb("idx", [P, 1], I32)
        gate_copy = s.sb("gate_copy", [P, 1])
        xr = s.sb("xr", [P, DM])
        x_hi = s.sb("x_hi", [P, KM, P], F32R)
        x_lo = s.sb("x_lo", [P, KM, P], F32R)
        g_hi = s.sb("g_hi", [P, KM, DE], F32R)
        g_lo = s.sb("g_lo", [P, KM, DE], F32R)
        u_hi = s.sb("u_hi", [P, KM, DE], F32R)
        u_lo = s.sb("u_lo", [P, KM, DE], F32R)
        d_hi = s.sb("d_hi", [P, KD, DM], F32R)
        d_lo = s.sb("d_lo", [P, KD, DM], F32R)
        sg = s.sb("sg", [P, DE])
        hm = s.sb("hm", [P, DE])
        m_hi = s.sb("m_hi", [P, KD, P], F32R)
        m_lo = s.sb("m_lo", [P, KD, P], F32R)
        yo = s.sb("yo", [P, DM])
        x_ps = s.ps("x_ps", [P, KM, P])
        g_ps = s.ps("g_ps", [P, DE])
        u_ps = s.ps("u_ps", [P, DE])
        m_ps = s.ps("m_ps", [P, KD, P])
        y_ps = s.ps("y_ps", [P, 2, 512])

        ident_step = s.sem("ident_step")
        consts = s.sem("consts")
        idx_in = s.pool_sem("idx_in")
        gated = s.sem("gated")
        x_in = s.pool_sem("x_in")
        xT_done = s.sem("xT_done")
        xhi_done = s.sem("xhi_done")
        xlo_done = s.sem("xlo_done")
        g_in = [s.sem(f"g_in{i}") for i in range(PC)]
        u_in = [s.sem(f"u_in{i}") for i in range(PC)]
        d_in = [s.sem(f"d_in{i}") for i in range(PC)]
        ghi_done = s.sem("ghi_done")
        uhi_done = s.sem("uhi_done")
        dhi_done = s.sem("dhi_done")
        glo_done = s.sem("glo_done")
        ulo_done = s.sem("ulo_done")
        dlo_done = s.sem("dlo_done")
        g_done = s.sem("g_done")
        u_done = s.sem("u_done")
        d_done = s.sem("d_done")
        silu_done = s.sem("silu_done")
        hm_done = s.sem("hm_done")
        mT_done = s.sem("mT_done")
        mhi_done = s.sem("mhi_done")
        mlo_done = s.sem("mlo_done")
        yev_done = [s.sem(f"yev_done{j}") for j in range(2)]
        y_out = s.pool_sem("y_out")
        x2_in = s.sem("x2_in")

        block = s.block()

        def read(engine, at, b, lo, hi):
            return table_entry(engine, table, at, b, lo, hi)

        def piece(raw, i):
            n = raw.shape[1] // PC
            return slice(i * n, (i + 1) * n)

        def begun(engine, b):
            return read(engine, B_ORD, b, 0, EXPERTS - 1) + 1

        def count(engine):
            return read(engine, B_COUNT, 0, 0, MAX_BLOCKS - MIN_BLOCKS) + MIN_BLOCKS

        @block.sync
        def _(sync):
            def load_if_new(b, weights):
                with sync.If(read(sync, B_NEW, b, 0, 1) > 0):
                    e = read(sync, B_EXP, b, 0, EXPERTS - 1)
                    o = begun(sync, b)
                    for raw, src, loaded, split in weights:
                        sync.wait_ge(split, PC * (o - 1))
                        for i in range(PC):
                            c = piece(raw, i)
                            sync.dma_start(raw[:, c, :], of_expert(src, e)[:, c, :]).then_inc(loaded[i], 16)

            gate_up = ((g_raw, w_gate, g_in, glo_done), (u_raw, w_up, u_in, ulo_done))
            down = ((d_raw, w_down, d_in, dlo_done),)
            load_if_new(1, gate_up)
            sync.dma_start(x2[:, :, :], x2_d.rearrange("(t p) c -> p t c", p=P)[:, 0:X2_SLOTS, :]
                           ).then_inc(x2_in, 16)
            nb = count(sync)
            with sync.Fori(1, MAX_BLOCKS) as b:
                with sync.If(b < nb):
                    load_if_new(b + 1, gate_up)
                    load_if_new(b, down)
            sync.wait_ge(x2_in, 16)

        @block.gpsimd
        def _(pool):
            pool.memset(ident[:, :], 0.0).then_inc(ident_step, 1)
            pool.wait_ge(ident_step, 1)
            pool.affine_select(out=ident[:, :], in_=ident[:, :], compare_op=ALU.not_equal, fill=1.0, base=0,
                               pattern=[[-1, P]], channel_multiplier=1).then_inc(consts, 1)
            pool.wait_ge(consts, 1)

            def load_ids(b):
                first = read(pool, B_FIRST, b, 0, TOP_K * SEQ)
                wait(pool, x_in, 16 * b)
                pool.dma_start(idx[:, :], slots_d[bass.ds(first, P), :]).then_inc(idx_in, 16)

            def gather(b):
                pool.wait_ge(idx_in, 16 * (b + 1))
                wait(pool, xT_done, b)
                wait(pool, gated, b)
                pool.tensor_tensor(gate_copy[:, :], ident[:, 0:1], ident[:, 0:1], ALU.mult).then_inc(gated, 1)
                pool.indirect_dma_start(xr[:, :], None, h_d, bass.IndirectOffsetOnAxis(idx[:, 0:1], 0)
                                        ).then_inc(x_in, 16)

            def store(b):
                for j in range(2):
                    pool.wait_ge(yev_done[j], b + 1)
                first = read(pool, B_FIRST, b, 0, TOP_K * SEQ)
                pool.dma_start(y_d[bass.ds(first, P), :], yo[:, :]).then_inc(y_out, 16)

            nb = count(pool)
            load_ids(0)
            for b in range(3):
                gather(b)
                load_ids(b + 1)
            with pool.Fori(1, MAX_BLOCKS) as b:
                with pool.If(b < nb):
                    gather(b + 2)
                    load_ids(b + 3)
                    store(b - 1)
            store(nb - 1)
            pool.wait_ge(x_in, 16 * (nb + 2))
            pool.wait_ge(idx_in, 16 * (nb + 3))
            pool.wait_ge(y_out, 16 * nb)

        @block.scalar
        def _(act):
            def split(b, o, raw, hi, loaded, used, done):
                wait(act, used, b)
                for i in range(PC):
                    wait(act, loaded[i], 16 * (o - 1))
                    c = piece(raw, i)
                    act.activation(hi[:, c, :], raw[:, c, :], ACT.Copy).then_inc(done, 1)

            def x_high(b):
                act.wait_ge(xT_done, b + 1)
                wait(act, u_done, b)
                act.activation(x_hi[:, :, :], x_ps[:, :, :], ACT.Copy).then_inc(xhi_done, 1)

            def silu(b):
                act.wait_ge(g_done, b + 1)
                wait(act, hm_done, b)
                act.activation(sg[:, :], g_ps[:, :], ACT.Silu).then_inc(silu_done, 1)

            def m_high(b):
                act.wait_ge(mT_done, b + 1)
                wait(act, d_done, b)
                act.activation(m_hi[:, :, :], m_ps[:, :, :], ACT.Copy).then_inc(mhi_done, 1)

            def y_half(b):
                act.wait_ge(d_done, b + 1)
                wait(act, y_out, 16 * b)
                act.activation(yo[:, 0:512], y_ps[:, 0, :], ACT.Copy).then_inc(yev_done[0], 1)

            g = (g_raw, g_hi, g_in, g_done, ghi_done)
            u = (u_raw, u_hi, u_in, u_done, uhi_done)
            d = (d_raw, d_hi, d_in, d_done, dhi_done)
            nb = count(act)
            split(0, 1, *g)
            split(0, 1, *u)
            x_high(0)
            split(0, 1, *d)
            silu(0)

            def new(b, *what):
                with act.If(read(act, B_NEW, b, 0, 1) > 0):
                    split(b, begun(act, b), *what)

            new(1, *g)
            x_high(1)
            new(1, *u)

            def body(b):
                silu(b)
                m_high(b - 1)
                new(b + 1, *g)
                x_high(b + 1)
                new(b + 1, *u)

            body(1)
            y_half(0)
            new(1, *d)
            body(2)
            with act.Fori(3, MAX_BLOCKS) as b:
                with act.If(b < nb):
                    y_half(b - 2)
                    new(b - 1, *d)
                    body(b)
            y_half(nb - 2)
            new(nb - 1, *d)
            m_high(nb - 1)
            y_half(nb - 1)

        @block.vector
        def _(dve):
            def split(b, o, raw, hi, lo, hi_done, done):
                for i in range(PC):
                    dve.wait_ge(hi_done, PC * (o - 1) + i + 1)
                    c = piece(raw, i)
                    dve.tensor_tensor(lo[:, c, :], raw[:, c, :], hi[:, c, :].bitcast(F32), ALU.subtract
                                      ).then_inc(done, 1)

            def x_low(b):
                dve.wait_ge(xhi_done, b + 1)
                dve.tensor_tensor(x_lo[:, :, :], x_ps[:, :, :], x_hi[:, :, :].bitcast(F32), ALU.subtract
                                  ).then_inc(xlo_done, 1)

            def middle(b):
                dve.wait_ge(silu_done, b + 1)
                dve.wait_ge(u_done, b + 1)
                wait(dve, mT_done, b)
                dve.tensor_tensor(hm[:, :], sg[:, :], u_ps[:, :], ALU.mult).then_inc(hm_done, 1)

            def m_low(b):
                dve.wait_ge(mhi_done, b + 1)
                dve.tensor_tensor(m_lo[:, :, :], m_ps[:, :, :], m_hi[:, :, :].bitcast(F32), ALU.subtract
                                  ).then_inc(mlo_done, 1)

            def y_half(b):
                dve.wait_ge(d_done, b + 1)
                wait(dve, y_out, 16 * b)
                dve.tensor_copy(yo[:, 512:], y_ps[:, 1, :]).then_inc(yev_done[1], 1)

            def new(b, *what):
                with dve.If(read(dve, B_NEW, b, 0, 1) > 0):
                    split(b, begun(dve, b), *what)

            g = (g_raw, g_hi, g_lo, ghi_done, glo_done)
            u = (u_raw, u_hi, u_lo, uhi_done, ulo_done)
            d = (d_raw, d_hi, d_lo, dhi_done, dlo_done)
            nb = count(dve)
            split(0, 1, *g)
            split(0, 1, *u)
            x_low(0)
            split(0, 1, *d)
            middle(0)
            new(1, *g)
            x_low(1)
            new(1, *u)

            def body(b):
                m_low(b - 1)
                new(b + 1, *g)
                middle(b)
                x_low(b + 1)
                new(b + 1, *u)

            body(1)
            y_half(0)
            new(1, *d)
            body(2)
            with dve.Fori(3, MAX_BLOCKS) as b:
                with dve.If(b < nb):
                    y_half(b - 2)
                    new(b - 1, *d)
                    body(b)
            y_half(nb - 2)
            new(nb - 1, *d)
            m_low(nb - 1)
            y_half(nb - 1)

        @block.tensor
        def _(pe):
            def x_transposes(b):
                pe.wait_ge(x_in, 16 * (b + 1))
                wait(pe, xlo_done, b)
                for k in range(KM):
                    ins = pe.transpose(x_ps[:, k, :], xr[:, k * P:(k + 1) * P], ident[:, :])
                ins.then_inc(xT_done, 1)

            def product(out, s_hi, s_lo, w_hi, w_lo, n):
                for k in range(n):
                    pe.matmul(out, s_lo[:, k, :], w_hi(k), start=(k == 0), stop=False)
                    pe.matmul(out, s_hi[:, k, :], w_lo(k), start=False, stop=False)
                    ins = pe.matmul(out, s_hi[:, k, :], w_hi(k), start=False, stop=(k == n - 1))
                return ins

            def gate(b, o):
                pe.wait_ge(glo_done, PC * o)
                pe.wait_ge(xlo_done, b + 1)
                wait(pe, silu_done, b)
                product(g_ps[:, :], x_hi, x_lo, lambda k: g_hi[:, k, :], lambda k: g_lo[:, k, :], KM
                        ).then_inc(g_done, 1)

            def up(b, o):
                pe.wait_ge(ulo_done, PC * o)
                wait(pe, hm_done, b)
                product(u_ps[:, :], x_hi, x_lo, lambda k: u_hi[:, k, :], lambda k: u_lo[:, k, :], KM
                        ).then_inc(u_done, 1)

            def m_transposes(b):
                pe.wait_ge(hm_done, b + 1)
                wait(pe, mlo_done, b)
                for k in range(KD):
                    ins = pe.transpose(m_ps[:, k, :], hm[:, k * P:(k + 1) * P], ident[:, :])
                ins.then_inc(mT_done, 1)

            def down(b, o):
                pe.wait_ge(dlo_done, PC * o)
                pe.wait_ge(mlo_done, b + 1)
                for j in range(2):
                    wait(pe, yev_done[j], b)
                    c = slice(j * 512, (j + 1) * 512)
                    ins = product(y_ps[:, j, :], m_hi, m_lo, lambda k: d_hi[:, k, c], lambda k: d_lo[:, k, c], KD)
                ins.then_inc(d_done, 1)

            pe.wait_ge(consts, 1)
            nb = count(pe)
            x_transposes(0)
            gate(0, 1)
            up(0, 1)
            x_transposes(1)

            def body(b):
                o = begun(pe, b)
                gate(b, o)
                m_transposes(b - 1)
                up(b, o)
                x_transposes(b + 1)
                down(b - 1, begun(pe, b - 1))

            body(1)
            with pe.Fori(2, MAX_BLOCKS) as b:
                with pe.If(b < nb):
                    body(b)
            m_transposes(nb - 1)
            down(nb - 1, begun(pe, nb - 1))


def combine(nc, x2_d, x2, y_d, gates, slots, out):
    NX = X2_SLOTS
    NS = 4

    with Scope(nc, "f") as s:
        y = s.sb("y", [P, NS, TOP_K, DM])
        x_in = [s.sem(f"x_in{j}") for j in range(NX)]
        y_in = [[s.pool_sem(f"y_in{j}_{k}") for k in range(TOP_K)] for j in range(NS)]
        first = s.sem("first")
        added = s.sem("added")
        stored = [s.sem(f"stored{j}") for j in range(NX)]
        block = s.block()

        def rows(ap, t):
            return ap.rearrange("(t p) c -> t p c", p=P)[bass.ds(t, 1), :, :].rearrange("a p c -> (a p) c")

        @block.sync
        def _(sync):
            def reload(i, j):
                sync.wait_ge(stored[j], 16 * i)
                sync.dma_start(x2[:, j, :], rows(x2_d, NX * i + j)).then_inc(x_in[j], 16)

            def store(i, j):
                sync.wait_ge(added, NX * i + j + 1)
                sync.dma_start(rows(out[0], NX * i + j), x2[:, j, :]).then_inc(stored[j], 16)

            with sync.Fori(1, TILES // NX) as i:
                for j in range(NX):
                    store(i - 1, j)
                    if j >= 2:
                        reload(i, j - 2)
                for j in range(NX - 2, NX):
                    reload(i, j)
            for j in range(NX):
                store(TILES // NX - 1, j)
            for j in range(NX):
                sync.wait_ge(stored[j], 16 * TILES // NX)

        @block.gpsimd
        def _(pool):
            for t in range(TILES):
                j = t % NS
                wait(pool, added, t - NS + 1)
                for k in range(TOP_K):
                    pool.indirect_dma_start(y[:, j, k, :], None, y_d[0:TOP_K * SEQ, :],
                                            bass.IndirectOffsetOnAxis(slots[:, k, t:t + 1], 0)
                                            ).then_inc(y_in[j][k], 16)

        @block.vector
        def _(dve):
            def body(i):
                for j in range(NX):
                    t, js, uses = NX * i + j, j % NS, NX // NS * i + j // NS + 1
                    xv = x2[:, j, :]
                    wait(dve, x_in[j], 16 * i)
                    dve.wait_ge(y_in[js][0], 16 * uses)
                    dve.scalar_tensor_tensor(out=xv, in0=y[:, js, 0, :], scalar=gates[:, 0, bass.ds(t, 1)],
                                             in1=xv, op0=ALU.mult, op1=ALU.add).then_inc(first, 1)
                    dve.wait_ge(first, t + 1)
                    dve.wait_ge(y_in[js][1], 16 * uses)
                    dve.scalar_tensor_tensor(out=xv, in0=y[:, js, 1, :], scalar=gates[:, 1, bass.ds(t, 1)],
                                             in1=xv, op0=ALU.mult, op1=ALU.add).then_inc(added, 1)

            body(0)
            with dve.Fori(1, TILES // NX) as i:
                body(i)


def build(nc, x, rel_bias_table, norm_mix, w_in, q_norm, k_norm, conv_w, conv_b, rg_w_a, rg_b_a, rg_w_x,
          rg_b_x, rg_lambda, norm_attn_out, norm_rnn_out, w_out, norm_ffn, router_group_w, router_group_b,
          router_expert_w, router_expert_b, expert_w_gate, expert_w_up, expert_w_down, one_hot, out):
    def scratch(name, shape, dt=F32):
        return nc.dram_tensor(name, shape, dt, kind="Internal").ap()

    qkv = scratch("qkv", [SEQ, D_QKV])
    rnn_t = scratch("rnn_t", [D_RNN, SEQ])
    toeplitz = scratch("toeplitz", [HEADS, len(BRANCHES) * TW])
    attn_o = scratch("attn_o", [len(BRANCHES) * SEQ, OW])
    x2_d = scratch("x2_d", [SEQ, DM])
    h_d = scratch("h_d", [SEQ, DM])
    slots_d = scratch("slots_d", [TOP_K * SEQ + P, 1], I32)
    y_d = scratch("y_d", [TOP_K * SEQ + P, DM])

    project_and_recur(nc, x, norm_mix, w_in, conv_w, conv_b, rg_w_a, rg_b_a, rg_w_x, rg_b_x, rg_lambda,
                      rel_bias_table, one_hot, qkv, rnn_t, toeplitz)
    with Scope(nc, "routing") as s:
        lg = s.sb("lg", [P, TILES, GROUPS + EXPERTS])
        gates = s.sb("gates", [P, TOP_K, TILES])
        slots = s.sb("slots", [P, TOP_K, TILES], I32)
        table = s.sb("table", [P, 4 * BLOCK_COLS + 1], I32)
        with Scope(nc, "w_out") as w:
            w_raw = w.sb("raw", [P, KM, DM])
            attend(nc, toeplitz, q_norm, k_norm, qkv, attn_o, w_out, w_raw)
            mix(nc, x, attn_o, rnn_t, norm_attn_out, norm_rnn_out, w_raw, norm_ffn, router_group_w,
                router_group_b, router_expert_w, router_expert_b, x2_d, h_d, lg)
        x2 = s.sb("x2", [P, X2_SLOTS, DM])
        with Scope(nc, "weights") as w:
            raws = ((w.sb("gate", [P, KM, DE]), expert_w_gate), (w.sb("up", [P, KM, DE]), expert_w_up),
                    (w.sb("down", [P, DE // P, DM]), expert_w_down))
            route(nc, lg, slots_d, gates, slots, table, raws)
            experts(nc, table, slots_d, h_d, raws, y_d, x2_d, x2)
        combine(nc, x2_d, x2, y_d, gates, slots, out)


def kernel(x, rel_bias_table, norm_mix, w_in, q_norm, k_norm, conv_w, conv_b, rg_w_a, rg_b_a, rg_w_x,
           rg_b_x, rg_lambda, norm_attn_out, norm_rnn_out, w_out, norm_ffn, router_group_w, router_group_b,
           router_expert_w, router_expert_b, expert_w_gate, expert_w_up, expert_w_down):
    import concourse.bacc as bacc
    from concourse import bass_utils

    arrays = {"x": x, "rel_bias_table": rel_bias_table, "norm_mix": norm_mix, "w_in": w_in,
              "q_norm": q_norm, "k_norm": k_norm, "conv_w": conv_w, "conv_b": conv_b, "rg_w_a": rg_w_a,
              "rg_b_a": rg_b_a, "rg_w_x": rg_w_x, "rg_b_x": rg_b_x, "rg_lambda": rg_lambda,
              "norm_attn_out": norm_attn_out, "norm_rnn_out": norm_rnn_out, "w_out": w_out,
              "norm_ffn": norm_ffn, "router_group_w": router_group_w, "router_group_b": router_group_b,
              "router_expert_w": router_expert_w, "router_expert_b": router_expert_b,
              "expert_w_gate": expert_w_gate, "expert_w_up": expert_w_up,
              "expert_w_down": expert_w_down, "one_hot": bias_buckets()}
    arrays = {n: np.ascontiguousarray(a) for n, a in arrays.items()}
    nc = bacc.Bacc("TRN2", target_bir_lowering=False, num_devices=1)
    ins = [nc.dram_tensor(n, a.shape, mybir.dt.from_np(a.dtype), kind="ExternalInput").ap()
           for n, a in arrays.items()]
    out = nc.dram_tensor("out", x.shape, F32, kind="ExternalOutput").ap()
    build(nc, *ins, out)
    nc.finalize()
    res = bass_utils.run_bass_kernel_spmd(nc, [arrays], core_ids=[0])
    return np.asarray(res.results[0]["out"])
```
